# Optimizing a Trainium2 kernel written in Bass

```python
import jax, jax.numpy as jnp
from jax import lax
import numpy as np

D_MODEL = 1024
BATCH = 1
SEQ = 256
DEPTH = 4

HEAD_DIM = 64
ROT_DIM = HEAD_DIM // 4
ROPE_THETA = 500000.0
N_MIXERS = 3
A_HEADS = D_MODEL // HEAD_DIM
A_KV_HEADS = 4
A_WINDOW = 128
WIN_BLK = 128
B_HEADS = D_MODEL // HEAD_DIM
B_GROUPS = ((128, 1), (512, 4), (2048, 16))
C_HEADS = D_MODEL // HEAD_DIM
MOBA_BLOCK = 256
MOBA_TOPK = 3
MOBA_QCHUNK = 16
D_FF = ((8 * D_MODEL + 3 * 256 - 1) // (3 * 256)) * 256
DN_ALPHA = (2 * DEPTH) ** 0.25
DN_BETA = (8 * DEPTH) ** -0.25
LN_EPS = 1e-5
NEG = -1e30


def layer_norm(x, g, b):
    xf = x.astype(jnp.float32)
    mu = xf.mean(-1, keepdims=True)
    var = jnp.square(xf - mu).mean(-1, keepdims=True)
    return ((xf - mu) * lax.rsqrt(var + LN_EPS) * g.astype(jnp.float32) + b.astype(jnp.float32)).astype(x.dtype)

def rope_tables(positions):
    inv = ROPE_THETA ** (-jnp.arange(0, ROT_DIM, 2, dtype=jnp.float32) / ROT_DIM)
    ang = positions.astype(jnp.float32)[..., None] * inv
    return jnp.cos(ang), jnp.sin(ang)

def apply_rope(x, cos, sin):
    xf = x.astype(jnp.float32)
    half = ROT_DIM // 2
    x1, x2 = xf[..., :half], xf[..., half:ROT_DIM]
    c, s = cos[:, :, None, :], sin[:, :, None, :]
    return jnp.concatenate([x1 * c - x2 * s, x2 * c + x1 * s, xf[..., ROT_DIM:]], axis=-1).astype(x.dtype)

def block_attention(q, k, v, blk, n_back, with_prev, sink=None):
    B, L, Hq, dh = q.shape
    Hkv = k.shape[2]
    G = Hq // Hkv
    nb = L // blk
    qb = q.astype(jnp.float32).reshape(B, nb, blk, Hkv, G, dh)
    kb = k.astype(jnp.float32).reshape(B, nb, blk, Hkv, dh)
    vb = v.astype(jnp.float32).reshape(B, nb, blk, Hkv, dh)
    if with_prev:
        shift = lambda t: jnp.pad(t, ((0, 0), (1, 0), (0, 0), (0, 0), (0, 0)))[:, :-1]
        kb = jnp.concatenate([shift(kb), kb], axis=2)
        vb = jnp.concatenate([shift(vb), vb], axis=2)
    off = blk if with_prev else 0
    nk = kb.shape[2]
    s = jnp.einsum('bnqhgd,bnkhd->bnhgqk', qb, kb) * (dh ** -0.5)
    diff = jnp.arange(blk)[:, None] + off - jnp.arange(nk)[None, :]
    ok = ((diff >= 0) & (diff <= n_back))[None]
    if with_prev:
        ok = ok & ((jnp.arange(nb)[:, None, None] > 0) | (jnp.arange(nk)[None, None, :] >= blk))
    s = jnp.where(ok[None, :, None, None], s, NEG)
    m = s.max(-1)
    if sink is not None:
        sk = sink.astype(jnp.float32).reshape(1, 1, Hkv, G, 1)
        m = jnp.maximum(m, sk)
    p = jnp.exp(s - m[..., None])
    l = p.sum(-1)
    if sink is not None:
        l = l + jnp.exp(sk - m)
    o = jnp.einsum('bnhgqk,bnkhd->bnqhgd', p, vb) / jnp.transpose(l, (0, 1, 4, 2, 3))[..., None]
    lse = jnp.transpose(m + jnp.log(l), (0, 1, 4, 2, 3)).reshape(B, L, Hq)
    return o.reshape(B, L, Hq, dh), lse

def mixer_a(x, w_qkv, b_qkv, sinks, w_o, b_o, cos, sin):
    B, S, _ = x.shape
    nq, nkv = A_HEADS * HEAD_DIM, A_KV_HEADS * HEAD_DIM
    qkv = x @ w_qkv + b_qkv
    q = apply_rope(qkv[..., :nq].reshape(B, S, A_HEADS, HEAD_DIM), cos, sin)
    k = apply_rope(qkv[..., nq:nq + nkv].reshape(B, S, A_KV_HEADS, HEAD_DIM), cos, sin)
    v = qkv[..., nq + nkv:].reshape(B, S, A_KV_HEADS, HEAD_DIM)
    o, _ = block_attention(q, k, v, WIN_BLK, A_WINDOW - 1, True, sinks)
    return o.reshape(B, S, nq).astype(x.dtype) @ w_o + b_o

def dilated_attention(q, k, v, window, dil):
    B, S, H, dh = q.shape
    span = dil * WIN_BLK
    S_pad = -(-S // span) * span
    L = S_pad // dil

    def to_phase(t):
        t = jnp.pad(t, ((0, 0), (0, S_pad - S), (0, 0), (0, 0)))
        return jnp.transpose(t.reshape(B, L, dil, H, dh), (0, 2, 1, 3, 4)).reshape(B * dil, L, H, dh)

    o, lse = block_attention(to_phase(q), to_phase(k), to_phase(v), WIN_BLK, window // dil, True)
    o = jnp.transpose(o.reshape(B, dil, L, H, dh), (0, 2, 1, 3, 4)).reshape(B, S_pad, H, dh)[:, :S]
    lse = jnp.transpose(lse.reshape(B, dil, L, H), (0, 2, 1, 3)).reshape(B, S_pad, H)[:, :S]
    return o, lse

def mixer_b(x, w_qkv, w_o, cos, sin):
    B, S, _ = x.shape
    qkv = (x @ w_qkv).reshape(B, S, len(B_GROUPS), 3, B_HEADS, HEAD_DIM)
    outs, lses = [], []
    for g, (window, dil) in enumerate(B_GROUPS):
        q = apply_rope(qkv[:, :, g, 0], cos, sin)
        k = apply_rope(qkv[:, :, g, 1], cos, sin)
        o, lse = dilated_attention(q, k, qkv[:, :, g, 2], window, dil)
        outs.append(o)
        lses.append(lse)
    w = jax.nn.softmax(jnp.stack(lses), axis=0)
    o = jnp.sum(w[..., None] * jnp.stack(outs), axis=0)
    return o.reshape(B, S, B_HEADS * HEAD_DIM).astype(x.dtype) @ w_o

def mixer_c(x, w_qkv, w_o, cos, sin):
    B, S, _ = x.shape
    H, dh = C_HEADS, HEAD_DIM
    qkv = (x @ w_qkv).reshape(B, S, 3, H, dh)
    q = apply_rope(qkv[:, :, 0], cos, sin)
    k = apply_rope(qkv[:, :, 1], cos, sin)
    v = qkv[:, :, 2]
    S_pad = -(-S // MOBA_BLOCK) * MOBA_BLOCK
    nblk = S_pad // MOBA_BLOCK
    pad = ((0, 0), (0, S_pad - S), (0, 0), (0, 0))
    q, k, v = jnp.pad(q, pad), jnp.pad(k, pad), jnp.pad(v, pad)
    o_self, lse_self = block_attention(q, k, v, MOBA_BLOCK, MOBA_BLOCK - 1, False)
    qf = q.astype(jnp.float32)
    kblk = k.reshape(B, nblk, MOBA_BLOCK, H, dh)
    vblk = v.reshape(B, nblk, MOBA_BLOCK, H, dh)
    kmean = kblk.astype(jnp.float32).mean(axis=2)
    gate = jnp.einsum('bshd,bnhd->bshn', qf, kmean)
    n_past = jnp.arange(S_pad) // MOBA_BLOCK
    gate = jnp.where((jnp.arange(nblk)[None, :] < n_past[:, None])[None, :, None, :], gate, NEG)
    topk = min(MOBA_TOPK, nblk)
    _, idx = lax.top_k(gate, topk)
    valid = jnp.arange(topk)[None, :] < n_past[:, None]
    kbt = jnp.transpose(kblk, (0, 3, 1, 2, 4))
    vbt = jnp.transpose(vblk, (0, 3, 1, 2, 4))
    nc = S_pad // MOBA_QCHUNK
    q_c = jnp.transpose(qf.reshape(B, nc, MOBA_QCHUNK, H, dh), (1, 0, 2, 3, 4))
    i_c = jnp.transpose(idx.reshape(B, nc, MOBA_QCHUNK, H, topk), (1, 0, 2, 3, 4))
    v_c = valid.reshape(nc, MOBA_QCHUNK, topk)
    bi = jnp.arange(B)[:, None, None, None]
    hi = jnp.arange(H)[None, None, :, None]
    scale = dh ** -0.5

    def chunk(args):
        qc, ic, vc = args
        kg = kbt[bi, hi, ic].astype(jnp.float32)
        vg = vbt[bi, hi, ic].astype(jnp.float32)
        s = jnp.einsum('bqhd,bqhjkd->bqhjk', qc, kg) * scale
        s = jnp.where(vc[None, :, None, :, None], s, NEG)
        m = s.max(axis=(-2, -1))
        p = jnp.exp(s - m[..., None, None])
        l = p.sum(axis=(-2, -1))
        o = jnp.einsum('bqhjk,bqhjkd->bqhd', p, vg) / l[..., None]
        return o, m + jnp.log(l)

    o_sel, lse_sel = lax.map(chunk, (q_c, i_c, v_c))
    o_sel = jnp.transpose(o_sel, (1, 0, 2, 3, 4)).reshape(B, S_pad, H, dh)
    lse_sel = jnp.transpose(lse_sel, (1, 0, 2, 3)).reshape(B, S_pad, H)
    m = jnp.maximum(lse_self, lse_sel)
    w1 = jnp.exp(lse_self - m)
    w2 = jnp.exp(lse_sel - m)
    o = (w1[..., None] * o_self + w2[..., None] * o_sel) / (w1 + w2)[..., None]
    return o[:, :S].reshape(B, S, H * dh).astype(x.dtype) @ w_o

def swiglu(x, w_gate_up, w_down):
    gu = x @ w_gate_up
    gate, up = gu[..., :D_FF], gu[..., D_FF:]
    return (jax.nn.silu(gate) * up) @ w_down

def first_inputs(seed: int = 0) -> dict:
    key = jax.random.key(seed)
    ks = jax.random.split(key, 16)
    n_a = (DEPTH + 2) // 3
    n_b = (DEPTH + 1) // 3
    n_c = DEPTH // 3
    D = D_MODEL
    a_cols = (A_HEADS + 2 * A_KV_HEADS) * HEAD_DIM
    b_cols = len(B_GROUPS) * 3 * B_HEADS * HEAD_DIM
    c_cols = 3 * C_HEADS * HEAD_DIM
    nrm = lambda k, shape, fan_in, s=1.0: jax.random.normal(k, shape, jnp.float32) * (fan_in ** -0.5) * s
    return {
        "x": jax.random.normal(ks[0], (BATCH, SEQ, D), jnp.float32),
        "positions": jnp.broadcast_to(jnp.arange(SEQ, dtype=jnp.int32), (BATCH, SEQ)),
        "ln_g": 1.0 + 0.02 * jax.random.normal(ks[1], (DEPTH, 2, D), jnp.float32),
        "ln_b": 0.02 * jax.random.normal(ks[2], (DEPTH, 2, D), jnp.float32),
        "a_w_qkv": nrm(ks[3], (n_a, D, a_cols), D),
        "a_b_qkv": 0.02 * jax.random.normal(ks[4], (n_a, a_cols), jnp.float32),
        "a_sinks": 0.5 * jax.random.normal(ks[5], (n_a, A_HEADS), jnp.float32),
        "a_w_o": nrm(ks[6], (n_a, A_HEADS * HEAD_DIM, D), A_HEADS * HEAD_DIM, DN_BETA),
        "a_b_o": 0.02 * jax.random.normal(ks[7], (n_a, D), jnp.float32),
        "b_w_qkv": nrm(ks[8], (n_b, D, b_cols), D),
        "b_w_o": nrm(ks[9], (n_b, B_HEADS * HEAD_DIM, D), B_HEADS * HEAD_DIM, DN_BETA),
        "c_w_qkv": nrm(ks[10], (n_c, D, c_cols), D),
        "c_w_o": nrm(ks[11], (n_c, C_HEADS * HEAD_DIM, D), C_HEADS * HEAD_DIM, DN_BETA),
        "w_gate_up": nrm(ks[12], (DEPTH, D, 2 * D_FF), D),
        "w_down": nrm(ks[13], (DEPTH, D_FF, D), D_FF, DN_BETA),
    }

def first_block(x, positions, ln_g, ln_b, a_w_qkv, a_b_qkv, a_sinks, a_w_o, a_b_o,
              b_w_qkv, b_w_o, c_w_qkv, c_w_o, w_gate_up, w_down):
    cos, sin = rope_tables(positions)
    for i in range(DEPTH):
        kind, j = i % N_MIXERS, i // N_MIXERS
        if kind == 0:
            h = mixer_a(x, a_w_qkv[j], a_b_qkv[j], a_sinks[j], a_w_o[j], a_b_o[j], cos, sin)
        elif kind == 1:
            h = mixer_b(x, b_w_qkv[j], b_w_o[j], cos, sin)
        else:
            h = mixer_c(x, c_w_qkv[j], c_w_o[j], cos, sin)
        x = layer_norm(DN_ALPHA * x + h, ln_g[i, 0], ln_b[i, 0])
        x = layer_norm(DN_ALPHA * x + swiglu(x, w_gate_up[i], w_down[i]), ln_g[i, 1], ln_b[i, 1])
    return x


DEPTH_2 = 2

MEM_TOKENS = 256
N_BRANCH = 4
BRANCH_DIM = 512
CONV_DIM = 512
CONV_WIDTH = 3
DSA_HEADS = 8
DSA_HEAD_DIM = 64
IDX_HEADS = 8
IDX_DIM = 64
TOPK_MAX = 256
Q_BLOCK = 128
HG_HEADS = 4
HG_DK = 128
HG_DV = 128
HG_CHUNK = 64
MEM_HEADS = 4
MEM_HEAD_DIM = 128
ROT_DIM_2 = DSA_HEAD_DIM // 4
FFN_DIM = ((8 * D_MODEL // 3 + 255) // 256) * 256
EPS = 1e-6

SPLIT_SIZES = (CONV_DIM, CONV_DIM, CONV_DIM,
               DSA_HEADS * DSA_HEAD_DIM, DSA_HEAD_DIM, DSA_HEAD_DIM,
               IDX_HEADS * IDX_DIM, IDX_DIM, IDX_HEADS,
               HG_HEADS * HG_DK, HG_HEADS * HG_DK, HG_HEADS * HG_DV, HG_HEADS * HG_DV,
               MEM_HEADS * MEM_HEAD_DIM,
               N_BRANCH * D_MODEL)
IN_COLS = sum(SPLIT_SIZES)


def rmsnorm(x, g):
    xf = x.astype(jnp.float32)
    y = xf * lax.rsqrt(jnp.mean(xf * xf, axis=-1, keepdims=True) + EPS)
    return (y * g.astype(jnp.float32)).astype(x.dtype)

def rope_tables_2(positions, dtype):
    inv_freq = 1.0 / (ROPE_THETA ** (jnp.arange(0, ROT_DIM_2, 2, dtype=jnp.float32) / ROT_DIM_2))
    ang = positions.astype(jnp.float32)[..., None] * inv_freq
    return jnp.cos(ang)[:, :, None, :].astype(dtype), jnp.sin(ang)[:, :, None, :].astype(dtype)

def partial_rope(x, cos, sin):
    half = ROT_DIM_2 // 2
    x1, x2, xp = x[..., :half], x[..., half:ROT_DIM_2], x[..., ROT_DIM_2:]
    return jnp.concatenate([x1 * cos - x2 * sin, x1 * sin + x2 * cos, xp], axis=-1)

def split_cols(z):
    idx = [int(i) for i in np.cumsum(SPLIT_SIZES)[:-1]]
    return jnp.split(z, idx, axis=-1)

def causal_conv3(u, w):
    up = jnp.pad(u, ((0, 0), (CONV_WIDTH - 1, 0), (0, 0)))
    s = u.shape[1]
    return up[:, 0:s] * w[0] + up[:, 1:s + 1] * w[1] + up[:, 2:s + 2] * w[2]

def dsa_attention(q, k, v, iq, ik, iw):
    b, s = q.shape[0], q.shape[1]
    nb = s // Q_BLOCK
    topk = min(TOPK_MAX, s // 4)
    key_pos = jnp.arange(s)
    idx_scale = IDX_DIM ** -0.5
    att_scale = DSA_HEAD_DIM ** -0.5

    def blockify(a):
        return a.reshape(b, nb, Q_BLOCK, *a.shape[2:]).swapaxes(0, 1)

    def one_block(args):
        qb, iqb, iwb, qpos = args
        rel = jax.nn.relu(jnp.einsum('bthd,bsd->bths', iqb, ik) * idx_scale)
        score = jnp.einsum('bths,bth->bts', rel, iwb).astype(jnp.float32)
        causal = key_pos[None, :] <= qpos[:, None]
        score = jnp.where(causal[None], score, -jnp.inf)
        _, sel = lax.top_k(score, topk)
        valid = sel <= qpos[None, :, None]
        k_sel = jax.vmap(lambda kb, ib: kb[ib])(k, sel)
        v_sel = jax.vmap(lambda vb, ib: vb[ib])(v, sel)
        logits = jnp.einsum('bthd,btkd->bthk', qb, k_sel).astype(jnp.float32) * att_scale
        logits = jnp.where(valid[:, :, None, :], logits, -jnp.inf)
        p = jax.nn.softmax(logits, axis=-1).astype(v.dtype)
        return jnp.einsum('bthk,btkd->bthd', p, v_sel)

    out = lax.map(one_block, (blockify(q), blockify(iq), blockify(iw),
                              jnp.arange(s).reshape(nb, Q_BLOCK)))
    return out.swapaxes(0, 1).reshape(b, s, q.shape[2], q.shape[3])

def hgrn2_chunkwise(q, k, v, log_f):
    q, k, v, log_f = (a.astype(jnp.float32) for a in (q, k, v, log_f))
    b, s, h, dk = q.shape
    dv = v.shape[-1]
    nc = s // HG_CHUNK

    def to_chunks(a):
        return a.reshape(b, nc, HG_CHUNK, h, a.shape[-1]).transpose(1, 0, 3, 2, 4)

    qc, kc, vc, gc = (to_chunks(a) for a in (q, k, v, log_f))
    cum = jnp.cumsum(gc, axis=3)
    ref = cum[:, :, :, HG_CHUNK // 2 - 1:HG_CHUNK // 2, :]
    last = cum[:, :, :, -1:, :]
    tri = jnp.tril(jnp.ones((HG_CHUNK, HG_CHUNK), dtype=bool))
    a_intra = jnp.einsum('nbhtk,nbhsk->nbhts', qc * jnp.exp(cum - ref), kc * jnp.exp(ref - cum))
    o_intra = jnp.einsum('nbhts,nbhsv->nbhtv', jnp.where(tri, a_intra, 0.0), vc)
    q_inter = qc * jnp.exp(cum)
    k_state = kc * jnp.exp(last - cum)
    decay_last = jnp.exp(last[:, :, :, 0, :])

    def step(state, inp):
        qi, ks, vv, dl = inp
        o = jnp.einsum('bhtk,bhkv->bhtv', qi, state)
        state = dl[..., None] * state + jnp.einsum('bhtk,bhtv->bhkv', ks, vv)
        return state, o

    s0 = jnp.zeros((b, h, dk, dv), jnp.float32)
    _, o_inter = lax.scan(step, s0, (q_inter, k_state, vc, decay_last))
    o = o_intra + o_inter
    return o.transpose(1, 0, 3, 2, 4).reshape(b, s, h, dv)

def hybrid_layer(x, mem_n, cos, sin, lb, norm_mix, w_in, conv_w, dsa_q_norm, dsa_k_norm,
                 hgrn_out_norm, mem_w_kv, mem_q_norm, mem_k_norm, w_lift, w_out,
                 norm_ffn, ffn_w_up, ffn_w_down):
    b, s, _ = x.shape
    h = rmsnorm(x, norm_mix)
    (a_x, a_b, a_c, d_q, d_k, d_v, i_q, i_k, i_w,
     g_q, g_f, g_i, g_g, m_q, gate_logits) = split_cols(h @ w_in)

    y_a = a_b * causal_conv3(a_c * a_x, conv_w)

    q = partial_rope(rmsnorm(d_q.reshape(b, s, DSA_HEADS, DSA_HEAD_DIM), dsa_q_norm), cos, sin)
    k = partial_rope(rmsnorm(d_k.reshape(b, s, 1, DSA_HEAD_DIM), dsa_k_norm), cos, sin)[:, :, 0]
    iq = partial_rope(i_q.reshape(b, s, IDX_HEADS, IDX_DIM), cos, sin)
    ik = partial_rope(i_k.reshape(b, s, 1, IDX_DIM), cos, sin)[:, :, 0]
    iw = i_w * (IDX_HEADS ** -0.5)
    y_b = dsa_attention(q, k, d_v, iq, ik, iw).reshape(b, s, DSA_HEADS * DSA_HEAD_DIM)

    hq = jax.nn.silu(g_q).reshape(b, s, HG_HEADS, HG_DK)
    zf = g_f.astype(jnp.float32).reshape(b, s, HG_HEADS, HG_DK)
    lbh = lb.reshape(HG_HEADS, HG_DK)
    log_f = jnp.logaddexp(jnp.log(lbh), jnp.log1p(-lbh) + jax.nn.log_sigmoid(zf))
    hk = -jnp.expm1(log_f)
    hv = g_i.reshape(b, s, HG_HEADS, HG_DV)
    o_c = hgrn2_chunkwise(hq, hk, hv, log_f).astype(x.dtype)
    o_c = rmsnorm(o_c, hgrn_out_norm) * jax.nn.silu(g_g.reshape(b, s, HG_HEADS, HG_DV))
    y_c = o_c.reshape(b, s, HG_HEADS * HG_DV)

    mk, mv = jnp.split(mem_n @ mem_w_kv, 2, axis=-1)
    mk = rmsnorm(mk.reshape(b, MEM_TOKENS, MEM_HEADS, MEM_HEAD_DIM), mem_k_norm)
    mv = mv.reshape(b, MEM_TOKENS, MEM_HEADS, MEM_HEAD_DIM)
    mq = rmsnorm(m_q.reshape(b, s, MEM_HEADS, MEM_HEAD_DIM), mem_q_norm)
    ml = jnp.einsum('bshd,bmhd->bhsm', mq, mk).astype(jnp.float32) * (MEM_HEAD_DIM ** -0.5)
    mp = jax.nn.softmax(ml, axis=-1).astype(mv.dtype)
    y_m = jnp.einsum('bhsm,bmhd->bshd', mp, mv).reshape(b, s, MEM_HEADS * MEM_HEAD_DIM)

    gates = jax.nn.sigmoid(gate_logits).reshape(b, s, N_BRANCH, D_MODEL)
    branches = (y_a, y_b, y_c, y_m)
    merged = gates[:, :, 0] * (branches[0] @ w_lift[0])
    for n in range(1, N_BRANCH):
        merged = merged + gates[:, :, n] * (branches[n] @ w_lift[n])
    x = x + merged @ w_out

    hf = rmsnorm(x, norm_ffn)
    gate, up = jnp.split(hf @ ffn_w_up, 2, axis=-1)
    return x + (jax.nn.silu(gate) * up) @ ffn_w_down

def second_inputs(seed: int = 0) -> dict:
    key = jax.random.key(seed)
    ks = jax.random.split(key, 20)
    f32 = jnp.float32

    def nrm(k, shape, scale):
        return jax.random.normal(k, shape, f32) * scale

    def gain(k, shape):
        return 1.0 + 0.02 * jax.random.normal(k, shape, f32)

    return {
        'x': nrm(ks[0], (BATCH, SEQ, D_MODEL), 1.0),
        'mem': nrm(ks[1], (BATCH, MEM_TOKENS, D_MODEL), 1.0),
        'positions': jnp.broadcast_to(jnp.arange(SEQ, dtype=jnp.int32), (BATCH, SEQ)),
        'norm_mix': gain(ks[2], (DEPTH_2, D_MODEL)),
        'w_in': nrm(ks[3], (DEPTH_2, D_MODEL, IN_COLS), D_MODEL ** -0.5),
        'conv_w': nrm(ks[4], (DEPTH_2, CONV_WIDTH, CONV_DIM), CONV_WIDTH ** -0.5),
        'dsa_q_norm': gain(ks[5], (DEPTH_2, DSA_HEAD_DIM)),
        'dsa_k_norm': gain(ks[6], (DEPTH_2, DSA_HEAD_DIM)),
        'hgrn_lower_bounds': nrm(ks[7], (DEPTH_2, HG_HEADS * HG_DK), 0.5),
        'hgrn_out_norm': gain(ks[8], (DEPTH_2, HG_DV)),
        'mem_norm': gain(ks[9], (D_MODEL,)),
        'mem_w_kv': nrm(ks[10], (DEPTH_2, D_MODEL, 2 * MEM_HEADS * MEM_HEAD_DIM), D_MODEL ** -0.5),
        'mem_q_norm': gain(ks[11], (DEPTH_2, MEM_HEAD_DIM)),
        'mem_k_norm': gain(ks[12], (DEPTH_2, MEM_HEAD_DIM)),
        'w_lift': nrm(ks[13], (DEPTH_2, N_BRANCH, BRANCH_DIM, D_MODEL), BRANCH_DIM ** -0.5),
        'w_out': nrm(ks[14], (DEPTH_2, D_MODEL, D_MODEL), D_MODEL ** -0.5),
        'norm_ffn': gain(ks[15], (DEPTH_2, D_MODEL)),
        'ffn_w_up': nrm(ks[16], (DEPTH_2, D_MODEL, 2 * FFN_DIM), D_MODEL ** -0.5),
        'ffn_w_down': nrm(ks[17], (DEPTH_2, FFN_DIM, D_MODEL), FFN_DIM ** -0.5),
    }

def second_block(x, mem, positions, norm_mix, w_in, conv_w, dsa_q_norm, dsa_k_norm,
              hgrn_lower_bounds, hgrn_out_norm, mem_norm, mem_w_kv, mem_q_norm, mem_k_norm,
              w_lift, w_out, norm_ffn, ffn_w_up, ffn_w_down):
    cos, sin = rope_tables_2(positions, x.dtype)
    mem_n = rmsnorm(mem, mem_norm)
    lbs = jnp.cumsum(jax.nn.softmax(hgrn_lower_bounds.astype(jnp.float32), axis=0), axis=0)
    lbs = lbs - lbs[0:1]
    for l in range(DEPTH_2):
        x = hybrid_layer(x, mem_n, cos, sin, lbs[l], norm_mix[l], w_in[l], conv_w[l],
                         dsa_q_norm[l], dsa_k_norm[l], hgrn_out_norm[l], mem_w_kv[l],
                         mem_q_norm[l], mem_k_norm[l], w_lift[l], w_out[l],
                         norm_ffn[l], ffn_w_up[l], ffn_w_down[l])
    return x


def setup_inputs(seed=0):
    out = dict(first_inputs(seed))
    for name, value in second_inputs(seed + 1).items():
        if name != "x":
            out[name + "_2"] = value
    return out


def reference(
    x, positions, ln_g, ln_b, a_w_qkv, a_b_qkv, a_sinks, a_w_o, a_b_o, b_w_qkv, b_w_o, c_w_qkv,
    c_w_o, w_gate_up, w_down, mem_2, positions_2, norm_mix_2, w_in_2, conv_w_2, dsa_q_norm_2,
    dsa_k_norm_2, hgrn_lower_bounds_2, hgrn_out_norm_2, mem_norm_2, mem_w_kv_2, mem_q_norm_2,
    mem_k_norm_2, w_lift_2, w_out_2, norm_ffn_2, ffn_w_up_2, ffn_w_down_2,
):
    x = first_block(
        x, positions, ln_g, ln_b, a_w_qkv, a_b_qkv, a_sinks, a_w_o, a_b_o, b_w_qkv, b_w_o,
        c_w_qkv, c_w_o, w_gate_up, w_down,
    )
    return second_block(
        x, mem_2, positions_2, norm_mix_2, w_in_2, conv_w_2, dsa_q_norm_2, dsa_k_norm_2,
        hgrn_lower_bounds_2, hgrn_out_norm_2, mem_norm_2, mem_w_kv_2, mem_q_norm_2,
        mem_k_norm_2, w_lift_2, w_out_2, norm_ffn_2, ffn_w_up_2, ffn_w_down_2,
    )


_drawn_inputs = setup_inputs


def setup_inputs(seed=0):
    import zlib

    import numpy as np

    out = dict(_drawn_inputs(seed))
    spreads = {}
    factors = {'a_b_qkv': 2.876,
     'a_sinks': 5.562,
     'dsa_q_norm_2': 8.0,
     'dsa_k_norm_2': 8.0,
     'hgrn_lower_bounds_2': 4.111,
     'hgrn_out_norm_2': 5.581,
     'mem_norm_2': 8.0,
     'mem_q_norm_2': 8.0,
     'mem_k_norm_2': 8.0,
     'norm_ffn_2': 2.752}
    for name, (base, spread) in spreads.items():
        noise = np.random.default_rng([zlib.crc32(name.encode()), seed]).standard_normal(out[name].shape)
        drawn = base * np.exp(spread * noise) if base else spread * noise
        out[name] = __import__('jax').numpy.asarray(drawn.astype(out[name].dtype))
    for name, factor in factors.items():
        out[name] = (out[name] * factor).astype(out[name].dtype)
    return out
```

```python
from contextlib import ExitStack

import concourse.bass as bass
from concourse import mybir
import numpy as np

F32 = mybir.dt.float32
F32R = mybir.dt.float32r
I32 = mybir.dt.int32
ALU = mybir.AluOpType
ACT = mybir.ActivationFunctionType
AX = mybir.AxisListType

P = 128
SEQ, D = 256, 1024
T = SEQ // P
KC = D // P
NW = 512
FF = 2816
FN = NW // 2
FJ = FF // FN
HD, ROT = 64, 16
HALF = ROT // 2
THETA = 500000.0
DEPTH, DEPTH2 = 4, 2
ALPHA = (2 * DEPTH) ** 0.25
NEG = -1e30
TAKEN = -3e38
LN_EPS, RMS_EPS = 1e-5, 1e-6
DILATIONS = (1, 4, 16)
A_REACH, B_REACH = 127, 128
TOPK = min(256, SEQ // 4)
GRP = 8
HG, HGD, HGC = 4, 128, 64
NCH = SEQ // HGC
TWO_PI = 2 * np.pi

SPLITS = (512, 512, 512, 512, 64, 64, 512, 64, 8, 512, 512, 512, 512, 512, 4096)
COL = [int(v) for v in np.cumsum((0,) + SPLITS)]
(C_AX, C_AB, C_AC, C_DQ, C_DK, C_DV, C_IQ, C_IK, C_IW, C_GQ, C_GF, C_GI, C_GG, C_MQ, C_GATE) = COL[:-1]
PI_PARTS = (6.28125, float(np.float32(TWO_PI - 6.28125)), float(TWO_PI - 6.28125 - float(np.float32(TWO_PI - 6.28125))))
PI_IN = 3.1415925
N_LOADED = 3 + DEPTH2 * 9
SMALL = 64 + 64 + 64 + 8


class Steps:

    def __init__(self, eng, sem):
        self.eng, self.sem, self.n = eng, sem, 0

    def did(self, ins):
        ins.then_inc(self.sem, 1)
        self.n += 1

    def settle(self):
        self.eng.wait_ge(self.sem, self.n)


def build(nc, x_in, positions, ln_g, ln_b, a_w_qkv, a_b_qkv, a_sinks, a_w_o, a_b_o, b_w_qkv, b_w_o, c_w_qkv, c_w_o,
          w_gate_up, w_down, mem, positions_2, norm_mix, w_in, conv_w, dsa_q_norm, dsa_k_norm, hg_lower, hg_out_norm,
          mem_norm, mem_w_kv, mem_q_norm, mem_k_norm, w_lift, w_out, norm_ffn, ffn_up, ffn_down, out):
    ctx = ExitStack()
    with ctx:
        def sb(name, shape, dt=F32):
            return ctx.enter_context(nc.sbuf_tensor(name, shape, dt))

        sems = {}

        def sem(name):
            sems[name] = ctx.enter_context(nc.semaphore(name))
            return sems[name]

        raw = sb("raw", [P, 2, KC * NW])
        whi = sb("whi", [P, 2, KC * NW], F32R)
        wlo = sb("wlo", [P, 2, KC * NW], F32R)
        xt_hi = sb("xt_hi", [P, KC, SEQ], F32R)
        xt_lo = sb("xt_lo", [P, KC, SEQ], F32R)
        yt_hi = sb("yt_hi", [P, 4, SEQ], F32R)
        yt_lo = sb("yt_lo", [P, 4, SEQ], F32R)
        x = sb("x", [P, T, D])
        r = sb("r", [P, T, D])
        tok = sb("tok", [P, 2, T, NW])
        sm = sb("sm", [P, 2, 768])
        pts = sb("pts", [P, 2, 768])
        masks = sb("masks", [P, 5, SEQ])
        zeros = sb("zeros", [P, SEQ])
        ident = sb("ident", [P, P])
        chmask = sb("chmask", [P, P])
        rope_c = sb("rope_c", [P, 2, T, HALF])
        rope_s = sb("rope_s", [P, 2, T, HALF])
        gains = sb("gains", [P, DEPTH2, 512])
        sinks = sb("sinks", [P, 2, 16])
        convw = sb("convw", [P, DEPTH2, 3, 4])
        lbp = sb("lbp", [P, 8, HG])
        small = sb("small", [P, 96])
        vst, rs, mhalf = small[:, 0:16], small[:, 16:32], small[:, 32:48]
        mxs = small[:, 48:64].rearrange("p (u s) -> p u s", s=4)
        mx1, nb, ls, rl = small[:, 64:68], small[:, 68:72], small[:, 72:76], small[:, 76:80]
        es = small[:, 80:84]
        mv = small[:, 84:88].rearrange("p (t s) -> p t s", s=2)
        bns = sb("bns", [P, T, 2, 6])
        iwb = sb("iwb", [P, T, 8])
        sk8 = sb("sk8", [P, 2, 16])
        hdl = sb("hdl", [P, NCH * HG])
        m8 = sb("m8", [P, GRP])
        AREA = 9 * 1024
        dn_off = -(-nc.sbuf_base // 32) * 32
        arena = sb("arena", [P, AREA])
        draw = nc.alloc_sbuf_tensor_at("draw", [P, 2, D], F32, offset=dn_off)
        dhi = nc.alloc_sbuf_tensor_at("dhi", [P, 2, D], F32R, offset=dn_off + 8 * D)
        dlo = nc.alloc_sbuf_tensor_at("dlo", [P, 2, D], F32R, offset=dn_off + 16 * D)
        gb = arena[:, 7 * 1024:9 * 1024].rearrange("p (a n) -> p a n", a=2)
        abias = arena[:, 3584:3584 + 1536]
        abo = arena[:, 5120:6144]

        def blk(i, n=1024):
            return arena[:, i * 1024:i * 1024 + n]

        pflat = pts[:, :, :].rearrange("p a b -> p (a b)")
        sqr, rtmp = pflat[:, 0:1024], pflat[:, 1024:1536].rearrange("p (k c) -> p k c", k=4)
        smflat = sm[:, :, :].rearrange("p a b -> p (a b)")
        hyc = smflat[:, 0:1024].rearrange("p (t c) -> p t c", t=T)
        hid = tok[:, 0].rearrange("p t c -> p (t c)").rearrange("p (b t f) -> p b t f", b=2, t=T)
        silu_g = tok[:, 1].rearrange("p t c -> p (t c)")[:, 0:T * FN].rearrange("p (t f) -> p t f", t=T)
        relu2 = blk(6).rearrange("p (b h s) -> p b h s", b=2, h=2)
        dist = blk(0, SEQ).bitcast(I32)
        dwork = blk(1, SEQ).bitcast(I32)
        rope_pos = blk(2, 2 * T).bitcast(I32).rearrange("p (b t) -> p b t", b=2)
        freq = blk(2)[:, 16:16 + HALF]
        rwork = blk(3, 6 * 2 * T * HALF).rearrange("p (k c) -> p k c", k=6)
        CH = NCH * HG
        HSTATE = [blk(0)[:, 0:512], blk(0)[:, 512:1024], blk(2)[:, 0:512]]

        def chunked(i):
            return blk(i).rearrange("p (c s) -> p c s", s=HGC)

        def headed(i):
            return blk(i).rearrange("p (h s) -> p h s", s=SEQ)

        def tiled(i):
            return blk(i).rearrange("p (t c) -> p t c", t=T)

        banks = {n: ctx.enter_context(nc.psum_tensor(f"bank_{n}", [P, 512], F32))
                 for n in ("L0", "L1", "S0", "S1", "T0", "T1", "O0", "O1")}
        LB, SB, TB, OB = (["L0", "L1"], ["S0", "S1"], ["T0", "T1"], ["O0", "O1"])
        ACC = [["S0", "S1"], ["O0", "O1"]]

        raw_full = [sem("raw_full0"), sem("raw_full1")]
        hi_done, lo_done = sem("hi_done"), sem("lo_done")
        draw_full, dhi_done, dlo_done = sem("draw_full"), sem("dhi_done"), sem("dlo_done")
        down_done = sem("down_done")
        lin_done = sem("lin_done")
        aev, dev = sem("act_evacuated"), sem("dve_evacuated")
        tp_done = sem("transposed")
        thi_done, tlo_done = sem("thi_done"), sem("tlo_done")
        turn_done = sem("turn_done")
        rope_done = sem("rope_done")
        s_done, ttr_done, nb_done = sem("s_done"), sem("ttr_done"), sem("nb_done")
        p_done, pt_done, pv_done = sem("p_done"), sem("pt_done"), sem("pv_done")
        rl_done, o_done = sem("rl_done"), sem("o_done")
        var_done, rstd_done = sem("var_done"), sem("rstd_done")
        x_ready = sem("x_ready")
        sg_done, h_done = sem("silu_done"), sem("hidden_done")
        loaded = sem("loaded")
        gb_full = sem("gb_full")
        const_done = sem("const_done")
        mask_done = sem("mask_done")
        trig = sem("trig")
        rel_done, rel_used = sem("rel_done"), sem("rel_used")
        conv_done = sem("conv_done")
        hg_act, hg_dve, hg_pe = sem("hg_act"), sem("hg_dve"), sem("hg_pe")
        sel_done = sem("sel_done")
        dve_step, act_step, pool_step = sem("dve_step"), sem("act_step"), sem("pool_step")
        out_full = sem("out_full")
        in_full = sem("in_full")
        rows_full = sem("rows_full")

        stages = []
        chunks = []
        n = dict(w=0, d=0, aev=0, dev=0, tp=0, sg=0, turn=0, rope=0, seg=0, unit=0, norm=0, stat=0, ffn=0, gb=0,
                 xr=0, h=0, rel=0, conv=0, hga=0, hgd=0, hgp=0, sel=0, inn=0)

        def add(kind, **kw):
            st = dict(kind=kind, at=dict(n), **kw)
            stages.append(st)
            return st

        def load_gains(rows, after):
            add("gains", rows=rows, after=after)
            n["gb"] += len(rows)

        def split(src, ready, dst, nkc=KC, dst_free=0):
            st = add("split", src=src, ready=ready, dst=dst, nkc=nkc)
            n["tp"] += nkc // 2
            n["sg"] += nkc // 2
            return (tlo_done, [st["at"]["sg"] + k // 2 + 1 for k in range(nkc)], dst)

        def linear(lhs, loads, ncols, evac, nkc=KC, turned=False, func=ACT.Copy, narrow=None, after=(), **kw):
            st = add("linear", lhs=lhs, ncols=ncols, nkc=nkc, turned=turned, evac=evac, w=n["w"], func=func,
                     narrow=narrow, after=after, **kw)
            chunks.append((loads, nkc, ncols))
            n["w"] += 1
            if evac in ("act",):
                n["aev"] += 2
            else:
                n["dev"] += 2
            return st

        def cols(w, c0, c1):
            return w[:, c0:c1].rearrange("(k p) n -> p k n", p=P)

        def turn(src, ready, dst, nb_=4):
            add("turn", src=src, ready=ready, dst=dst, nb=nb_)
            n["tp"] += T
            n["turn"] += T

        def rope(buf, nh, table, after):
            add("rope", buf=buf, nh=nh, table=table, after=after)
            n["rope"] += 1
            return (rope_done, n["rope"])

        def headnorm(buf, nh, hd, gain, after, gate=None):
            add("headnorm", buf=buf, nh=nh, hd=hd, gain=gain, after=after, gate=gate)
            n["stat"] += 1
            n["rope"] += 1
            return (rope_done, n["rope"])

        def attention(units, scale, ready):
            st = add("attention", units=units, scale=scale, ready=ready)
            seg = n["seg"]
            tp = n["tp"]
            for u in units:
                u["seg0"], u["tp0"] = seg, tp
                seg += len(u["segs"])
                tp += len(u["segs"])
            n["seg"], n["tp"] = seg, tp
            n["unit"] += len(units)
            return (o_done, n["unit"])

        def ffn(lhs, w_up, w_dn, dst, alpha):
            add("ffn", lhs=lhs, w=n["w"], d=n["d"], wu=w_up, wd=w_dn, dst=dst, alpha=alpha)
            for j in range(FJ):
                chunks.append((("ffn", w_up, j), KC, NW))
            n["w"] += FJ
            n["d"] += FJ
            n["dev"] += 4
            n["h"] += 2 * FJ
            n["tp"] += FJ
            n["sg"] += FJ
            return (dev, n["dev"])

        def layer_norm():
            add("layer_norm", gbv=n["gb"])
            n["stat"] += 1
            n["xr"] += T
            return (x_ready, n["xr"])

        def rms_norm(src, slot, after=None):
            add("rms_norm", src=src, slot=slot, after=after, gbv=n["gb"])
            n["stat"] += 1
            n["xr"] += T
            return (x_ready, n["xr"])

        tok_i = [0]

        def next_tok():
            tok_i[0] += 1
            return tok[:, tok_i[0] % 2]

        def causal(i, t):
            return (masks[:, i, P:SEQ], P) if t == 0 else (masks[:, i, :], SEQ)

        def head_ap(buf, h, c0, c1):
            return buf[HD * (h % 2):HD * (h % 2) + HD, h // 2, c0:c1]

        add("setup")
        n["stat"] += 0
        x_is = (in_full, 16)
        for i in range(DEPTH):
            kind, j = i % 3, i // 3
            lhs = split(x, x_is, (xt_hi, xt_lo))
            if kind == 0:
                qT = blk(0, 2048).rearrange("p (h s) -> p h s", s=SEQ)
                kT = blk(2, 1024).rearrange("p (h s) -> p h s", s=SEQ)
                vv = blk(3, 512).rearrange("p (t c) -> p t c", t=T)
                add("abias", j=j, after=[x_is])
                n["inn"] += 2
                pend = []
                for c in range(3):
                    tk = next_tok()
                    st = linear(lhs, [(0, cols(a_w_qkv[j], c * NW, (c + 1) * NW))], NW, "bias", tk=tk, c=c, v=vv,
                                inn=n["inn"])
                    done = (dev, n["dev"])
                    hs = tk.rearrange("p t (h d) -> p t h d", d=HD)
                    ok = rope(hs, 8, 0, done)
                    for f in pend:
                        turn(*f)
                    pend = [(tk, ok, qT[:, 4 * c:4 * c + 4] if c < 2 else kT)]
                for f in pend:
                    turn(*f)
                units = []
                for h in range(16):
                    for t in range(T):
                        m, nk = causal(1, t)
                        kv = h // 4
                        units.append(dict(
                            q=head_ap(qT, h, t * P, t * P + P),
                            segs=[(kT[HD * (h % 2):HD * (h % 2) + HD, kv, 0:nk], m, nk,
                                   [vv[:, s, kv * HD:kv * HD + HD] for s in range(nk // P)])],
                            o=r[:, t, h * HD:h * HD + HD], dv=HD, sink=(j, h)))
                o_is = attention(units, HD ** -0.5, [(turn_done, n["turn"]), (dev, n["dev"])])
                wo, bias = a_w_o[j], True
            elif kind == 1:
                qT = [blk(g).rearrange("p (h s) -> p h s", s=SEQ) for g in range(3)]
                kT = [blk(3 + g).rearrange("p (h s) -> p h s", s=SEQ) for g in range(3)]
                vv = [blk(6 + g).rearrange("p (t c) -> p t c", t=T) for g in range(3)]
                for half in range(2):
                    pend = []
                    for g in range(3):
                        for which in range(3):
                            c0 = (g * 3 + which) * D + half * NW
                            dst = vv[g] if which == 2 else next_tok()
                            after = [(o_done, n["unit"])] if which == 2 and n["unit"] else []
                            linear(lhs, [(0, cols(b_w_qkv[j], c0, c0 + NW))], NW, "act", dst=dst, after=after)
                            done = (aev, n["aev"])
                            if which < 2:
                                ok = rope(dst.rearrange("p t (h d) -> p t h d", d=HD), 8, 0, done)
                            for f in pend:
                                turn(*f)
                            pend = [(dst, ok, (qT, kT)[which][g])] if which < 2 else []
                    for f in pend:
                        turn(*f)
                    units = []
                    for h in range(8):
                        for t in range(T):
                            segs = []
                            for g in range(3):
                                m, nk = causal(2 + g, t)
                                segs.append((head_ap(kT[g], h, 0, nk), m, nk,
                                             [vv[g][:, s, h * HD:h * HD + HD] for s in range(nk // P)]))
                            hh = half * 8 + h
                            units.append(dict(q=[head_ap(qT[g], h, t * P, t * P + P) for g in range(3)], segs=segs,
                                              o=r[:, t, hh * HD:hh * HD + HD], dv=HD, sink=None))
                    o_is = attention(units, HD ** -0.5, [(turn_done, n["turn"]), (aev, n["aev"])])
                wo, bias = b_w_o[j], False
            else:
                qT = blk(0, 2048).rearrange("p (h s) -> p h s", s=SEQ)
                kT = blk(2, 2048).rearrange("p (h s) -> p h s", s=SEQ)
                vv = blk(4, 2048).rearrange("p (t c) -> p t c", t=T)
                pend = []
                for c in range(6):
                    which, half = c // 2, c % 2
                    dst = vv[:, :, half * NW:(half + 1) * NW] if which == 2 else next_tok()
                    linear(lhs, [(0, cols(c_w_qkv[j], c * NW, (c + 1) * NW))], NW, "act", dst=dst, after=[])
                    done = (aev, n["aev"])
                    if which < 2:
                        ok = rope(dst.rearrange("p t (h d) -> p t h d", d=HD), 8, 0, done)
                    for f in pend:
                        turn(*f)
                    pend = [(dst, ok, (qT, kT)[which][:, 4 * half:4 * half + 4])] if which < 2 else []
                units = []
                for h in range(16):
                    for t in range(T):
                        m, nk = causal(0, t)
                        units.append(dict(q=head_ap(qT, h, t * P, t * P + P),
                                          segs=[(head_ap(kT, h, 0, nk), m, nk,
                                                 [vv[:, s, h * HD:h * HD + HD] for s in range(nk // P)])],
                                          o=r[:, t, h * HD:h * HD + HD], dv=HD, sink=None))
                o_is = attention(units, HD ** -0.5, [(turn_done, n["turn"]), (aev, n["aev"])])
                wo, bias = c_w_o[j], False
            load_gains([ln_g[i, 0], ln_b[i, 0]], [o_is, (x_ready, n["xr"])])
            lhs = split(r, o_is, (xt_hi, xt_lo))
            for half in range(2):
                linear(lhs, [(0, cols(wo, half * NW, (half + 1) * NW))], NW, "resid", dst=r, alpha=ALPHA, half=half,
                       bias=abo if bias else None, split_r=True)
            x_is = layer_norm()
            lhs = split(x, x_is, (xt_hi, xt_lo))
            load_gains([ln_g[i, 1], ln_b[i, 1]], [x_is])
            ffn(lhs, w_gate_up[i], w_down[i], r, ALPHA)
            x_is = layer_norm()
        for l in range(DEPTH2):
            load_gains([mem_norm, norm_mix[l]], [x_is, (o_done, n["unit"])])
            add("load_mem", after=[x_is, (tp_done, n["tp"])])
            n["inn"] += 1
            m_is = rms_norm(r, 0, after=(rows_full, 16 * n["inn"]))
            lhs = split(r, m_is, (xt_hi, xt_lo))
            mkT = blk(0).rearrange("p (h s) -> p h s", s=SEQ)
            mvv = blk(1).rearrange("p (t c) -> p t c", t=T)
            mqT = blk(2).rearrange("p (h s) -> p h s", s=SEQ)
            tk = next_tok()
            linear(lhs, [(0, cols(mem_w_kv[l], 0, NW))], NW, "act", dst=tk, after=[])
            k_ok = headnorm(tk.rearrange("p t (h d) -> p t h d", d=128), 4, 128, gains[:, l, 384:512], (aev, n["aev"]))
            linear(lhs, [(0, cols(mem_w_kv[l], NW, 2 * NW))], NW, "act", dst=mvv, after=[])
            turn(tk, k_ok, mkT)
            h_is = rms_norm(x, 1)
            lhs = split(r, h_is, (xt_hi, xt_lo))

            def w_cols(c0, width=NW):
                return [(0, cols(w_in[l], c0, c0 + width))]

            def gates(branch):
                held = []
                for half in range(2):
                    gtk = next_tok()
                    linear(lhs, w_cols(C_GATE + branch * D + half * NW), NW, "act", dst=gtk, func=ACT.Sigmoid,
                           after=[(dev, n["dev"])])
                    held.append((gtk, n["aev"]))
                return held

            def lift(branch, ylhs, held, first=False):
                for half, (gtk, gate_is) in enumerate(held):
                    linear(ylhs, [(0, cols(w_lift[l, branch], half * NW, (half + 1) * NW))], NW, "lift", nkc=4,
                           gate=gtk, gate_is=gate_is, half=half, first=first)

            tk = next_tok()
            linear(lhs, w_cols(C_MQ), NW, "act", dst=tk, after=[])
            q_ok = headnorm(tk.rearrange("p t (h d) -> p t h d", d=128), 4, 128, gains[:, l, 256:384], (aev, n["aev"]))
            for b_, c0 in enumerate((C_AX, C_AC, C_AB)):
                linear(lhs, w_cols(c0), NW, "act", turned=True, dst=blk(4 + b_).rearrange("p (h s) -> p h s", s=SEQ),
                       after=[])
            conv_in = (aev, n["aev"])
            turn(tk, q_ok, mqT)
            ym = blk(3).rearrange("p (t c) -> p t c", t=T)
            units = []
            for h in range(4):
                for t in range(T):
                    units.append(dict(q=mqT[:, h, t * P:t * P + P],
                                      segs=[(mkT[:, h, :], zeros[:, :], SEQ,
                                             [mvv[:, s, h * 128:h * 128 + 128] for s in range(T)])],
                                      o=ym[:, t, h * 128:h * 128 + 128], dv=128, sink=None))
            o_is = attention(units, 128 ** -0.5, [(turn_done, n["turn"]), (aev, n["aev"])])
            ylhs = split(ym, o_is, (yt_hi, yt_lo), nkc=4)
            lift(3, ylhs, gates(3), first=True)
            add("conv", l=l, after=conv_in)
            n["conv"] += 1
            ylhs = (conv_done, [n["conv"]] * 4, (yt_hi, yt_lo))
            lift(0, ylhs, gates(0))
            hq = blk(0).rearrange("p (h s) -> p h s", s=SEQ)
            hz = blk(1).rearrange("p (h s) -> p h s", s=SEQ)
            hv, hgate = tok[:, 0], tok[:, 1]
            linear(lhs, w_cols(C_GF), NW, "act", turned=True, dst=hz, after=[])
            linear(lhs, w_cols(C_GQ), NW, "act", turned=True, dst=hq, func=ACT.Silu, after=[])
            counts = (n["hga"], n["hgd"], n["hgp"])
            add("decay_sums", l=l, counts=counts, aev_z=n["aev"] - 2)
            linear(lhs, w_cols(C_GI), NW, "act", dst=hv, after=[(dev, n["dev"])])
            add("decays", l=l, counts=counts)
            linear(lhs, w_cols(C_GG), NW, "act", dst=hgate, func=ACT.Silu, after=[(dev, n["dev"])])
            add("hgrn", l=l, counts=counts, aev_all=n["aev"], hv=hv)
            n["tp"] += T
            n["hga"] += 2 + (l > 0) + 2 * T
            n["hgd"] += 2 + (l > 0) + T + 3
            n["hgp"] += T + 3 + T
            y_ok = headnorm(hyc.rearrange("p t (h d) -> p t h d", d=128), 4, 128, gains[:, l, 128:256],
                            (hg_act, n["hga"]), gate=hgate.rearrange("p t (h d) -> p t h d", d=128))
            ylhs = split(hyc, y_ok, (yt_hi, yt_lo), nkc=4)
            lift(2, ylhs, gates(2))
            iqT = blk(0).rearrange("p (h s) -> p h s", s=SEQ)
            dqT = blk(1).rearrange("p (h s) -> p h s", s=SEQ)
            kkT = blk(2, 512).rearrange("p (h s) -> p h s", s=SEQ)
            kd = blk(2)[:, 512:1024].rearrange("p (t c) -> p t c", t=T)
            dvv = blk(3, 128).rearrange("p (t c) -> p t c", t=T)
            sel = blk(4, 512).rearrange("p (t c) -> p t c", t=T)
            yb = blk(5).rearrange("p (t c) -> p t c", t=T)
            linear(lhs, [(0, cols(w_in[l], C_DK, C_DK + 128)), (128, cols(w_in[l], C_IK, C_IK + 72))], SMALL, "act",
                   narrow=(kd, dvv), after=[])
            small_ok = (aev, n["aev"])
            headnorm(kd[:, :, 0:HD].rearrange("p t (h d) -> p t h d", d=HD), 1, HD, gains[:, l, 64:128], small_ok)
            rope(kd.rearrange("p t (h e) -> p t h e", e=128)[:, :, :, 0:HD], 2, 1, small_ok)
            add("dup", buf=kd.rearrange("p t (h e) -> p t h e", e=128))
            n["rope"] += 1
            kd_ok = (rope_done, n["rope"])
            tk = next_tok()
            linear(lhs, w_cols(C_DQ), NW, "act", dst=tk, after=[(dev, n["dev"])])
            headnorm(tk.rearrange("p t (h d) -> p t h d", d=HD), 8, HD, gains[:, l, 0:64], (aev, n["aev"]))
            q_ok = rope(tk.rearrange("p t (h d) -> p t h d", d=HD), 8, 1, (aev, n["aev"]))
            turn(kd, kd_ok, kkT, 2)
            tk2 = next_tok()
            linear(lhs, w_cols(C_IQ), NW, "act", dst=tk2, after=[(dev, n["dev"])])
            i_ok = rope(tk2.rearrange("p t (h d) -> p t h d", d=HD), 8, 1, (aev, n["aev"]))
            turn(tk, q_ok, dqT)
            turn(tk2, i_ok, iqT)
            add("ahead", w=n["w"] + 1)
            add("select", iqT=iqT, kkT=kkT, sel=sel, ready=(turn_done, n["turn"]))
            n["rel"] += 4 * T
            n["seg"] += 4 * T
            n["sel"] += T
            held_gates = gates(1)
            units = []
            for h in range(8):
                for t in range(T):
                    nk = P * (t + 1)
                    units.append(dict(q=head_ap(dqT, h, t * P, t * P + P),
                                      segs=[(kkT[HD * (h % 2):HD * (h % 2) + HD, 0, 0:nk], sel[:, t, 0:nk], nk,
                                             [dvv[:, s, :] for s in range(t + 1)])],
                                      o=yb[:, t, h * HD:h * HD + HD], dv=HD, sink=None))
            o_is = attention(units, HD ** -0.5, [(turn_done, n["turn"]), (aev, n["aev"])])
            ylhs = split(yb, o_is, (yt_hi, yt_lo), nkc=4)
            lift(1, ylhs, held_gates)
            load_gains([norm_ffn[l]], [(dev, n["dev"]), (o_done, n["unit"])])
            lhs = split(r, (dev, n["dev"]), (xt_hi, xt_lo))
            for half in range(2):
                linear(lhs, [(0, cols(w_out[l], half * NW, (half + 1) * NW))], NW, "resid", dst=x, alpha=1.0, half=half,
                       bias=None, split_r=False)
            h_is = rms_norm(x, 0)
            lhs = split(r, h_is, (xt_hi, xt_lo))
            x_is = ffn(lhs, ffn_up[l], ffn_down[l], x, 1.0)
        end = n
        WIDE = len(chunks)
        early = [st["w"] for st in stages if st["kind"] == "ahead"]

        pt_of, pt = [], 0
        for st in stages:
            if st["kind"] == "attention":
                for u in st["units"]:
                    pt_of.append(pt)
                    pt += len(u["segs"])

        full, count = [], [0, 0]
        for w, (loads, _, _) in enumerate(chunks):
            count[w % 2] += 16 * (2 if loads[0] == "ffn" else len(loads))
            full.append(count[w % 2])

        def wide(buf, w, nkc, ncols):
            return buf[:, w % 2, 0:nkc * ncols].rearrange("p (k n) -> p k n", n=ncols)

        block = ctx.enter_context(nc.Block())

        @block.sync
        def _(sp):
            sp.dma_start(x[:, :, :], x_in[0].rearrange("(t p) d -> p t d", p=P)).then_inc(in_full, 16)
            for st in stages:
                if st["kind"] == "linear":
                    w = st["w"]
                    loads, nkc, ncols = chunks[w]
                    if w >= 2:
                        sp.wait_ge(lo_done, 2 * (w - 1))
                    for c0, src in loads:
                        sp.dma_start(wide(raw, w, nkc, ncols)[:, :, c0:c0 + src.shape[2]], src) \
                          .then_inc(raw_full[w % 2], 16)
                elif st["kind"] == "ffn":
                    wu = st["wu"].rearrange("(k p) (g f) -> p k g f", p=P, g=2)
                    wd = st["wd"].rearrange("(j k p) n -> p (j k) n", k=2, p=P)

                    def up(j, s):
                        sp.wait_ge(lo_done, 2 * (st["w"] - 1) + 2 * j)
                        for g in range(2):
                            sp.dma_start(raw[:, s, :].rearrange("p (k g f) -> p k g f", k=KC, g=2)[:, :, g, :],
                                         wu[:, :, g, bass.ds(j * FN, FN)]).then_inc(raw_full[s], 16)

                    def down(j):
                        sp.wait_ge(dlo_done, st["d"] + j)
                        sp.dma_start(draw[:, :, :], wd[:, bass.ds(j * 2, 2), :]).then_inc(draw_full, 16)

                    up(0, st["w"] % 2)
                    up(1, (st["w"] + 1) % 2)
                    sp.wait_ge(o_done, st["at"]["unit"])
                    sp.wait_ge(dev, st["at"]["dev"])
                    down(0)
                    up(2, st["w"] % 2)
                    with sp.Fori(0, (FJ - 3) // 2) as i:
                        for u in range(2):
                            up(i * 2 + 3 + u, (st["w"] + 1 + u) % 2)
                            down(i * 2 + 1 + u)
                    down(FJ - 2)
                    down(FJ - 1)
            sp.wait_ge(dev, end["dev"])
            sp.dma_start(out[0].rearrange("(t p) d -> p t d", p=P), x[:, :, :]) \
              .then_inc(out_full, 16)
            sp.wait_ge(out_full, 16)

        @block.gpsimd
        def _(pool):
            for t_, pos in enumerate((positions, positions_2)):
                pool.dma_start(rope_pos[:, t_, :], pos[0].rearrange("(t p) -> p t", p=P), allow_slow_non_contiguous=True).then_inc(loaded, 16)
            pool.dma_start(sinks[:, :, :], a_sinks.partition_broadcast(P)).then_inc(loaded, 16)
            for l in range(DEPTH2):
                for k, (g, o, w) in enumerate(((dsa_q_norm, 0, 64), (dsa_k_norm, 64, 64), (hg_out_norm, 128, 128),
                                               (mem_q_norm, 256, 128), (mem_k_norm, 384, 128))):
                    pool.dma_start(gains[:, l, o:o + w], g[l].partition_broadcast(P)).then_inc(loaded, 16)
                for k in range(3):
                    pool.dma_start(convw[:, l, k, :], conv_w[l, k].rearrange("(b p) -> p b", p=P),
                                   allow_slow_non_contiguous=True).then_inc(loaded, 16)
                pool.dma_start(lbp[:, l, :], hg_lower[l].rearrange("(h p) -> p h", p=P),
                               allow_slow_non_contiguous=True).then_inc(loaded, 16)
            step = Steps(pool, pool_step)
            step.did(pool.memset(ident[:, :], 0.0))
            step.did(pool.memset(chmask[:, :], 1.0))
            step.settle()
            pool.affine_select(out=ident[:, :], in_=ident[:, :], compare_op=ALU.not_equal, fill=1.0, base=0,
                               pattern=[[-1, P]], channel_multiplier=1).then_inc(const_done, 1)
            step.did(pool.affine_select(out=chmask[:, :], in_=chmask[:, :], compare_op=ALU.is_ge, fill=0.0, base=0,
                                        pattern=[[1, P]], channel_multiplier=-1))
            step.settle()
            pool.memset(chmask[0:HGC, HGC:P], 0.0).then_inc(const_done, 1)
            pool.memset(mhalf, -0.5).then_inc(const_done, 1)
            pool.memset(zeros[:, :], 0.0).then_inc(const_done, 1)
            pool.iota(dist[:, :], pattern=[[-1, SEQ]], base=P, channel_multiplier=1).then_inc(const_done, 1)
            for i in range(HALF):
                pool.memset(freq[:, i:i + 1], float(np.float32(THETA) ** np.float32(-2.0 * i / ROT))) \
                    .then_inc(const_done, 1)

            def rstd(st, count, scale, eps):
                pool.wait_ge(var_done, st["at"]["stat"] + 1)
                step.did(pool.tensor_scalar(vst[:, 0:count], vst[:, 0:count], scale, eps, ALU.mult, ALU.add))
                step.settle()
                pool.tensor_tensor(rs[:, 0:count], vst[:, 0:count], mhalf[:, 0:count], ALU.pow).then_inc(rstd_done, 1)

            for st in stages:
                if st["kind"] == "gains":
                    for s_, v in st["after"]:
                        if v:
                            pool.wait_ge(s_, v)
                    for k, row in enumerate(st["rows"]):
                        pool.dma_start(gb[:, k, :], row.partition_broadcast(P)).then_inc(gb_full, 16)
                elif st["kind"] == "abias":
                    for s_, v in st["after"]:
                        pool.wait_ge(s_, v)
                    pool.dma_start(abias, a_b_qkv[st["j"]].partition_broadcast(P)).then_inc(rows_full, 16)
                    pool.dma_start(abo, a_b_o[st["j"]].partition_broadcast(P)).then_inc(rows_full, 16)
                elif st["kind"] == "load_mem":
                    for s_, v in st["after"]:
                        pool.wait_ge(s_, v)
                    pool.dma_start(r[:, :, :], mem[0].rearrange("(t p) d -> p t d", p=P)).then_inc(rows_full, 16)
                elif st["kind"] == "layer_norm":
                    rstd(st, T, 1.0, LN_EPS)
                elif st["kind"] == "rms_norm":
                    rstd(st, T, 1.0 / D, RMS_EPS)
                elif st["kind"] == "headnorm":
                    rstd(st, T * st["nh"], 1.0 / st["hd"], RMS_EPS)

        @block.scalar
        def _(act):
            step = Steps(act, act_step)

            def split_hi(w):
                if w >= WIDE:
                    return
                _, nkc, ncols = chunks[w]
                act.wait_ge(raw_full[w % 2], full[w])
                if w >= 2:
                    act.wait_ge(lin_done, 2 * (w - 1))
                for h in range(2):
                    ks = slice(h * nkc // 2, (h + 1) * nkc // 2)
                    act.activation(wide(whi, w, nkc, ncols)[:, ks, :], wide(raw, w, nkc, ncols)[:, ks, :], ACT.Copy) \
                       .then_inc(hi_done, 1)

            for st in stages:
                at = st["at"]
                if st["kind"] == "setup":
                    act.wait_ge(trig, 1)
                    act.activation(rope_c[:, :, :, :], rope_c[:, :, :, :], ACT.Sin).then_inc(trig, 1)
                    act.activation(rope_s[:, :, :, :], rope_s[:, :, :, :], ACT.Sin).then_inc(trig, 1)
                    step.did(act.activation(lbp[:, 3, :], lbp[:, 2, :], ACT.Abs))
                    step.settle()
                    step.did(act.activation(lbp[:, 4, :], lbp[:, 3, :], ACT.Exp, scale=-1.0))
                    step.settle()
                    act.activation(lbp[:, 5, :], lbp[:, 4, :], ACT.Ln, bias=1.0).then_inc(trig, 1)
                    split_hi(0)
                elif st["kind"] == "ahead":
                    split_hi(st["w"])
                elif st["kind"] == "linear":
                    if st["w"] + 1 not in early:
                        split_hi(st["w"] + 1)
                    if st["evac"] == "act":
                        for s_, v in st["after"]:
                            if v:
                                act.wait_ge(s_, v)
                        for t in range(T):
                            act.wait_ge(lin_done, 2 * st["w"] + t + 1)
                            ps = banks[LB[t]]
                            if st["turned"]:
                                act.activation(st["dst"][:, 2 * t:2 * t + 2, :],
                                               ps[:, :].rearrange("p (h s) -> p h s", s=SEQ), st["func"]).then_inc(aev, 1)
                            elif st["narrow"]:
                                kd, dvv = st["narrow"]
                                step.did(act.activation(kd[:, t, 0:HD], ps[:, 0:HD], ACT.Copy))
                                step.did(act.activation(dvv[:, t, :], ps[:, 64:128], ACT.Copy))
                                step.did(act.activation(kd[:, t, 128:128 + HD], ps[:, 128:192], ACT.Copy))
                                act.activation(iwb[:, t, :], ps[:, 192:200], ACT.Copy, scale=8 ** -0.5).then_inc(aev, 1)
                            else:
                                act.activation(st["dst"][:, t, :], ps[:, 0:st["ncols"]], st["func"]).then_inc(aev, 1)
                elif st["kind"] == "split":
                    hi, _ = st["dst"]
                    for g in range(st["nkc"] // 2):
                        act.wait_ge(tp_done, at["tp"] + g + 1)
                        act.activation(hi[:, 2 * g:2 * g + 2, :],
                                       banks[TB[(at["tp"] + g) % 2]][:, :].rearrange("p (k s) -> p k s", s=SEQ),
                                       ACT.Copy).then_inc(thi_done, 1)
                elif st["kind"] == "turn":
                    for t in range(T):
                        act.wait_ge(tp_done, at["tp"] + t + 1)
                        act.activation(st["dst"][:, 0:st["nb"], t * P:t * P + P],
                                       banks[TB[(at["tp"] + t) % 2]][:, 0:st["nb"] * P].rearrange("p (h s) -> p h s", s=P),
                                       ACT.Copy).then_inc(turn_done, 1)
                elif st["kind"] == "attention":
                    U = st["units"]

                    def exps(i):
                        u, k = U[i], at["unit"] + i
                        tot = sum(s[2] for s in u["segs"])
                        act.wait_ge(nb_done, k + 1)
                        if u["sink"]:
                            j, h = u["sink"]
                            step.did(act.activation(es[:, k % 4:k % 4 + 1], sinks[:, j, h:h + 1], ACT.Exp,
                                                    bias=nb[:, k % 4:k % 4 + 1]))
                        act.activation(sm[:, k % 2, 0:tot], sm[:, k % 2, 0:tot], ACT.Exp, bias=nb[:, k % 4:k % 4 + 1],
                                       scale=st["scale"], accum_out=ls[:, k % 4:k % 4 + 1]).then_inc(p_done, 1)

                    def evacuate(i):
                        u, k = U[i], at["unit"] + i
                        act.wait_ge(rl_done, k + 1)
                        act.wait_ge(pv_done, k + 1)
                        act.activation(u["o"], banks[OB[k % 2]][:, 0:u["dv"]], ACT.Copy,
                                       scale=rl[:, k % 4:k % 4 + 1]).then_inc(o_done, 1)

                    for i in range(len(U) + 2):
                        if i < len(U):
                            exps(i)
                        if i >= 2:
                            evacuate(i - 2)
                elif st["kind"] == "ffn":
                    w0, d0 = st["w"], st["d"]

                    def hi_up(j, s, f):
                        act.wait_ge(raw_full[s], f)
                        act.wait_ge(lin_done, 2 * (w0 - 1) + 2 * j)
                        for h in range(2):
                            q = slice(h * 2048, (h + 1) * 2048)
                            act.activation(whi[:, s, q], raw[:, s, q], ACT.Copy).then_inc(hi_done, 1)

                    def hi_down(j):
                        act.wait_ge(draw_full, 16 * (d0 + j + 1))
                        act.wait_ge(down_done, d0 + j)
                        act.activation(dhi[:, :, :], draw[:, :, :], ACT.Copy).then_inc(dhi_done, 1)

                    def silu(j, t):
                        act.wait_ge(lin_done, 2 * w0 + 2 * j + t + 1)
                        act.activation(silu_g[:, t, :], banks[LB[t]][:, 0:FN], ACT.Silu).then_inc(sg_done, 1)

                    def hidden_hi(j, b):
                        act.wait_ge(tp_done, at["tp"] + j + 1)
                        act.activation(yt_hi[:, 2 * b:2 * b + 2, :],
                                       banks[TB[(at["tp"] + b) % 2]][:, :].rearrange("p (k s) -> p k s", s=SEQ),
                                       ACT.Copy).then_inc(thi_done, 1)

                    def slot(j, u, f):
                        hi_up(j + 1, (w0 + u + 1) % 2, f)
                        hi_down(j - 1)
                        silu(j, 0)
                        hidden_hi(j - 1, (u + 1) % 2)
                        silu(j, 1)

                    split_hi(w0 + 1)
                    silu(0, 0)
                    silu(0, 1)
                    slot(1, 1, full[w0 + 2])
                    with act.Fori(0, (FJ - 3) // 2) as i:
                        slot(i * 2 + 2, 0, i * 32 + full[w0 + 3])
                        slot(i * 2 + 3, 1, i * 32 + full[w0 + 4])
                    hi_down(FJ - 2)
                    silu(FJ - 1, 0)
                    hidden_hi(FJ - 2, 1)
                    silu(FJ - 1, 1)
                    hi_down(FJ - 1)
                    split_hi(w0 + FJ)
                    hidden_hi(FJ - 1, 0)
                elif st["kind"] == "select":
                    for e in range(4 * T):
                        t, k = e // 4, at["rel"] + e
                        nk = P * (t + 1)
                        act.wait_ge(s_done, at["seg"] + e + 1)
                        if k >= 2:
                            act.wait_ge(rel_used, k - 1)
                        act.activation(relu2[:, k % 2, :, 0:nk],
                                       banks[SB[(at["seg"] + e) % 2]][:, :].rearrange("p (h s) -> p h s", s=SEQ)[:, :, 0:nk],
                                       ACT.Relu, scale=HD ** -0.5).then_inc(rel_done, 1)
                elif st["kind"] == "decay_sums":
                    k = 1 if st["l"] > 0 else 0
                    ha, hd_, hp = st["counts"]
                    act.wait_ge(aev, st["aev_z"])
                    step.did(act.activation(blk(2), blk(1), ACT.Abs))
                    step.settle()
                    step.did(act.activation(blk(2), blk(2), ACT.Exp, scale=-1.0))
                    step.settle()
                    act.activation(blk(2), blk(2), ACT.Ln, bias=1.0).then_inc(hg_act, 1)
                    if k:
                        act.wait_ge(hg_dve, hd_ + 1)
                        step.did(act.activation(blk(7), blk(7), ACT.Abs))
                        step.settle()
                        step.did(act.activation(blk(7), blk(7), ACT.Exp, scale=-1.0))
                        step.settle()
                        act.activation(blk(7), blk(7), ACT.Ln, bias=1.0).then_inc(hg_act, 1)
                elif st["kind"] == "decays":
                    k = 1 if st["l"] > 0 else 0
                    ha, hd_, hp = st["counts"]
                    act.wait_ge(hg_dve, hd_ + k + 1)
                    step.did(act.activation(blk(4), blk(4), ACT.Exp, scale=-1.0))
                    step.did(act.activation(blk(7), blk(6), ACT.Exp, scale=-1.0))
                    step.settle()
                    step.did(act.activation(blk(6), blk(6), ACT.Exp))
                    step.did(act.activation(blk(2), blk(5), ACT.Exp))
                    step.did(act.activation(hdl[:, :], chunked(5)[:, :, HGC - 1], ACT.Exp))
                    act.activation(blk(8), blk(8), ACT.Exp).then_inc(hg_act, 1)
                elif st["kind"] == "hgrn":
                    ha, hd_, hp = st["counts"]
                    for t in range(T):
                        act.wait_ge(tp_done, at["tp"] + t + 1)
                        act.activation(tiled(4)[:, t, :], banks[TB[(at["tp"] + t) % 2]][:, :], ACT.Copy) \
                           .then_inc(hg_act, 1)
                    for t in range(T):
                        act.wait_ge(hg_pe, hp + T + 3 + t + 1)
                        act.activation(hyc[:, t, :], banks[OB[t]][:, :], ACT.Copy).then_inc(hg_act, 1)

        @block.vector
        def _(dve):
            step = Steps(dve, dve_step)

            def split_lo(w):
                if w >= WIDE:
                    return
                _, nkc, ncols = chunks[w]
                for h in range(2):
                    ks = slice(h * nkc // 2, (h + 1) * nkc // 2)
                    dve.wait_ge(hi_done, 2 * w + h + 1)
                    dve.tensor_tensor(wide(wlo, w, nkc, ncols)[:, ks, :], wide(raw, w, nkc, ncols)[:, ks, :],
                                      wide(whi, w, nkc, ncols)[:, ks, :].bitcast(F32), ALU.subtract).then_inc(lo_done, 1)

            for st in stages:
                at = st["at"]
                if st["kind"] == "setup":
                    dve.wait_ge(const_done, 5 + HALF)
                    dve.wait_ge(loaded, 16 * N_LOADED)
                    ang, turns_i, turns_f, sub, r_, c_ = (rwork[:, q, :] for q in range(6))
                    for b in range(2):
                        for t in range(T):
                            q = (b * T + t) * HALF
                            step.did(dve.tensor_copy(sub[:, q:q + HALF],
                                                     rope_pos[:, b, t:t + 1].to_broadcast([P, HALF])))
                    step.settle()
                    for q in range(2 * T):
                        step.did(dve.tensor_tensor(ang[:, q * HALF:(q + 1) * HALF], sub[:, q * HALF:(q + 1) * HALF], freq,
                                                   ALU.mult))
                    step.settle()
                    step.did(dve.tensor_scalar(turns_i.bitcast(I32), ang, 1 / TWO_PI, None, ALU.mult))
                    step.settle()
                    step.did(dve.tensor_copy(turns_f, turns_i.bitcast(I32)))
                    step.settle()
                    src = ang
                    for part in PI_PARTS:
                        step.did(dve.scalar_tensor_tensor(out=r_, in0=turns_f, scalar=-part, in1=src, op0=ALU.mult,
                                                          op1=ALU.add))
                        step.settle()
                        src = r_
                    for op, edge, by in ((ALU.is_gt, np.pi, -TWO_PI), (ALU.is_lt, -np.pi, TWO_PI)):
                        step.did(dve.tensor_scalar(sub, r_, float(edge), float(by), op, ALU.mult))
                        step.settle()
                        step.did(dve.tensor_tensor(r_, r_, sub, ALU.add))
                        step.settle()
                    step.did(dve.tensor_scalar(c_, r_, float(np.pi / 2), None, ALU.add))
                    step.settle()
                    step.did(dve.tensor_scalar(sub, c_, float(np.pi), float(-TWO_PI), ALU.is_gt, ALU.mult))
                    step.settle()
                    step.did(dve.tensor_tensor(c_, c_, sub, ALU.add))
                    step.settle()
                    for dst, a in ((rope_s, r_), (rope_c, c_)):
                        step.did(dve.tensor_scalar(dst[:, :, :, :].rearrange("p b t c -> p (b t c)"), a, PI_IN, -PI_IN,
                                                   ALU.min, ALU.max))
                    dve.tensor_tensor(lbp[:, 2, :], lbp[:, 1, :], lbp[:, 0, :], ALU.subtract).then_inc(trig, 1)
                    step.did(dve.tensor_scalar(masks[:, 0, :], dist, 0, NEG, ALU.is_lt, ALU.mult))
                    step.did(dve.tensor_scalar(masks[:, 1, :], dist, A_REACH, NEG, ALU.is_gt, ALU.mult))
                    step.did(dve.tensor_scalar(masks[:, 2, :], dist, B_REACH, NEG, ALU.is_gt, ALU.mult))
                    for g, dil in enumerate(DILATIONS[1:]):
                        step.did(dve.tensor_scalar(dwork, dist, dil - 1, None, ALU.bitwise_and))
                        step.settle()
                        step.did(dve.tensor_scalar(masks[:, 3 + g, :], dwork, 0, NEG, ALU.is_gt, ALU.mult))
                        step.settle()
                    for q in range(1, 5):
                        step.did(dve.tensor_tensor(masks[:, q, :], masks[:, q, :], masks[:, 0, :], ALU.add))
                    step.did(dve.tensor_scalar(sk8[:, :, :], sinks[:, :, :], HD ** 0.5, None, ALU.mult))
                    dve.wait_ge(trig, 4)
                    step.did(dve.scalar_tensor_tensor(out=lbp[:, 6, :], in0=lbp[:, 2, :], scalar=0.0, in1=lbp[:, 5, :],
                                                      op0=ALU.min, op1=ALU.subtract))
                    step.settle()
                    step.did(dve.tensor_tensor(lbp[:, 7, :], lbp[:, 6, :], lbp[:, 2, :], ALU.subtract))
                    split_lo(0)
                    step.settle()
                elif st["kind"] == "ahead":
                    split_lo(st["w"])
                elif st["kind"] == "linear":
                    if st["w"] + 1 not in early:
                        split_lo(st["w"] + 1)
                    if st["evac"] == "act":
                        continue
                    if st["evac"] == "bias":
                        dve.wait_ge(rows_full, 16 * st["inn"])
                    if st["evac"] == "lift":
                        dve.wait_ge(aev, st["gate_is"])
                    for t in range(T):
                        dve.wait_ge(lin_done, 2 * st["w"] + t + 1)
                        ps = banks[LB[t]]
                        if st["evac"] == "bias":
                            c0 = st["c"] * NW
                            if st["c"] < 2:
                                dve.tensor_tensor(st["tk"][:, t, :], ps[:, :], abias[:, c0:c0 + NW], ALU.add).then_inc(dev, 1)
                                continue
                            kd = st["tk"][:, t, :].rearrange("p (h e d) -> p h e d", e=2, d=HD)
                            for e in range(2):
                                step.did(dve.tensor_tensor(kd[:, :, e, :],
                                                           ps[:, 0:256].rearrange("p (h d) -> p h d", d=HD),
                                                           abias[:, c0:c0 + 256].rearrange("p (h d) -> p h d", d=HD),
                                                           ALU.add))
                            dve.tensor_tensor(st["v"][:, t, :], ps[:, 256:512], abias[:, c0 + 256:c0 + 512], ALU.add) \
                               .then_inc(dev, 1)
                        elif st["evac"] == "resid":
                            h0 = st["half"] * NW
                            dst, old = st["dst"][:, t, h0:h0 + NW], x[:, t, h0:h0 + NW]
                            if st["bias"] is None:
                                dve.scalar_tensor_tensor(out=dst, in0=old, scalar=st["alpha"], in1=ps[:, :], op0=ALU.mult,
                                                         op1=ALU.add).then_inc(dev, 1)
                            else:
                                step.did(dve.scalar_tensor_tensor(out=dst, in0=old, scalar=st["alpha"], in1=ps[:, :],
                                                                  op0=ALU.mult, op1=ALU.add))
                                step.settle()
                                dve.tensor_tensor(dst, dst, st["bias"][:, h0:h0 + NW], ALU.add).then_inc(dev, 1)
                        else:
                            h0 = st["half"] * NW
                            if st["first"]:
                                dve.tensor_tensor(r[:, t, h0:h0 + NW], st["gate"][:, t, :], ps[:, :], ALU.mult) \
                                   .then_inc(dev, 1)
                            else:
                                step.did(dve.tensor_tensor(st["gate"][:, t, :], st["gate"][:, t, :], ps[:, :], ALU.mult))
                                step.settle()
                                dve.tensor_tensor(r[:, t, h0:h0 + NW], r[:, t, h0:h0 + NW], st["gate"][:, t, :], ALU.add) \
                                   .then_inc(dev, 1)
                elif st["kind"] == "split":
                    hi, lo = st["dst"]
                    for g in range(st["nkc"] // 2):
                        dve.wait_ge(thi_done, at["sg"] + g + 1)
                        dve.tensor_tensor(lo[:, 2 * g:2 * g + 2, :],
                                          banks[TB[(at["tp"] + g) % 2]][:, :].rearrange("p (k s) -> p k s", s=SEQ),
                                          hi[:, 2 * g:2 * g + 2, :].bitcast(F32), ALU.subtract).then_inc(tlo_done, 1)
                elif st["kind"] == "rope":
                    dve.wait_ge(*st["after"])
                    if at["rope"]:
                        dve.wait_ge(rope_done, at["rope"])
                    nh = st["nh"]
                    x1, x2 = st["buf"][:, :, :, 0:HALF], st["buf"][:, :, :, HALF:ROT]
                    cs, sn = (f[:, st["table"]].unsqueeze(2).to_broadcast([P, T, nh, HALF]) for f in (rope_c, rope_s))
                    tm = [rtmp[:, q, 0:T * nh * HALF].rearrange("p (t h c) -> p t h c", t=T, h=nh) for q in range(4)]
                    for q, (a, b) in enumerate(((x1, cs), (x2, sn), (x2, cs), (x1, sn))):
                        step.did(dve.tensor_tensor(tm[q], a, b, ALU.mult))
                    step.settle()
                    step.did(dve.tensor_tensor(x1, tm[0], tm[1], ALU.subtract))
                    dve.tensor_tensor(x2, tm[2], tm[3], ALU.add).then_inc(rope_done, 1)
                elif st["kind"] == "dup":
                    dve.wait_ge(rope_done, at["rope"])
                    dve.tensor_copy(st["buf"][:, :, :, HD:2 * HD], st["buf"][:, :, :, 0:HD]).then_inc(rope_done, 1)
                elif st["kind"] == "headnorm":
                    nh, hd = st["nh"], st["hd"]
                    dve.wait_ge(*st["after"])
                    if at["rope"]:
                        dve.wait_ge(rope_done, at["rope"])
                    sq = sqr[:, 0:T * nh * hd].rearrange("p (t h d) -> p t h d", t=T, h=nh)
                    step.did(dve.tensor_tensor(sq, st["buf"], st["buf"], ALU.mult))
                    step.settle()
                    dve.tensor_reduce(vst[:, 0:T * nh].rearrange("p (t h) -> p t h", t=T), sq, AX.X, ALU.add) \
                       .then_inc(var_done, 1)
                    dve.wait_ge(rstd_done, at["stat"] + 1)
                    by = rs[:, 0:T * nh].rearrange("p (t h) -> p t h", t=T).unsqueeze(3).to_broadcast([P, T, nh, hd])
                    step.did(dve.tensor_tensor(st["buf"], st["buf"], by, ALU.mult))
                    step.settle()
                    g = st["gain"].unsqueeze(1).unsqueeze(1).to_broadcast([P, T, nh, hd])
                    if st["gate"] is None:
                        dve.tensor_tensor(st["buf"], st["buf"], g, ALU.mult).then_inc(rope_done, 1)
                    else:
                        step.did(dve.tensor_tensor(st["buf"], st["buf"], g, ALU.mult))
                        step.settle()
                        dve.tensor_tensor(st["buf"], st["buf"], st["gate"], ALU.mult).then_inc(rope_done, 1)
                elif st["kind"] == "layer_norm":
                    dve.wait_ge(dev, at["dev"])
                    for t in range(T):
                        for h in range(2):
                            step.did(dve.bn_stats(bns[:, t, h, :], r[:, t, h * NW:(h + 1) * NW]))
                    step.settle()
                    for t in range(T):
                        step.did(dve.bn_aggr(mv[:, t, :], bns[:, t, :, :].rearrange("p h s -> p (h s)")))
                    step.settle()
                    dve.tensor_copy(vst[:, 0:T], mv[:, :, 1]).then_inc(var_done, 1)
                    dve.wait_ge(rstd_done, at["stat"] + 1)
                    dve.wait_ge(gb_full, 16 * st["gbv"])
                    for t in range(T):
                        step.did(dve.tensor_scalar(x[:, t, :], r[:, t, :], mv[:, t, 0:1], rs[:, t:t + 1], ALU.subtract,
                                                   ALU.mult))
                        step.settle()
                        step.did(dve.tensor_tensor(x[:, t, :], x[:, t, :], gb[:, 0, :], ALU.mult))
                        step.settle()
                        dve.tensor_tensor(x[:, t, :], x[:, t, :], gb[:, 1, :], ALU.add).then_inc(x_ready, 1)
                elif st["kind"] == "rms_norm":
                    dve.wait_ge(dev, at["dev"])
                    if st["after"]:
                        dve.wait_ge(*st["after"])
                    if at["xr"]:
                        dve.wait_ge(x_ready, at["xr"])
                    for t in range(T):
                        ins = dve.tensor_tensor_reduce(out=smflat[:, 0:D], in0=st["src"][:, t, :], in1=st["src"][:, t, :], scale=1.0,
                                                       scalar=0.0, op0=ALU.mult, op1=ALU.add, accum_out=vst[:, t:t + 1])
                        if t < T - 1:
                            step.did(ins)
                            step.settle()
                    ins.then_inc(var_done, 1)
                    dve.wait_ge(rstd_done, at["stat"] + 1)
                    dve.wait_ge(gb_full, 16 * st["gbv"])
                    for t in range(T):
                        dve.scalar_tensor_tensor(out=r[:, t, :], in0=st["src"][:, t, :], scalar=rs[:, t:t + 1],
                                                 in1=gb[:, st["slot"], :], op0=ALU.mult, op1=ALU.mult).then_inc(x_ready, 1)
                elif st["kind"] == "attention":
                    U = st["units"]
                    if at["sel"]:
                        dve.wait_ge(sel_done, at["sel"])

                    def maxima(i):
                        u, k = U[i], at["unit"] + i
                        off = 0
                        for q, (_, m, nk, _) in enumerate(u["segs"]):
                            dve.wait_ge(s_done, u["seg0"] + q + 1)
                            dve.tensor_tensor_reduce(out=sm[:, k % 2, off:off + nk],
                                                     in0=banks[SB[(u["seg0"] + q) % 2]][:, 0:nk], in1=m, scale=1.0,
                                                     scalar=TAKEN, op0=ALU.add, op1=ALU.max,
                                                     accum_out=mxs[:, k % 4, q:q + 1]).then_inc(ttr_done, 1)
                            off += nk
                        dve.wait_ge(ttr_done, pt_of[k] + len(u["segs"]))
                        mx = mxs[:, k % 4, 0:1]
                        one = mx1[:, k % 4:k % 4 + 1]
                        if len(u["segs"]) > 1:
                            step.did(dve.tensor_reduce(one, mxs[:, k % 4, 0:len(u["segs"])], AX.X, ALU.max))
                            step.settle()
                            mx = one
                        if u["sink"]:
                            j, h = u["sink"]
                            step.did(dve.tensor_tensor(one, mx, sk8[:, j, h:h + 1], ALU.max))
                            step.settle()
                            mx = one
                        dve.tensor_scalar(nb[:, k % 4:k % 4 + 1], mx, -st["scale"], None, ALU.mult).then_inc(nb_done, 1)

                    def copies(i):
                        u, k = U[i], at["unit"] + i
                        if k >= 2:
                            dve.wait_ge(pv_done, k - 1)
                        off = 0
                        for q, (_, _, nk, _) in enumerate(u["segs"]):
                            dve.wait_ge(tp_done, u["tp0"] + q + 1)
                            dve.tensor_copy(pts[:, k % 2, off:off + nk], banks[TB[(u["tp0"] + q) % 2]][:, 0:nk]) \
                               .then_inc(pt_done, 1)
                            off += nk

                    def reciprocal(i):
                        u, k = U[i], at["unit"] + i
                        q = slice(k % 4, k % 4 + 1)
                        dve.wait_ge(p_done, k + 1)
                        if u["sink"]:
                            step.did(dve.tensor_tensor(ls[:, q], ls[:, q], es[:, q], ALU.add))
                            step.settle()
                        dve.reciprocal(rl[:, q], ls[:, q]).then_inc(rl_done, 1)

                    for i in range(len(U) + 2):
                        if i < len(U):
                            maxima(i)
                        if 1 <= i <= len(U):
                            copies(i - 1)
                            reciprocal(i - 1)
                elif st["kind"] == "ffn":
                    w0, d0 = st["w"], st["d"]

                    def lo_up(j, s):
                        for h in range(2):
                            q = slice(h * 2048, (h + 1) * 2048)
                            dve.wait_ge(hi_done, 2 * w0 + 2 * j + h + 1)
                            dve.tensor_tensor(wlo[:, s, q], raw[:, s, q], whi[:, s, q].bitcast(F32), ALU.subtract) \
                               .then_inc(lo_done, 1)

                    def lo_down(j):
                        dve.wait_ge(dhi_done, d0 + j + 1)
                        dve.tensor_tensor(dlo[:, :, :], draw[:, :, :], dhi[:, :, :].bitcast(F32), ALU.subtract) \
                           .then_inc(dlo_done, 1)

                    def gated(j, t, b):
                        dve.wait_ge(sg_done, at["h"] + 2 * j + t + 1)
                        dve.tensor_tensor(hid[:, b, t, :], silu_g[:, t, :], banks[LB[t]][:, FN:2 * FN], ALU.mult) \
                           .then_inc(h_done, 1)

                    def hidden_lo(j, b):
                        dve.wait_ge(thi_done, at["sg"] + j + 1)
                        dve.tensor_tensor(yt_lo[:, 2 * b:2 * b + 2, :],
                                          banks[TB[(at["tp"] + b) % 2]][:, :].rearrange("p (k s) -> p k s", s=SEQ),
                                          yt_hi[:, 2 * b:2 * b + 2, :].bitcast(F32), ALU.subtract).then_inc(tlo_done, 1)

                    def slot(j, u):
                        lo_up(j + 1, (w0 + u + 1) % 2)
                        lo_down(j - 1)
                        gated(j, 0, u)
                        hidden_lo(j - 1, (u + 1) % 2)
                        gated(j, 1, u)

                    split_lo(w0 + 1)
                    gated(0, 0, 0)
                    gated(0, 1, 0)
                    slot(1, 1)
                    with dve.Fori(0, (FJ - 3) // 2) as i:
                        slot(i * 2 + 2, 0)
                        slot(i * 2 + 3, 1)
                    lo_down(FJ - 2)
                    gated(FJ - 1, 0, 0)
                    hidden_lo(FJ - 2, 1)
                    gated(FJ - 1, 1, 0)
                    lo_down(FJ - 1)
                    split_lo(w0 + FJ)
                    hidden_lo(FJ - 1, 0)
                    dve.wait_ge(down_done, d0 + FJ)
                    for t in range(T):
                        for h in range(2):
                            q = slice(h * NW, (h + 1) * NW)
                            dve.scalar_tensor_tensor(out=st["dst"][:, t, q], in0=x[:, t, q], scalar=st["alpha"],
                                                     in1=banks[ACC[t][h]][:, :], op0=ALU.mult, op1=ALU.add).then_inc(dev, 1)
                elif st["kind"] == "conv":
                    dve.wait_ge(*st["after"])
                    u, y = headed(4), headed(7)
                    step.did(dve.tensor_tensor(blk(4), blk(4), blk(5), ALU.mult))
                    step.settle()
                    for b in range(4):
                        step.did(dve.tensor_scalar(y[:, b, :], u[:, b, :], convw[:, st["l"], 2, b:b + 1], None, ALU.mult))
                    step.settle()
                    for back in (1, 2):
                        for b in range(4):
                            step.did(dve.scalar_tensor_tensor(out=y[:, b, back:SEQ], in0=u[:, b, 0:SEQ - back],
                                                              scalar=convw[:, st["l"], 2 - back, b:b + 1],
                                                              in1=y[:, b, back:SEQ], op0=ALU.mult, op1=ALU.add))
                        step.settle()
                    step.did(dve.tensor_tensor(blk(7), blk(7), blk(6), ALU.mult))
                    step.settle()
                    step.did(dve.tensor_copy(yt_hi[:, :, :], y))
                    step.settle()
                    dve.tensor_tensor(yt_lo[:, :, :], y, yt_hi[:, :, :].bitcast(F32), ALU.subtract).then_inc(conv_done, 1)
                elif st["kind"] == "decay_sums":
                    k = 1 if st["l"] > 0 else 0
                    ha, hd_, hp = st["counts"]
                    by_channel = [lbp[:, q, :].unsqueeze(2).to_broadcast([P, HG, SEQ]) for q in (6, 7)]
                    step.did(dve.memset(sqr, 1.0))
                    step.settle()
                    step.did(dve.memset(sqr.rearrange("p (c s) -> p c s", s=HGC)[:, :, 0:1], 0.0))
                    dve.wait_ge(hg_act, ha + 1)
                    step.did(dve.scalar_tensor_tensor(out=blk(3), in0=blk(1), scalar=0.0, in1=blk(2), op0=ALU.min,
                                                      op1=ALU.subtract))
                    step.did(dve.scalar_tensor_tensor(out=blk(4), in0=blk(1), scalar=0.0, in1=blk(2), op0=ALU.max,
                                                      op1=ALU.add))
                    step.settle()
                    if k:
                        step.did(dve.tensor_tensor(headed(3), headed(3), by_channel[1], ALU.add))
                        step.did(dve.tensor_tensor(headed(4), headed(4), by_channel[1], ALU.subtract))
                        step.settle()
                        dve.tensor_tensor(headed(7), headed(3), by_channel[0], ALU.subtract).then_inc(hg_dve, 1)
                        step.did(dve.tensor_tensor(headed(6), headed(3), by_channel[0], ALU.max))
                        dve.wait_ge(hg_act, ha + 2)
                        step.settle()
                        step.did(dve.tensor_tensor(blk(3), blk(6), blk(7), ALU.add))
                        step.settle()
                    step.did(dve.tensor_tensor_scan(blk(5), sqr, blk(3), 0.0, ALU.mult, ALU.add))
                    step.settle()
                    cum = chunked(5)
                    mid, last = (cum[:, :, q:q + 1].to_broadcast([P, CH, HGC]) for q in (HGC // 2 - 1, HGC - 1))
                    step.did(dve.tensor_tensor(chunked(6), cum, mid, ALU.subtract))
                    dve.tensor_tensor(chunked(8), last, cum, ALU.subtract).then_inc(hg_dve, 1)
                elif st["kind"] == "hgrn":
                    k = 1 if st["l"] > 0 else 0
                    ha, hd_, hp = st["counts"]
                    dve.wait_ge(hg_act, ha + k + 2)
                    dve.wait_ge(aev, st["aev_all"])
                    step.did(dve.tensor_tensor(blk(6), blk(0), blk(6), ALU.mult))
                    step.did(dve.tensor_tensor(blk(7), blk(4), blk(7), ALU.mult))
                    step.did(dve.tensor_tensor(blk(8), blk(4), blk(8), ALU.mult))
                    for q in (1, 3):
                        step.did(dve.memset(blk(q), 0.0))
                    step.settle()
                    for q, dst in enumerate((1, 3)):
                        even = [blk(z).rearrange("p (b c s) -> p b c s", c=2, s=HGC)[:, :, q, :] for z in (dst, 0, 2)]
                        ins = dve.tensor_tensor(even[0], even[1], even[2], ALU.mult)
                        if q == 0:
                            step.did(ins)
                    ins.then_inc(hg_dve, 1)
                    for t in range(T):
                        dve.wait_ge(hg_pe, hp + t + 1)
                        dve.tensor_tensor(tiled(5)[:, t, :].rearrange("p (h s) -> p h s", s=P),
                                          banks[SB[t]][:, :].rearrange("p (h s) -> p h s", s=P),
                                          chmask[:, :].unsqueeze(1).to_broadcast([P, HG, P]), ALU.mult).then_inc(hg_dve, 1)
                    dve.wait_ge(hg_pe, hp + T + 1)
                    dve.tensor_copy(HSTATE[0], banks["O0"][:, :]).then_inc(hg_dve, 1)
                    for c, bank in ((1, "O1"), (2, "S0")):
                        dve.wait_ge(hg_pe, hp + T + 1 + c)
                        dve.wait_ge(hg_dve, hd_ + k + 2 + T + c)
                        for h in range(HG):
                            q = slice(h * P, (h + 1) * P)
                            ins = dve.scalar_tensor_tensor(out=HSTATE[c][:, q], in0=HSTATE[c - 1][:, q],
                                                           scalar=hdl[:, h * NCH + c:h * NCH + c + 1],
                                                           in1=banks[bank][:, q], op0=ALU.mult, op1=ALU.add)
                            if h < HG - 1:
                                step.did(ins)
                        ins.then_inc(hg_dve, 1)
                elif st["kind"] == "select":
                    A, B = blk(7, 512).rearrange("p (b s) -> p b s", b=2), None
                    for t in range(T):
                        nk = P * (t + 1)
                        acc, alt = A[:, 0, 0:nk], A[:, 1, 0:nk]
                        m, _ = causal(0, t)
                        for e in range(4):
                            k = at["rel"] + 4 * t + e
                            dve.wait_ge(rel_done, k + 1)
                            for q in range(2):
                                h = 2 * (2 * (e % 2) + q) + e // 2
                                rel = relu2[:, k % 2, q, 0:nk]
                                w = iwb[:, t, h:h + 1]
                                if e == 0 and q == 0:
                                    ins = dve.tensor_scalar(acc, rel, w, None, ALU.mult)
                                else:
                                    ins = dve.scalar_tensor_tensor(out=acc, in0=rel, scalar=w, in1=acc, op0=ALU.mult,
                                                                   op1=ALU.add)
                                if q == 0:
                                    step.did(ins)
                                    step.settle()
                            ins.then_inc(rel_used, 1)
                            dve.wait_ge(rel_used, k + 1)
                        step.did(dve.tensor_tensor(acc, acc, m, ALU.add))
                        step.settle()
                        for _ in range(TOPK // GRP):
                            step.did(dve.max(m8[:, :], acc))
                            step.settle()
                            step.did(dve.match_replace(alt, m8[:, :], acc, TAKEN))
                            step.settle()
                            acc, alt = alt, acc
                        step.did(dve.tensor_scalar(st["sel"][:, t, 0:nk], acc, TAKEN / 2, NEG, ALU.is_gt, ALU.mult))
                        step.settle()
                        dve.tensor_tensor(st["sel"][:, t, 0:nk], st["sel"][:, t, 0:nk], m, ALU.add).then_inc(sel_done, 1)
                        dve.wait_ge(sel_done, at["sel"] + t + 1)

        @block.tensor
        def _(pe):
            held = {}

            def take(bank):
                if bank in held:
                    pe.wait_ge(*held.pop(bank))

            for st in stages:
                at = st["at"]
                if st["kind"] == "setup":
                    pe.wait_ge(const_done, 5 + HALF)
                elif st["kind"] == "split":
                    pe.wait_ge(*st["ready"])
                    for g in range(st["nkc"] // 2):
                        name = TB[(at["tp"] + g) % 2]
                        take(name)
                        for k in range(2):
                            for t in range(T):
                                c0, o0 = (2 * g + k) * P, k * SEQ + t * P
                                mm = pe.transpose(banks[name][:, o0:o0 + P], st["src"][:, t, c0:c0 + P], ident[:, :])
                        mm.then_inc(tp_done, 1)
                        held[name] = (tlo_done, at["sg"] + g + 1)
                elif st["kind"] == "turn":
                    pe.wait_ge(*st["ready"])
                    for t in range(T):
                        name = TB[(at["tp"] + t) % 2]
                        take(name)
                        for b in range(st["nb"]):
                            mm = pe.transpose(banks[name][:, b * P:(b + 1) * P], st["src"][:, t, b * P:(b + 1) * P], ident[:, :])
                        mm.then_inc(tp_done, 1)
                        held[name] = (turn_done, at["turn"] + t + 1)
                elif st["kind"] == "linear":
                    w, nkc = st["w"], st["nkc"]
                    ready, values, (xh, xl) = st["lhs"]
                    wh, wl = wide(whi, w, nkc, st["ncols"]), wide(wlo, w, nkc, st["ncols"])
                    frees = (aev, at["aev"]) if st["evac"] == "act" else (dev, at["dev"])

                    def needs(k):
                        if k % 2 == 0:
                            pe.wait_ge(ready, values[k + 1])
                        if k in (0, nkc // 2):
                            pe.wait_ge(lo_done, 2 * w + 1 + (k > 0))

                    for t in range(T):
                        ps = banks[LB[t]]
                        take(LB[t])
                        parts = [(0, st["ncols"], None)] if not st["turned"] else [(0, SEQ, 2 * t), (SEQ, 2 * SEQ, 2 * t + 1)]
                        for o0, o1, b in parts:
                            for k in range(nkc):
                                if t == 0 and o0 == 0:
                                    needs(k)
                                for q, (xx, ww) in enumerate(((xh, wh), (xl, wh), (xh, wl))):
                                    if st["turned"]:
                                        a, m = ww[:, k, b * P:(b + 1) * P], xx[:, k, :]
                                    else:
                                        a, m = xx[:, k, t * P:(t + 1) * P], ww[:, k, :]
                                    mm = pe.matmul(ps[:, o0:o1], a, m, start=(k == 0 and q == 0),
                                                   stop=(k == nkc - 1 and q == 2))
                        mm.then_inc(lin_done, 1)
                        held[LB[t]] = (frees[0], frees[1] + t + 1)
                elif st["kind"] == "attention":
                    U = st["units"]
                    for s_, v in st["ready"]:
                        pe.wait_ge(s_, v)

                    def scores(i):
                        u = U[i]
                        for q, (kk, _, nk, _) in enumerate(u["segs"]):
                            name = SB[(u["seg0"] + q) % 2]
                            take(name)
                            qq = u["q"][q] if len(u["segs"]) > 1 else u["q"]
                            pe.matmul(banks[name][:, 0:nk], qq, kk, start=True, stop=True).then_inc(s_done, 1)
                            held[name] = (ttr_done, pt_of[at["unit"] + i] + q + 1)

                    def turned(i):
                        u, k = U[i], at["unit"] + i
                        pe.wait_ge(p_done, k + 1)
                        off = 0
                        pt0 = pt_of[k]
                        for q, (_, _, nk, _) in enumerate(u["segs"]):
                            name = TB[(u["tp0"] + q) % 2]
                            take(name)
                            for c in range(0, nk, P):
                                mm = pe.transpose(banks[name][:, c:c + P], sm[:, k % 2, off + c:off + c + P], ident[:, :])
                            mm.then_inc(tp_done, 1)
                            held[name] = (pt_done, pt0 + q + 1)
                            off += nk

                    def values_(i):
                        u, k = U[i], at["unit"] + i
                        name = OB[k % 2]
                        take(name)
                        vs = [v for s_ in u["segs"] for v in s_[3]]
                        pe.wait_ge(pt_done, pt_of[k] + len(u["segs"]))
                        for c, v in enumerate(vs):
                            mm = pe.matmul(banks[name][:, 0:u["dv"]], pts[:, k % 2, c * P:(c + 1) * P], v, start=(c == 0),
                                           stop=(c == len(vs) - 1))
                        mm.then_inc(pv_done, 1)
                        held[name] = (o_done, k + 1)

                    for i in range(len(U) + 2):
                        if i < len(U):
                            scores(i)
                        if 1 <= i <= len(U):
                            turned(i - 1)
                        if i >= 2:
                            values_(i - 2)
                elif st["kind"] == "ffn":
                    w0, d0, sg0, tp0, h0 = st["w"], st["d"], at["sg"], at["tp"], at["h"]
                    ready, values, (xh, xl) = st["lhs"]
                    for name in list(held):
                        take(name)

                    def up(j, s, first=False):
                        wh, wl = (f[:, s, :].rearrange("p (k n) -> p k n", n=NW) for f in (whi, wlo))
                        for t in range(T):
                            if not first:
                                pe.wait_ge(h_done, h0 + 2 * j + t - 1)
                            for k in range(KC):
                                if t == 0 and first and k % 2 == 0:
                                    pe.wait_ge(ready, values[k + 1])
                                if t == 0 and k in (0, KC // 2):
                                    pe.wait_ge(lo_done, 2 * w0 + 2 * j + 1 + (k > 0))
                                for q, (xx, ww) in enumerate(((xh, wh), (xl, wh), (xh, wl))):
                                    mm = pe.matmul(banks[LB[t]][:, :], xx[:, k, t * P:(t + 1) * P], ww[:, k, :],
                                                   start=(k == 0 and q == 0), stop=(k == KC - 1 and q == 2))
                            mm.then_inc(lin_done, 1)
                            if t == 0 and not first:
                                turned_hidden(j - 1, (s + w0 + 1) % 2)

                    def turned_hidden(j, b):
                        name = TB[(tp0 + b) % 2]
                        pe.wait_ge(h_done, h0 + 2 * j + 2)
                        pe.wait_ge(tlo_done, sg0 + j - 1)
                        for k in range(2):
                            for t in range(T):
                                o0 = k * SEQ + t * P
                                mm = pe.transpose(banks[name][:, o0:o0 + P], hid[:, b, t, k * P:(k + 1) * P], ident[:, :])
                        mm.then_inc(tp_done, 1)

                    def down(j, b, first=False, last=False):
                        pe.wait_ge(dlo_done, d0 + j + 1)
                        pe.wait_ge(tlo_done, sg0 + j + 1)
                        for k in range(2):
                            for t in range(T):
                                for h in range(2):
                                    for q, (yy, ww) in enumerate(((yt_hi, dhi), (yt_lo, dhi), (yt_hi, dlo))):
                                        mm = pe.matmul(banks[ACC[t][h]][:, :], yy[:, 2 * b + k, t * P:(t + 1) * P],
                                                       ww[:, k, h * NW:(h + 1) * NW],
                                                       start=(first and k == 0 and q == 0),
                                                       stop=(last and k == 1 and q == 2))
                        mm.then_inc(down_done, 1)

                    up(0, w0 % 2, first=True)
                    up(1, (w0 + 1) % 2)
                    down(0, 0, first=True)
                    with pe.Fori(0, (FJ - 3) // 2) as i:
                        up(i * 2 + 2, w0 % 2)
                        down(i * 2 + 1, 1)
                        up(i * 2 + 3, (w0 + 1) % 2)
                        down(i * 2 + 2, 0)
                    up(FJ - 1, w0 % 2)
                    down(FJ - 2, 1)
                    turned_hidden(FJ - 1, 0)
                    down(FJ - 1, 0, last=True)
                    for q in range(4):
                        held[ACC[q // 2][q % 2]] = (dev, at["dev"] + q + 1)
                elif st["kind"] == "select":
                    pe.wait_ge(*st["ready"])
                    for e in range(4 * T):
                        t, half, pair = e // 4, (e % 4) // 2, e % 2
                        nk = P * (t + 1)
                        name = SB[(at["seg"] + e) % 2]
                        take(name)
                        q = slice(half * HD, (half + 1) * HD)
                        for b in range(2):
                            mm = pe.matmul(banks[name][:, b * SEQ:b * SEQ + nk], st["iqT"][q, 2 * pair + b, t * P:(t + 1) * P],
                                           st["kkT"][q, 1, 0:nk], start=True, stop=True)
                        mm.then_inc(s_done, 1)
                        held[name] = (rel_done, at["rel"] + e + 1)
                elif st["kind"] == "hgrn":
                    k = 1 if st["l"] > 0 else 0
                    ha, hd_, hp = st["counts"]
                    pe.wait_ge(hg_dve, hd_ + k + 2)
                    for t in range(T):
                        take(SB[t])
                        for h in range(HG):
                            q = slice(t * P, (t + 1) * P)
                            mm = pe.matmul(banks[SB[t]][:, h * P:(h + 1) * P], headed(7)[:, h, q], headed(6)[:, h, q],
                                           start=True, stop=True)
                        mm.then_inc(hg_pe, 1)
                        held[SB[t]] = (hg_dve, hd_ + k + 3 + t)
                    for t in range(T):
                        name = TB[(at["tp"] + t) % 2]
                        take(name)
                        for h in range(HG):
                            mm = pe.transpose(banks[name][:, h * P:(h + 1) * P], headed(8)[:, h, t * P:(t + 1) * P],
                                              ident[:, :])
                        mm.then_inc(tp_done, 1)
                        held[name] = (hg_act, ha + k + 3 + t)
                    pe.wait_ge(hg_act, ha + k + 2 + T)
                    pe.wait_ge(aev, st["aev_all"])
                    for c, name in enumerate(("O0", "O1", "S0")):
                        take(name)
                        rows = slice((c % 2) * HGC, (c % 2 + 1) * HGC)
                        for h in range(HG):
                            q = slice(h * P, (h + 1) * P)
                            mm = pe.matmul(banks[name][:, q], tiled(4)[rows, c // 2, q], st["hv"][rows, c // 2, q], start=True,
                                           stop=True)
                        mm.then_inc(hg_pe, 1)
                        held[name] = (hg_dve, hd_ + k + 2 + T + c + 1)
                    pe.wait_ge(hg_dve, hd_ + k + 2 + T + 3)
                    for t in range(T):
                        name = OB[t]
                        take(name)
                        for h in range(HG):
                            q = slice(h * P, (h + 1) * P)
                            pe.matmul(banks[name][:, q], tiled(5)[:, t, q], st["hv"][:, t, q], start=True, stop=False)
                            if t:
                                pe.matmul(banks[name][:, q], headed(1)[:, h, t * P:(t + 1) * P], HSTATE[2 * t - 1][:, q],
                                          start=False, stop=False)
                            mm = pe.matmul(banks[name][:, q], headed(3)[:, h, t * P:(t + 1) * P], HSTATE[2 * t][:, q],
                                           start=False, stop=True)
                        mm.then_inc(hg_pe, 1)
                        held[name] = (hg_act, ha + k + 2 + T + t + 1)


_INS = ["x", "positions", "ln_g", "ln_b", "a_w_qkv", "a_b_qkv", "a_sinks", "a_w_o", "a_b_o", "b_w_qkv", "b_w_o", "c_w_qkv",
        "c_w_o", "w_gate_up", "w_down", "mem_2", "positions_2", "norm_mix_2", "w_in_2", "conv_w_2", "dsa_q_norm_2",
        "dsa_k_norm_2", "hgrn_lower_bounds_2", "hgrn_out_norm_2", "mem_norm_2", "mem_w_kv_2", "mem_q_norm_2",
        "mem_k_norm_2", "w_lift_2", "w_out_2", "norm_ffn_2", "ffn_w_up_2", "ffn_w_down_2"]
_OUT = ((1, SEQ, D), "float32")


def kernel(**inputs):
    import concourse.bacc as _bacc
    from concourse.bass_utils import run_bass_kernel_spmd as _run

    nc = _bacc.Bacc("TRN2", target_bir_lowering=False, num_devices=1)
    arrays, args = {}, []
    for name in _INS:
        a = np.ascontiguousarray(inputs[name])
        arrays[f"in_{name}"] = a
        args.append(nc.dram_tensor(f"in_{name}", a.shape, mybir.dt.from_np(a.dtype), kind="ExternalInput").ap())
    args.append(nc.dram_tensor("out_0", _OUT[0], mybir.dt.from_np(np.dtype(_OUT[1])), kind="ExternalOutput").ap())
    build(nc, *args)
    return _run(nc, [arrays], core_ids=[0]).results[0]["out_0"]
```

```python
from contextlib import ExitStack

import concourse.bass as bass
from concourse import mybir
import numpy as np

F32 = mybir.dt.float32
F32R = mybir.dt.float32r
I32 = mybir.dt.int32
ALU = mybir.AluOpType
ACT = mybir.ActivationFunctionType
AX = mybir.AxisListType

P = 128
SEQ, D = 256, 1024
T = SEQ // P
KC = D // P
NW = 512
FF = 2816
FN = NW // 2
FJ = FF // FN
HD, ROT = 64, 16
HALF = ROT // 2
THETA = 500000.0
DEPTH, DEPTH2 = 4, 2
ALPHA = (2 * DEPTH) ** 0.25
NEG = -1e30
TAKEN = -3e38
LN_EPS, RMS_EPS = 1e-5, 1e-6
DILATIONS = (1, 4, 16)
A_REACH, B_REACH = 127, 128
TOPK = min(256, SEQ // 4)
GRP = 8
HG, HGD, HGC = 4, 128, 64
NCH = SEQ // HGC
TWO_PI = 2 * np.pi

SPLITS = (512, 512, 512, 512, 64, 64, 512, 64, 8, 512, 512, 512, 512, 512, 4096)
COL = [int(v) for v in np.cumsum((0,) + SPLITS)]
(C_AX, C_AB, C_AC, C_DQ, C_DK, C_DV, C_IQ, C_IK, C_IW, C_GQ, C_GF, C_GI, C_GG, C_MQ, C_GATE) = COL[:-1]
PI_PARTS = (6.28125, float(np.float32(TWO_PI - 6.28125)), float(TWO_PI - 6.28125 - float(np.float32(TWO_PI - 6.28125))))
PI_IN = 3.1415925
N_LOADED = 3 + DEPTH2 * 9
SMALL = 64 + 64 + 64 + 8


class Steps:

    def __init__(self, eng, sem):
        self.eng, self.sem, self.n = eng, sem, 0

    def did(self, ins):
        ins.then_inc(self.sem, 1)
        self.n += 1

    def settle(self):
        self.eng.wait_ge(self.sem, self.n)


def build(nc, x_in, positions, ln_g, ln_b, a_w_qkv, a_b_qkv, a_sinks, a_w_o, a_b_o, b_w_qkv, b_w_o, c_w_qkv, c_w_o,
          w_gate_up, w_down, mem, positions_2, norm_mix, w_in, conv_w, dsa_q_norm, dsa_k_norm, hg_lower, hg_out_norm,
          mem_norm, mem_w_kv, mem_q_norm, mem_k_norm, w_lift, w_out, norm_ffn, ffn_up, ffn_down, out):
    ctx = ExitStack()
    with ctx:
        def sb(name, shape, dt=F32):
            return ctx.enter_context(nc.sbuf_tensor(name, shape, dt))

        sems = {}

        def sem(name):
            sems[name] = ctx.enter_context(nc.semaphore(name))
            return sems[name]

        raw = sb("raw", [P, 2, KC * NW])
        whi = sb("whi", [P, 2, KC * NW], F32R)
        wlo = sb("wlo", [P, 2, KC * NW], F32R)
        xt_hi = sb("xt_hi", [P, KC, SEQ], F32R)
        xt_lo = sb("xt_lo", [P, KC, SEQ], F32R)
        yt_hi = sb("yt_hi", [P, 4, SEQ], F32R)
        yt_lo = sb("yt_lo", [P, 4, SEQ], F32R)
        x = sb("x", [P, T, D])
        r = sb("r", [P, T, D])
        tok = sb("tok", [P, 2, T, NW])
        sm = sb("sm", [P, 2, 768])
        pts = sb("pts", [P, 2, 768])
        masks = sb("masks", [P, 5, SEQ])
        zeros = sb("zeros", [P, SEQ])
        ident = sb("ident", [P, P])
        chmask = sb("chmask", [P, P])
        rope_c = sb("rope_c", [P, 2, T, HALF])
        rope_s = sb("rope_s", [P, 2, T, HALF])
        gains = sb("gains", [P, DEPTH2, 512])
        sinks = sb("sinks", [P, 2, 16])
        convw = sb("convw", [P, DEPTH2, 3, 4])
        lbp = sb("lbp", [P, 8, HG])
        small = sb("small", [P, 112])
        vst, rs, mhalf = small[:, 0:16], small[:, 16:32], small[:, 32:48]
        mv = small[:, 48:52].rearrange("p (t s) -> p t s", s=2)
        mxs = small[:, 56:72].rearrange("p (u s) -> p u s", s=4)
        mx1, nb, ls, rl, es = (small[:, q:q + 8].rearrange("p (u s) -> p u s", s=2) for q in range(72, 112, 8))
        bns = sb("bns", [P, T, 2, 6])
        iwb = sb("iwb", [P, T, 8])
        sk8 = sb("sk8", [P, 2, 16])
        hdl = sb("hdl", [P, NCH * HG])
        m8 = sb("m8", [P, GRP])
        AREA = 9 * 1024
        dn_off = -(-nc.sbuf_base // 32) * 32
        arena = sb("arena", [P, AREA])
        draw = nc.alloc_sbuf_tensor_at("draw", [P, 2, D], F32, offset=dn_off)
        dhi = nc.alloc_sbuf_tensor_at("dhi", [P, 2, D], F32R, offset=dn_off + 8 * D)
        dlo = nc.alloc_sbuf_tensor_at("dlo", [P, 2, D], F32R, offset=dn_off + 16 * D)
        gb = arena[:, 7 * 1024:9 * 1024].rearrange("p (a n) -> p a n", a=2)
        abias = arena[:, 3584:3584 + 1536]
        abo = arena[:, 5120:6144]

        def blk(i, n=1024):
            return arena[:, i * 1024:i * 1024 + n]

        pflat = pts[:, :, :].rearrange("p a b -> p (a b)")
        sqr, rtmp = pflat[:, 0:1024], pflat[:, 1024:1536].rearrange("p (k c) -> p k c", k=4)
        smflat = sm[:, :, :].rearrange("p a b -> p (a b)")
        hyc = smflat[:, 0:1024].rearrange("p (t c) -> p t c", t=T)
        hid = tok[:, 0].rearrange("p t c -> p (t c)").rearrange("p (b t f) -> p b t f", b=2, t=T)
        silu_g = tok[:, 1].rearrange("p t c -> p (t c)")[:, 0:T * FN].rearrange("p (t f) -> p t f", t=T)
        relu2 = blk(6).rearrange("p (b h s) -> p b h s", b=2, h=2)
        dist = blk(0, SEQ).bitcast(I32)
        dwork = blk(1, SEQ).bitcast(I32)
        rope_pos = blk(2, 2 * T).bitcast(I32).rearrange("p (b t) -> p b t", b=2)
        freq = blk(2)[:, 16:16 + HALF]
        rwork = blk(3, 6 * 2 * T * HALF).rearrange("p (k c) -> p k c", k=6)
        CH = NCH * HG
        HSTATE = [blk(0)[:, 0:512], blk(0)[:, 512:1024], blk(2)[:, 0:512]]

        def chunked(i):
            return blk(i).rearrange("p (c s) -> p c s", s=HGC)

        def headed(i):
            return blk(i).rearrange("p (h s) -> p h s", s=SEQ)

        def tiled(i):
            return blk(i).rearrange("p (t c) -> p t c", t=T)

        banks = {n: ctx.enter_context(nc.psum_tensor(f"bank_{n}", [P, 512], F32))
                 for n in ("L0", "L1", "S0", "S1", "T0", "T1", "O0", "O1")}
        LB, SB, TB, OB = (["L0", "L1"], ["S0", "S1"], ["T0", "T1"], ["O0", "O1"])
        QB = SB + LB
        ACC = [["S0", "S1"], ["O0", "O1"]]

        raw_full = [sem("raw_full0"), sem("raw_full1")]
        hi_done, lo_done = sem("hi_done"), sem("lo_done")
        draw_full, dhi_done, dlo_done = sem("draw_full"), sem("dhi_done"), sem("dlo_done")
        down_done = sem("down_done")
        sum_done = sem("sum_done")
        lin_done = sem("lin_done")
        aev, dev = sem("act_evacuated"), sem("dve_evacuated")
        tp_done = sem("transposed")
        thi_done, tlo_done = sem("thi_done"), sem("tlo_done")
        turn_done = sem("turn_done")
        rope_done = sem("rope_done")
        s_done, ttr_done, nb_done = sem("s_done"), sem("ttr_done"), sem("nb_done")
        p_done, pt_done, pv_done = sem("p_done"), sem("pt_done"), sem("pv_done")
        rl_done, o_done = sem("rl_done"), sem("o_done")
        var_done, rstd_done = sem("var_done"), sem("rstd_done")
        x_ready = sem("x_ready")
        sg_done, h_done = sem("silu_done"), sem("hidden_done")
        loaded = sem("loaded")
        gb_full = sem("gb_full")
        const_done = sem("const_done")
        mask_done = sem("mask_done")
        trig = sem("trig")
        rel_done, rel_used = sem("rel_done"), sem("rel_used")
        conv_done = sem("conv_done")
        hg_act, hg_dve, hg_pe = sem("hg_act"), sem("hg_dve"), sem("hg_pe")
        sel_done = sem("sel_done")
        dve_step, act_step, pool_step = sem("dve_step"), sem("act_step"), sem("pool_step")
        out_full = sem("out_full")
        in_full = sem("in_full")
        rows_full = sem("rows_full")

        stages = []
        chunks = []
        n = dict(w=0, d=0, aev=0, dev=0, tp=0, sg=0, turn=0, rope=0, seg=0, unit=0, norm=0, stat=0, ffn=0, gb=0,
                 xr=0, h=0, ttr=0, p=0, pt=0, rel=0, conv=0, hga=0, hgd=0, hgp=0, sel=0, inn=0)

        def add(kind, **kw):
            st = dict(kind=kind, at=dict(n), **kw)
            stages.append(st)
            return st

        def load_gains(rows, after):
            add("gains", rows=rows, after=after)
            n["gb"] += len(rows)

        def split(src, ready, dst, nkc=KC, dst_free=0):
            st = add("split", src=src, ready=ready, dst=dst, nkc=nkc)
            n["tp"] += nkc // 2
            n["sg"] += nkc // 2
            return (tlo_done, [[st["at"]["sg"] + k // 2 + 1 for k in range(nkc)]] * T, dst)

        second = [None]

        def take_second():
            st, second[0] = second[0], None
            return st

        def renorm(norm, dst, alpha, lhs=None, weights=None, bias=None):
            st = add("renorm", norm=norm, dst=dst, alpha=alpha, lhs=lhs, bias=bias, w=n["w"], gbv=n["gb"],
                     rows=x if norm == "layer" else r)
            if lhs:
                for half in range(2):
                    chunks.append(([(0, cols(weights, half * NW, (half + 1) * NW))], KC, NW))
                n["w"] += 2
            n["dev"] += 2 * T
            n["stat"] += T
            n["xr"] += T
            n["tp"] += 2 * T
            n["sg"] += 2 * T
            second[0] = st
            return (tlo_done, [[st["at"]["sg"] + 2 * t + k // 4 + 1 for k in range(KC)] for t in range(T)], (xt_hi, xt_lo))

        def linear(lhs, loads, ncols, evac, nkc=KC, turned=False, func=ACT.Copy, narrow=None, after=(), **kw):
            st = add("linear", lhs=lhs, second=take_second(), ncols=ncols, nkc=nkc, turned=turned, evac=evac, w=n["w"], func=func,
                     narrow=narrow, after=after, **kw)
            chunks.append((loads, nkc, ncols))
            n["w"] += 1
            if evac in ("act",):
                n["aev"] += 2
            else:
                n["dev"] += 2
            return st

        def cols(w, c0, c1):
            return w[:, c0:c1].rearrange("(k p) n -> p k n", p=P)

        def turn(src, ready, dst, nb_=4):
            add("turn", src=src, ready=ready, dst=dst, nb=nb_)
            n["tp"] += T
            n["turn"] += T

        def rope(buf, nh, table, after):
            add("rope", buf=buf, nh=nh, table=table, after=after)
            n["rope"] += 1
            return (rope_done, n["rope"])

        def headnorm(buf, nh, hd, gain, after, gate=None):
            add("headnorm", buf=buf, nh=nh, hd=hd, gain=gain, after=after, gate=gate)
            n["stat"] += 1
            n["rope"] += 1
            return (rope_done, n["rope"])

        def attention(units, scale, ready):
            add("attention", units=units, scale=scale, ready=ready)
            for u in units:
                u["seg0"], u["ttr0"], u["p0"], u["tp0"], u["pt0"] = n["seg"], n["ttr"], n["p"], n["tp"], n["pt"]
                u["pieces"], off, bank, used = [], 0, 0, 0
                for row, (pieces, _, _) in enumerate(u["rows"]):
                    for mask, products in pieces:
                        width = sum(c for _, _, c in products)
                        if used + width > NW:
                            bank, used = bank + 1, 0
                        u["pieces"].append((row, off, width, bank, used, mask, products))
                        off, used = off + width, used + width
                u["cols"], u["banks"] = off, bank + 1
                u["turns"] = [(c, min(c + 3 * P if off > NW else c + NW, off)) for c in range(0, off, 3 * P if off > NW else NW)]
                n["seg"] += u["banks"]
                n["ttr"] += len(u["pieces"])
                n["p"] += 1
                n["tp"] += len(u["turns"])
                n["pt"] += len(u["turns"])
            n["unit"] += len(units)
            return (o_done, n["unit"])

        def ffn(lhs, w_up, w_dn, dst, alpha, evacuate=False):
            add("ffn", lhs=lhs, second=take_second(), w=n["w"], d=n["d"], wu=w_up, wd=w_dn, dst=dst, alpha=alpha,
                evacuate=evacuate, index=n["ffn"])
            n["ffn"] += 1
            for j in range(FJ):
                chunks.append((("ffn", w_up, j), KC, NW))
            n["w"] += FJ
            n["d"] += FJ
            n["dev"] += 4 if evacuate else 0
            n["h"] += 2 * FJ
            n["tp"] += FJ
            n["sg"] += FJ
            return (dev, n["dev"])

        def layer_norm():
            add("layer_norm", gbv=n["gb"])
            n["stat"] += 1
            n["xr"] += T
            return (x_ready, n["xr"])

        def rms_norm(src, slot, after=None):
            add("rms_norm", src=src, slot=slot, after=after, gbv=n["gb"])
            n["stat"] += 1
            n["xr"] += T
            return (x_ready, n["xr"])

        tok_i = [0]

        def next_tok():
            tok_i[0] += 1
            return tok[:, tok_i[0] % 2]

        def causal(i, t):
            return (masks[:, i, P:SEQ], P) if t == 0 else (masks[:, i, :], SEQ)

        def head_ap(buf, h, c0, c1):
            return buf[HD * (h % 2):HD * (h % 2) + HD, h // 2, c0:c1]

        add("setup")
        n["stat"] += 0
        x_is = (in_full, 16)
        lhs = split(x, x_is, (xt_hi, xt_lo))
        for i in range(DEPTH):
            kind, j = i % 3, i // 3
            if kind == 0:
                qT = blk(0, 2048).rearrange("p (h s) -> p h s", s=SEQ)
                kT = blk(2, 1024).rearrange("p (h s) -> p h s", s=SEQ)
                vv = blk(3, 512).rearrange("p (t c) -> p t c", t=T)
                add("abias", j=j, after=[x_is])
                n["inn"] += 2
                pend = []
                for c in range(3):
                    tk = next_tok()
                    st = linear(lhs, [(0, cols(a_w_qkv[j], c * NW, (c + 1) * NW))], NW, "bias", tk=tk, c=c, v=vv,
                                inn=n["inn"])
                    done = (dev, n["dev"])
                    hs = tk.rearrange("p t (h d) -> p t h d", d=HD)
                    ok = rope(hs, 8, 0, done)
                    for f in pend:
                        turn(*f)
                    pend = [(tk, ok, qT[:, 4 * c:4 * c + 4] if c < 2 else kT)]
                for f in pend:
                    turn(*f)
                units = []
                for h in range(16):
                    kv, rows = h // 4, []
                    for t in range(T):
                        m, nk = causal(1, t)
                        rows.append(([(m, [(head_ap(qT, h, t * P, t * P + P),
                                            kT[HD * (h % 2):HD * (h % 2) + HD, kv, 0:nk], nk)])],
                                     [vv[:, s, kv * HD:kv * HD + HD] for s in range(nk // P)],
                                     r[:, t, h * HD:h * HD + HD]))
                    units.append(dict(rows=rows, dv=HD, sink=(j, h)))
                o_is = attention(units, HD ** -0.5, [(turn_done, n["turn"]), (dev, n["dev"])])
                wo, bias = a_w_o[j], True
            elif kind == 1:
                qT = [blk(g).rearrange("p (h s) -> p h s", s=SEQ) for g in range(3)]
                kT = [blk(3 + g).rearrange("p (h s) -> p h s", s=SEQ) for g in range(3)]
                vv = [blk(6 + g).rearrange("p (t c) -> p t c", t=T) for g in range(3)]
                for half in range(2):
                    pend = []
                    for g in range(3):
                        for which in range(3):
                            c0 = (g * 3 + which) * D + half * NW
                            dst = vv[g] if which == 2 else next_tok()
                            after = [(o_done, n["unit"])] if which == 2 and n["unit"] else []
                            linear(lhs, [(0, cols(b_w_qkv[j], c0, c0 + NW))], NW, "act", dst=dst, after=after)
                            done = (aev, n["aev"])
                            if which < 2:
                                ok = rope(dst.rearrange("p t (h d) -> p t h d", d=HD), 8, 0, done)
                            for f in pend:
                                turn(*f)
                            pend = [(dst, ok, (qT, kT)[which][g])] if which < 2 else []
                    for f in pend:
                        turn(*f)
                    units = []
                    for h in range(8):
                        hh = half * 8 + h
                        for t in range(T):
                            k0, nk = (P, P) if t == 0 else (0, SEQ)
                            prod = [(head_ap(qT[g], h, t * P, t * P + P), head_ap(kT[g], h, 0, nk), nk) for g in range(3)]
                            pieces = [(masks[:, 2:5, P:SEQ], prod)] if t == 0 else \
                                [(masks[:, 2:4, :], prod[0:2]), (masks[:, 4, :], prod[2:3])]
                            rows = [(pieces, [vv[g][:, s, h * HD:h * HD + HD] for g in range(3) for s in range(nk // P)],
                                     r[:, t, hh * HD:hh * HD + HD])]
                            units.append(dict(rows=rows, dv=HD, sink=None))
                    o_is = attention(units, HD ** -0.5, [(turn_done, n["turn"]), (aev, n["aev"])])
                wo, bias = b_w_o[j], False
            else:
                qT = blk(0, 2048).rearrange("p (h s) -> p h s", s=SEQ)
                kT = blk(2, 2048).rearrange("p (h s) -> p h s", s=SEQ)
                vv = blk(4, 2048).rearrange("p (t c) -> p t c", t=T)
                pend = []
                for c in range(6):
                    which, half = c // 2, c % 2
                    dst = vv[:, :, half * NW:(half + 1) * NW] if which == 2 else next_tok()
                    linear(lhs, [(0, cols(c_w_qkv[j], c * NW, (c + 1) * NW))], NW, "act", dst=dst, after=[])
                    done = (aev, n["aev"])
                    if which < 2:
                        ok = rope(dst.rearrange("p t (h d) -> p t h d", d=HD), 8, 0, done)
                    for f in pend:
                        turn(*f)
                    pend = [(dst, ok, (qT, kT)[which][:, 4 * half:4 * half + 4])] if which < 2 else []
                units = []
                for h in range(16):
                    rows = []
                    for t in range(T):
                        m, nk = causal(0, t)
                        rows.append(([(m, [(head_ap(qT, h, t * P, t * P + P), head_ap(kT, h, 0, nk), nk)])],
                                     [vv[:, s, h * HD:h * HD + HD] for s in range(nk // P)],
                                     r[:, t, h * HD:h * HD + HD]))
                    units.append(dict(rows=rows, dv=HD, sink=None))
                o_is = attention(units, HD ** -0.5, [(turn_done, n["turn"]), (aev, n["aev"])])
                wo, bias = c_w_o[j], False
            load_gains([ln_g[i, 0], ln_b[i, 0]], [o_is, (x_ready, n["xr"])])
            lhs = split(r, o_is, (xt_hi, xt_lo))
            lhs = renorm("layer", r, ALPHA, lhs, wo, abo if bias else None)
            x_is = (x_ready, n["xr"])
            load_gains([ln_g[i, 1], ln_b[i, 1]], [x_is])
            ffn(lhs, w_gate_up[i], w_down[i], r, ALPHA, evacuate=(i == DEPTH - 1))
            if i < DEPTH - 1:
                lhs = renorm("layer", r, ALPHA)
                x_is = (x_ready, n["xr"])
            else:
                x_is = layer_norm()
        for l in range(DEPTH2):
            load_gains([mem_norm, norm_mix[l]], [x_is, (o_done, n["unit"])])
            add("load_mem", after=[x_is, (tp_done, n["tp"])])
            n["inn"] += 1
            m_is = rms_norm(r, 0, after=(rows_full, 16 * n["inn"]))
            lhs = split(r, m_is, (xt_hi, xt_lo))
            mkT = blk(0).rearrange("p (h s) -> p h s", s=SEQ)
            mvv = blk(1).rearrange("p (t c) -> p t c", t=T)
            mqT = blk(2).rearrange("p (h s) -> p h s", s=SEQ)
            tk = next_tok()
            linear(lhs, [(0, cols(mem_w_kv[l], 0, NW))], NW, "act", dst=tk, after=[])
            k_ok = headnorm(tk.rearrange("p t (h d) -> p t h d", d=128), 4, 128, gains[:, l, 384:512], (aev, n["aev"]))
            linear(lhs, [(0, cols(mem_w_kv[l], NW, 2 * NW))], NW, "act", dst=mvv, after=[])
            turn(tk, k_ok, mkT)
            h_is = rms_norm(x, 1)
            lhs = split(r, h_is, (xt_hi, xt_lo))

            def w_cols(c0, width=NW):
                return [(0, cols(w_in[l], c0, c0 + width))]

            def gates(branch):
                held = []
                for half in range(2):
                    gtk = next_tok()
                    linear(lhs, w_cols(C_GATE + branch * D + half * NW), NW, "act", dst=gtk, func=ACT.Sigmoid,
                           after=[(dev, n["dev"])])
                    held.append((gtk, n["aev"]))
                return held

            def lift(branch, ylhs, held, first=False):
                for half, (gtk, gate_is) in enumerate(held):
                    linear(ylhs, [(0, cols(w_lift[l, branch], half * NW, (half + 1) * NW))], NW, "lift", nkc=4,
                           gate=gtk, gate_is=gate_is, half=half, first=first)

            tk = next_tok()
            linear(lhs, w_cols(C_MQ), NW, "act", dst=tk, after=[])
            q_ok = headnorm(tk.rearrange("p t (h d) -> p t h d", d=128), 4, 128, gains[:, l, 256:384], (aev, n["aev"]))
            for b_, c0 in enumerate((C_AX, C_AC, C_AB)):
                linear(lhs, w_cols(c0), NW, "act", turned=True, dst=blk(4 + b_).rearrange("p (h s) -> p h s", s=SEQ),
                       after=[])
            conv_in = (aev, n["aev"])
            turn(tk, q_ok, mqT)
            ym = blk(3).rearrange("p (t c) -> p t c", t=T)
            units = []
            for h in range(4):
                units.append(dict(dv=128, sink=None, rows=[
                    ([(zeros[:, :], [(mqT[:, h, t * P:t * P + P], mkT[:, h, :], SEQ)])],
                     [mvv[:, s, h * 128:h * 128 + 128] for s in range(T)], ym[:, t, h * 128:h * 128 + 128])
                    for t in range(T)]))
            o_is = attention(units, 128 ** -0.5, [(turn_done, n["turn"]), (aev, n["aev"])])
            ylhs = split(ym, o_is, (yt_hi, yt_lo), nkc=4)
            lift(3, ylhs, gates(3), first=True)
            add("conv", l=l, after=conv_in)
            n["conv"] += 1
            ylhs = (conv_done, [[n["conv"]] * 4] * T, (yt_hi, yt_lo))
            lift(0, ylhs, gates(0))
            hq = blk(0).rearrange("p (h s) -> p h s", s=SEQ)
            hz = blk(1).rearrange("p (h s) -> p h s", s=SEQ)
            hv, hgate = tok[:, 0], tok[:, 1]
            linear(lhs, w_cols(C_GF), NW, "act", turned=True, dst=hz, after=[])
            linear(lhs, w_cols(C_GQ), NW, "act", turned=True, dst=hq, func=ACT.Silu, after=[])
            counts = (n["hga"], n["hgd"], n["hgp"])
            add("decay_sums", l=l, counts=counts, aev_z=n["aev"] - 2)
            linear(lhs, w_cols(C_GI), NW, "act", dst=hv, after=[(dev, n["dev"])])
            add("decays", l=l, counts=counts)
            linear(lhs, w_cols(C_GG), NW, "act", dst=hgate, func=ACT.Silu, after=[(dev, n["dev"])])
            add("hgrn", l=l, counts=counts, aev_all=n["aev"], hv=hv)
            n["tp"] += T
            n["hga"] += 2 + (l > 0) + 2 * T
            n["hgd"] += 2 + (l > 0) + T + 3
            n["hgp"] += T + 3 + T
            y_ok = headnorm(hyc.rearrange("p t (h d) -> p t h d", d=128), 4, 128, gains[:, l, 128:256],
                            (hg_act, n["hga"]), gate=hgate.rearrange("p t (h d) -> p t h d", d=128))
            ylhs = split(hyc, y_ok, (yt_hi, yt_lo), nkc=4)
            lift(2, ylhs, gates(2))
            iqT = blk(0).rearrange("p (h s) -> p h s", s=SEQ)
            dqT = blk(1).rearrange("p (h s) -> p h s", s=SEQ)
            kkT = blk(2, 512).rearrange("p (h s) -> p h s", s=SEQ)
            kd = blk(2)[:, 512:1024].rearrange("p (t c) -> p t c", t=T)
            dvv = blk(3, 128).rearrange("p (t c) -> p t c", t=T)
            sel = blk(4, 512).rearrange("p (t c) -> p t c", t=T)
            yb = blk(5).rearrange("p (t c) -> p t c", t=T)
            linear(lhs, [(0, cols(w_in[l], C_DK, C_DK + 128)), (128, cols(w_in[l], C_IK, C_IK + 72))], SMALL, "act",
                   narrow=(kd, dvv), after=[])
            small_ok = (aev, n["aev"])
            headnorm(kd[:, :, 0:HD].rearrange("p t (h d) -> p t h d", d=HD), 1, HD, gains[:, l, 64:128], small_ok)
            rope(kd.rearrange("p t (h e) -> p t h e", e=128)[:, :, :, 0:HD], 2, 1, small_ok)
            add("dup", buf=kd.rearrange("p t (h e) -> p t h e", e=128))
            n["rope"] += 1
            kd_ok = (rope_done, n["rope"])
            tk = next_tok()
            linear(lhs, w_cols(C_DQ), NW, "act", dst=tk, after=[(dev, n["dev"])])
            headnorm(tk.rearrange("p t (h d) -> p t h d", d=HD), 8, HD, gains[:, l, 0:64], (aev, n["aev"]))
            q_ok = rope(tk.rearrange("p t (h d) -> p t h d", d=HD), 8, 1, (aev, n["aev"]))
            turn(kd, kd_ok, kkT, 2)
            tk2 = next_tok()
            linear(lhs, w_cols(C_IQ), NW, "act", dst=tk2, after=[(dev, n["dev"])])
            i_ok = rope(tk2.rearrange("p t (h d) -> p t h d", d=HD), 8, 1, (aev, n["aev"]))
            turn(tk, q_ok, dqT)
            turn(tk2, i_ok, iqT)
            add("ahead", w=n["w"] + 1)
            add("select", iqT=iqT, kkT=kkT, sel=sel, ready=(turn_done, n["turn"]))
            n["rel"] += 4 * T
            n["seg"] += 4 * T
            n["sel"] += T
            held_gates = gates(1)
            units = []
            for h in range(8):
                rows = []
                for t in range(T):
                    nk = P * (t + 1)
                    rows.append(([(sel[:, t, 0:nk], [(head_ap(dqT, h, t * P, t * P + P),
                                                      kkT[HD * (h % 2):HD * (h % 2) + HD, 0, 0:nk], nk)])],
                                 [dvv[:, s, :] for s in range(t + 1)], yb[:, t, h * HD:h * HD + HD]))
                units.append(dict(rows=rows, dv=HD, sink=None))
            o_is = attention(units, HD ** -0.5, [(turn_done, n["turn"]), (aev, n["aev"])])
            ylhs = split(yb, o_is, (yt_hi, yt_lo), nkc=4)
            lift(1, ylhs, held_gates)
            load_gains([norm_ffn[l]], [(dev, n["dev"]), (o_done, n["unit"])])
            lhs = split(r, (dev, n["dev"]), (xt_hi, xt_lo))
            lhs = renorm("rms", x, 1.0, lhs, w_out[l])
            x_is = ffn(lhs, ffn_up[l], ffn_down[l], x, 1.0, evacuate=True)
        end = n
        WIDE = len(chunks)
        early = [st["w"] for st in stages if st["kind"] == "ahead"]

        full, count = [], [0, 0]
        for w, (loads, _, _) in enumerate(chunks):
            count[w % 2] += 16 * (2 if loads[0] == "ffn" else len(loads))
            full.append(count[w % 2])

        def wide(buf, w, nkc, ncols):
            return buf[:, w % 2, 0:nkc * ncols].rearrange("p (k n) -> p k n", n=ncols)

        block = ctx.enter_context(nc.Block())

        @block.sync
        def _(sp):
            sp.dma_start(x[:, :, :], x_in[0].rearrange("(t p) d -> p t d", p=P)).then_inc(in_full, 16)
            for st in stages:
                if st["kind"] == "linear" or st["kind"] == "renorm" and st["lhs"]:
                    for w in range(st["w"], st["w"] + (2 if st["kind"] == "renorm" else 1)):
                        loads, nkc, ncols = chunks[w]
                        if w >= 2:
                            sp.wait_ge(lo_done, 2 * (w - 1))
                        for c0, src in loads:
                            sp.dma_start(wide(raw, w, nkc, ncols)[:, :, c0:c0 + src.shape[2]], src) \
                              .then_inc(raw_full[w % 2], 16)
                elif st["kind"] == "ffn":
                    wu = st["wu"].rearrange("(k p) (g f) -> p k g f", p=P, g=2)
                    wd = st["wd"].rearrange("(j k p) n -> p (j k) n", k=2, p=P)

                    def up(j, s):
                        sp.wait_ge(lo_done, 2 * (st["w"] - 1) + 2 * j)
                        for g in range(2):
                            sp.dma_start(raw[:, s, :].rearrange("p (k g f) -> p k g f", k=KC, g=2)[:, :, g, :],
                                         wu[:, :, g, bass.ds(j * FN, FN)]).then_inc(raw_full[s], 16)

                    def down(j):
                        sp.wait_ge(dlo_done, st["d"] + j)
                        sp.dma_start(draw[:, :, :], wd[:, bass.ds(j * 2, 2), :]).then_inc(draw_full, 16)

                    up(0, st["w"] % 2)
                    up(1, (st["w"] + 1) % 2)
                    sp.wait_ge(o_done, st["at"]["unit"])
                    sp.wait_ge(dev, st["at"]["dev"])
                    down(0)
                    up(2, st["w"] % 2)
                    with sp.Fori(0, (FJ - 3) // 2) as i:
                        for u in range(2):
                            up(i * 2 + 3 + u, (st["w"] + 1 + u) % 2)
                            down(i * 2 + 1 + u)
                    down(FJ - 2)
                    down(FJ - 1)
            sp.wait_ge(dev, end["dev"])
            sp.dma_start(out[0].rearrange("(t p) d -> p t d", p=P), x[:, :, :]) \
              .then_inc(out_full, 16)
            sp.wait_ge(out_full, 16)

        @block.gpsimd
        def _(pool):
            for t_, pos in enumerate((positions, positions_2)):
                pool.dma_start(rope_pos[:, t_, :], pos[0].rearrange("(t p) -> p t", p=P), allow_slow_non_contiguous=True).then_inc(loaded, 16)
            pool.dma_start(sinks[:, :, :], a_sinks.partition_broadcast(P)).then_inc(loaded, 16)
            for l in range(DEPTH2):
                for k, (g, o, w) in enumerate(((dsa_q_norm, 0, 64), (dsa_k_norm, 64, 64), (hg_out_norm, 128, 128),
                                               (mem_q_norm, 256, 128), (mem_k_norm, 384, 128))):
                    pool.dma_start(gains[:, l, o:o + w], g[l].partition_broadcast(P)).then_inc(loaded, 16)
                for k in range(3):
                    pool.dma_start(convw[:, l, k, :], conv_w[l, k].rearrange("(b p) -> p b", p=P),
                                   allow_slow_non_contiguous=True).then_inc(loaded, 16)
                pool.dma_start(lbp[:, l, :], hg_lower[l].rearrange("(h p) -> p h", p=P),
                               allow_slow_non_contiguous=True).then_inc(loaded, 16)
            step = Steps(pool, pool_step)
            step.did(pool.memset(ident[:, :], 0.0))
            step.did(pool.memset(chmask[:, :], 1.0))
            step.settle()
            pool.affine_select(out=ident[:, :], in_=ident[:, :], compare_op=ALU.not_equal, fill=1.0, base=0,
                               pattern=[[-1, P]], channel_multiplier=1).then_inc(const_done, 1)
            step.did(pool.affine_select(out=chmask[:, :], in_=chmask[:, :], compare_op=ALU.is_ge, fill=0.0, base=0,
                                        pattern=[[1, P]], channel_multiplier=-1))
            step.settle()
            pool.memset(chmask[0:HGC, HGC:P], 0.0).then_inc(const_done, 1)
            pool.memset(mhalf, -0.5).then_inc(const_done, 1)
            pool.memset(zeros[:, :], 0.0).then_inc(const_done, 1)
            pool.iota(dist[:, :], pattern=[[-1, SEQ]], base=P, channel_multiplier=1).then_inc(const_done, 1)
            for i in range(HALF):
                pool.memset(freq[:, i:i + 1], float(np.float32(THETA) ** np.float32(-2.0 * i / ROT))) \
                    .then_inc(const_done, 1)

            def rstd(st, count, scale, eps):
                pool.wait_ge(var_done, st["at"]["stat"] + 1)
                step.did(pool.tensor_scalar(vst[:, 0:count], vst[:, 0:count], scale, eps, ALU.mult, ALU.add))
                step.settle()
                pool.tensor_tensor(rs[:, 0:count], vst[:, 0:count], mhalf[:, 0:count], ALU.pow).then_inc(rstd_done, 1)

            for st in stages:
                if st["kind"] == "gains":
                    for s_, v in st["after"]:
                        if v:
                            pool.wait_ge(s_, v)
                    for k, row in enumerate(st["rows"]):
                        pool.dma_start(gb[:, k, :], row.partition_broadcast(P)).then_inc(gb_full, 16)
                elif st["kind"] == "abias":
                    for s_, v in st["after"]:
                        pool.wait_ge(s_, v)
                    pool.dma_start(abias, a_b_qkv[st["j"]].partition_broadcast(P)).then_inc(rows_full, 16)
                    pool.dma_start(abo, a_b_o[st["j"]].partition_broadcast(P)).then_inc(rows_full, 16)
                elif st["kind"] == "load_mem":
                    for s_, v in st["after"]:
                        pool.wait_ge(s_, v)
                    pool.dma_start(r[:, :, :], mem[0].rearrange("(t p) d -> p t d", p=P)).then_inc(rows_full, 16)
                elif st["kind"] == "renorm":
                    for t in range(T):
                        pool.wait_ge(var_done, st["at"]["stat"] + t + 1)
                        v = vst[:, t:t + 1]
                        if st["norm"] == "layer":
                            step.did(pool.tensor_scalar(v, mv[:, t, 1:2], 1.0, LN_EPS, ALU.mult, ALU.add))
                        else:
                            step.did(pool.tensor_scalar(v, v, 1.0 / D, RMS_EPS, ALU.mult, ALU.add))
                        step.settle()
                        pool.tensor_tensor(rs[:, t:t + 1], v, mhalf[:, 0:1], ALU.pow).then_inc(rstd_done, 1)
                elif st["kind"] == "layer_norm":
                    rstd(st, T, 1.0, LN_EPS)
                elif st["kind"] == "rms_norm":
                    rstd(st, T, 1.0 / D, RMS_EPS)
                elif st["kind"] == "headnorm":
                    rstd(st, T * st["nh"], 1.0 / st["hd"], RMS_EPS)

        @block.scalar
        def _(act):
            step = Steps(act, act_step)

            def split_hi(w, late=0):
                if w >= WIDE:
                    return
                _, nkc, ncols = chunks[w]
                act.wait_ge(raw_full[w % 2], full[w])
                if w >= 2:
                    act.wait_ge(lin_done, 2 * (w - 1) + late)
                for h in range(2):
                    ks = slice(h * nkc // 2, (h + 1) * nkc // 2)
                    act.activation(wide(whi, w, nkc, ncols)[:, ks, :], wide(raw, w, nkc, ncols)[:, ks, :], ACT.Copy) \
                       .then_inc(hi_done, 1)

            def rows_hi(st, t):
                for g in range(2):
                    q = st["at"]["tp"] + 2 * t + g
                    act.wait_ge(tp_done, q + 1)
                    act.activation(xt_hi[:, 4 * g:4 * g + 4, t * P:(t + 1) * P],
                                   banks[TB[q % 2]][:, :].rearrange("p (k s) -> p k s", s=P), ACT.Copy).then_inc(thi_done, 1)

            for st in stages:
                at = st["at"]
                if st["kind"] == "setup":
                    act.wait_ge(trig, 1)
                    act.activation(rope_c[:, :, :, :], rope_c[:, :, :, :], ACT.Sin).then_inc(trig, 1)
                    act.activation(rope_s[:, :, :, :], rope_s[:, :, :, :], ACT.Sin).then_inc(trig, 1)
                    step.did(act.activation(lbp[:, 3, :], lbp[:, 2, :], ACT.Abs))
                    step.settle()
                    step.did(act.activation(lbp[:, 4, :], lbp[:, 3, :], ACT.Exp, scale=-1.0))
                    step.settle()
                    act.activation(lbp[:, 5, :], lbp[:, 4, :], ACT.Ln, bias=1.0).then_inc(trig, 1)
                    split_hi(0)
                elif st["kind"] == "ahead":
                    split_hi(st["w"])
                elif st["kind"] == "linear":
                    if st["w"] + 1 not in early:
                        split_hi(st["w"] + 1)
                    if st["second"]:
                        rows_hi(st["second"], 1)
                    if st["evac"] == "act":
                        for s_, v in st["after"]:
                            if v:
                                act.wait_ge(s_, v)
                        for t in range(T):
                            act.wait_ge(lin_done, 2 * st["w"] + t + 1)
                            ps = banks[LB[t]]
                            if st["turned"]:
                                act.activation(st["dst"][:, 2 * t:2 * t + 2, :],
                                               ps[:, :].rearrange("p (h s) -> p h s", s=SEQ), st["func"]).then_inc(aev, 1)
                            elif st["narrow"]:
                                kd, dvv = st["narrow"]
                                step.did(act.activation(kd[:, t, 0:HD], ps[:, 0:HD], ACT.Copy))
                                step.did(act.activation(dvv[:, t, :], ps[:, 64:128], ACT.Copy))
                                step.did(act.activation(kd[:, t, 128:128 + HD], ps[:, 128:192], ACT.Copy))
                                act.activation(iwb[:, t, :], ps[:, 192:200], ACT.Copy, scale=8 ** -0.5).then_inc(aev, 1)
                            else:
                                act.activation(st["dst"][:, t, :], ps[:, 0:st["ncols"]], st["func"]).then_inc(aev, 1)
                elif st["kind"] == "renorm":
                    if st["lhs"]:
                        split_hi(st["w"] + 1)
                        split_hi(st["w"] + 2, late=1)
                    rows_hi(st, 0)
                elif st["kind"] == "split":
                    hi, _ = st["dst"]
                    for g in range(st["nkc"] // 2):
                        act.wait_ge(tp_done, at["tp"] + g + 1)
                        act.activation(hi[:, 2 * g:2 * g + 2, :],
                                       banks[TB[(at["tp"] + g) % 2]][:, :].rearrange("p (k s) -> p k s", s=SEQ),
                                       ACT.Copy).then_inc(thi_done, 1)
                elif st["kind"] == "turn":
                    for t in range(T):
                        act.wait_ge(tp_done, at["tp"] + t + 1)
                        act.activation(st["dst"][:, 0:st["nb"], t * P:t * P + P],
                                       banks[TB[(at["tp"] + t) % 2]][:, 0:st["nb"] * P].rearrange("p (h s) -> p h s", s=P),
                                       ACT.Copy).then_inc(turn_done, 1)
                elif st["kind"] == "attention":
                    U = st["units"]

                    def exps(i):
                        u, k = U[i], at["unit"] + i
                        act.wait_ge(nb_done, k + 1)
                        if u["sink"]:
                            j, h = u["sink"]
                            step.did(act.activation(es[:, k % 4, 0:len(u["rows"])], nb[:, k % 4, 0:len(u["rows"])], ACT.Exp,
                                                    bias=sinks[:, j, h:h + 1]))
                        for row in range(len(u["rows"])):
                            mine = [q for q in u["pieces"] if q[0] == row]
                            q = slice(mine[0][1], mine[-1][1] + mine[-1][2])
                            ins = act.activation(sm[:, k % 2, q], sm[:, k % 2, q], ACT.Exp, bias=nb[:, k % 4, row:row + 1],
                                                 scale=st["scale"], accum_out=ls[:, k % 4, row:row + 1])
                        ins.then_inc(p_done, 1)

                    def evacuate(i):
                        u, k = U[i], at["unit"] + i
                        act.wait_ge(rl_done, k + 1)
                        act.wait_ge(pv_done, k + 1)
                        for row, (_, _, o) in enumerate(u["rows"]):
                            ins = act.activation(o, banks[OB[k % 2]][:, row * u["dv"]:(row + 1) * u["dv"]], ACT.Copy,
                                                 scale=rl[:, k % 4, row:row + 1])
                        ins.then_inc(o_done, 1)

                    for i in range(len(U) + 2):
                        if i < len(U):
                            exps(i)
                        if i >= 2:
                            evacuate(i - 2)
                elif st["kind"] == "ffn":
                    w0, d0 = st["w"], st["d"]

                    def hi_up(j, s, f):
                        act.wait_ge(raw_full[s], f)
                        act.wait_ge(lin_done, 2 * (w0 - 1) + 2 * j)
                        for h in range(2):
                            q = slice(h * 2048, (h + 1) * 2048)
                            act.activation(whi[:, s, q], raw[:, s, q], ACT.Copy).then_inc(hi_done, 1)

                    def hi_down(j):
                        act.wait_ge(draw_full, 16 * (d0 + j + 1))
                        act.wait_ge(down_done, d0 + j)
                        act.activation(dhi[:, :, :], draw[:, :, :], ACT.Copy).then_inc(dhi_done, 1)

                    def silu(j, t):
                        act.wait_ge(lin_done, 2 * w0 + 2 * j + t + 1)
                        act.activation(silu_g[:, t, :], banks[LB[t]][:, 0:FN], ACT.Silu).then_inc(sg_done, 1)

                    def hidden_hi(j, b):
                        act.wait_ge(tp_done, at["tp"] + j + 1)
                        act.activation(yt_hi[:, 2 * b:2 * b + 2, :],
                                       banks[TB[(at["tp"] + b) % 2]][:, :].rearrange("p (k s) -> p k s", s=SEQ),
                                       ACT.Copy).then_inc(thi_done, 1)

                    def slot(j, u, f):
                        hi_up(j + 1, (w0 + u + 1) % 2, f)
                        hi_down(j - 1)
                        silu(j, 0)
                        hidden_hi(j - 1, (u + 1) % 2)
                        silu(j, 1)

                    split_hi(w0 + 1)
                    if st["second"]:
                        rows_hi(st["second"], 1)
                    silu(0, 0)
                    silu(0, 1)
                    slot(1, 1, full[w0 + 2])
                    with act.Fori(0, (FJ - 3) // 2) as i:
                        slot(i * 2 + 2, 0, i * 32 + full[w0 + 3])
                        slot(i * 2 + 3, 1, i * 32 + full[w0 + 4])
                    hi_down(FJ - 2)
                    silu(FJ - 1, 0)
                    hidden_hi(FJ - 2, 1)
                    silu(FJ - 1, 1)
                    hi_down(FJ - 1)
                    split_hi(w0 + FJ)
                    hidden_hi(FJ - 1, 0)
                elif st["kind"] == "select":
                    for e in range(4 * T):
                        t, k = e // 4, at["rel"] + e
                        nk = P * (t + 1)
                        act.wait_ge(s_done, at["seg"] + e + 1)
                        if k >= 2:
                            act.wait_ge(rel_used, k - 1)
                        act.activation(relu2[:, k % 2, :, 0:nk],
                                       banks[SB[(at["seg"] + e) % 2]][:, :].rearrange("p (h s) -> p h s", s=SEQ)[:, :, 0:nk],
                                       ACT.Relu, scale=HD ** -0.5).then_inc(rel_done, 1)
                elif st["kind"] == "decay_sums":
                    k = 1 if st["l"] > 0 else 0
                    ha, hd_, hp = st["counts"]
                    act.wait_ge(aev, st["aev_z"])
                    step.did(act.activation(blk(2), blk(1), ACT.Abs))
                    step.settle()
                    step.did(act.activation(blk(2), blk(2), ACT.Exp, scale=-1.0))
                    step.settle()
                    act.activation(blk(2), blk(2), ACT.Ln, bias=1.0).then_inc(hg_act, 1)
                    if k:
                        act.wait_ge(hg_dve, hd_ + 1)
                        step.did(act.activation(blk(7), blk(7), ACT.Abs))
                        step.settle()
                        step.did(act.activation(blk(7), blk(7), ACT.Exp, scale=-1.0))
                        step.settle()
                        act.activation(blk(7), blk(7), ACT.Ln, bias=1.0).then_inc(hg_act, 1)
                elif st["kind"] == "decays":
                    k = 1 if st["l"] > 0 else 0
                    ha, hd_, hp = st["counts"]
                    act.wait_ge(hg_dve, hd_ + k + 1)
                    step.did(act.activation(blk(4), blk(4), ACT.Exp, scale=-1.0))
                    step.did(act.activation(blk(7), blk(6), ACT.Exp, scale=-1.0))
                    step.settle()
                    step.did(act.activation(blk(6), blk(6), ACT.Exp))
                    step.did(act.activation(blk(2), blk(5), ACT.Exp))
                    step.did(act.activation(hdl[:, :], chunked(5)[:, :, HGC - 1], ACT.Exp))
                    act.activation(blk(8), blk(8), ACT.Exp).then_inc(hg_act, 1)
                elif st["kind"] == "hgrn":
                    ha, hd_, hp = st["counts"]
                    for t in range(T):
                        act.wait_ge(tp_done, at["tp"] + t + 1)
                        act.activation(tiled(4)[:, t, :], banks[TB[(at["tp"] + t) % 2]][:, :], ACT.Copy) \
                           .then_inc(hg_act, 1)
                    for t in range(T):
                        act.wait_ge(hg_pe, hp + T + 3 + t + 1)
                        act.activation(hyc[:, t, :], banks[OB[t]][:, :], ACT.Copy).then_inc(hg_act, 1)

        @block.vector
        def _(dve):
            step = Steps(dve, dve_step)

            def split_lo(w, halves=(0, 1)):
                if w >= WIDE:
                    return
                _, nkc, ncols = chunks[w]
                for h in halves:
                    ks = slice(h * nkc // 2, (h + 1) * nkc // 2)
                    dve.wait_ge(hi_done, 2 * w + h + 1)
                    dve.tensor_tensor(wide(wlo, w, nkc, ncols)[:, ks, :], wide(raw, w, nkc, ncols)[:, ks, :],
                                      wide(whi, w, nkc, ncols)[:, ks, :].bitcast(F32), ALU.subtract).then_inc(lo_done, 1)

            def rows_lo(st, t):
                for g in range(2):
                    q = st["at"]["tp"] + 2 * t + g
                    dst = (slice(None), slice(4 * g, 4 * g + 4), slice(t * P, (t + 1) * P))
                    dve.wait_ge(thi_done, st["at"]["sg"] + 2 * t + g + 1)
                    dve.tensor_tensor(xt_lo[dst], banks[TB[q % 2]][:, :].rearrange("p (k s) -> p k s", s=P),
                                      xt_hi[dst].bitcast(F32), ALU.subtract).then_inc(tlo_done, 1)

            def next_lo(st, w):
                split_lo(w, (0,))
                if st["second"]:
                    rows_lo(st["second"], 1)
                split_lo(w, (1,))

            for st in stages:
                at = st["at"]
                if st["kind"] == "setup":
                    dve.wait_ge(const_done, 5 + HALF)
                    dve.wait_ge(loaded, 16 * N_LOADED)
                    ang, turns_i, turns_f, sub, r_, c_ = (rwork[:, q, :] for q in range(6))
                    for b in range(2):
                        for t in range(T):
                            q = (b * T + t) * HALF
                            step.did(dve.tensor_copy(sub[:, q:q + HALF],
                                                     rope_pos[:, b, t:t + 1].to_broadcast([P, HALF])))
                    step.settle()
                    for q in range(2 * T):
                        step.did(dve.tensor_tensor(ang[:, q * HALF:(q + 1) * HALF], sub[:, q * HALF:(q + 1) * HALF], freq,
                                                   ALU.mult))
                    step.settle()
                    step.did(dve.tensor_scalar(turns_i.bitcast(I32), ang, 1 / TWO_PI, None, ALU.mult))
                    step.settle()
                    step.did(dve.tensor_copy(turns_f, turns_i.bitcast(I32)))
                    step.settle()
                    src = ang
                    for part in PI_PARTS:
                        step.did(dve.scalar_tensor_tensor(out=r_, in0=turns_f, scalar=-part, in1=src, op0=ALU.mult,
                                                          op1=ALU.add))
                        step.settle()
                        src = r_
                    for op, edge, by in ((ALU.is_gt, np.pi, -TWO_PI), (ALU.is_lt, -np.pi, TWO_PI)):
                        step.did(dve.tensor_scalar(sub, r_, float(edge), float(by), op, ALU.mult))
                        step.settle()
                        step.did(dve.tensor_tensor(r_, r_, sub, ALU.add))
                        step.settle()
                    step.did(dve.tensor_scalar(c_, r_, float(np.pi / 2), None, ALU.add))
                    step.settle()
                    step.did(dve.tensor_scalar(sub, c_, float(np.pi), float(-TWO_PI), ALU.is_gt, ALU.mult))
                    step.settle()
                    step.did(dve.tensor_tensor(c_, c_, sub, ALU.add))
                    step.settle()
                    for dst, a in ((rope_s, r_), (rope_c, c_)):
                        step.did(dve.tensor_scalar(dst[:, :, :, :].rearrange("p b t c -> p (b t c)"), a, PI_IN, -PI_IN,
                                                   ALU.min, ALU.max))
                    dve.tensor_tensor(lbp[:, 2, :], lbp[:, 1, :], lbp[:, 0, :], ALU.subtract).then_inc(trig, 1)
                    step.did(dve.tensor_scalar(masks[:, 0, :], dist, 0, NEG, ALU.is_lt, ALU.mult))
                    step.did(dve.tensor_scalar(masks[:, 1, :], dist, A_REACH, NEG, ALU.is_gt, ALU.mult))
                    step.did(dve.tensor_scalar(masks[:, 2, :], dist, B_REACH, NEG, ALU.is_gt, ALU.mult))
                    for g, dil in enumerate(DILATIONS[1:]):
                        step.did(dve.tensor_scalar(dwork, dist, dil - 1, None, ALU.bitwise_and))
                        step.settle()
                        step.did(dve.tensor_scalar(masks[:, 3 + g, :], dwork, 0, NEG, ALU.is_gt, ALU.mult))
                        step.settle()
                    for q in range(1, 5):
                        step.did(dve.tensor_tensor(masks[:, q, :], masks[:, q, :], masks[:, 0, :], ALU.add))
                    step.did(dve.tensor_scalar(sk8[:, :, :], sinks[:, :, :], HD ** 0.5, None, ALU.mult))
                    dve.wait_ge(trig, 4)
                    step.did(dve.scalar_tensor_tensor(out=lbp[:, 6, :], in0=lbp[:, 2, :], scalar=0.0, in1=lbp[:, 5, :],
                                                      op0=ALU.min, op1=ALU.subtract))
                    step.settle()
                    step.did(dve.tensor_tensor(lbp[:, 7, :], lbp[:, 6, :], lbp[:, 2, :], ALU.subtract))
                    split_lo(0)
                    step.settle()
                elif st["kind"] == "ahead":
                    split_lo(st["w"])
                elif st["kind"] == "linear":
                    if st["w"] + 1 not in early:
                        next_lo(st, st["w"] + 1)
                    if st["evac"] == "act":
                        continue
                    if st["evac"] == "bias":
                        dve.wait_ge(rows_full, 16 * st["inn"])
                    if st["evac"] == "lift":
                        dve.wait_ge(aev, st["gate_is"])
                    for t in range(T):
                        dve.wait_ge(lin_done, 2 * st["w"] + t + 1)
                        ps = banks[LB[t]]
                        if st["evac"] == "bias":
                            c0 = st["c"] * NW
                            if st["c"] < 2:
                                dve.tensor_tensor(st["tk"][:, t, :], ps[:, :], abias[:, c0:c0 + NW], ALU.add).then_inc(dev, 1)
                                continue
                            kd = st["tk"][:, t, :].rearrange("p (h e d) -> p h e d", e=2, d=HD)
                            for e in range(2):
                                step.did(dve.tensor_tensor(kd[:, :, e, :],
                                                           ps[:, 0:256].rearrange("p (h d) -> p h d", d=HD),
                                                           abias[:, c0:c0 + 256].rearrange("p (h d) -> p h d", d=HD),
                                                           ALU.add))
                            dve.tensor_tensor(st["v"][:, t, :], ps[:, 256:512], abias[:, c0 + 256:c0 + 512], ALU.add) \
                               .then_inc(dev, 1)
                        else:
                            h0 = st["half"] * NW
                            if st["first"]:
                                dve.tensor_tensor(r[:, t, h0:h0 + NW], st["gate"][:, t, :], ps[:, :], ALU.mult) \
                                   .then_inc(dev, 1)
                            else:
                                step.did(dve.tensor_tensor(st["gate"][:, t, :], st["gate"][:, t, :], ps[:, :], ALU.mult))
                                step.settle()
                                dve.tensor_tensor(r[:, t, h0:h0 + NW], r[:, t, h0:h0 + NW], st["gate"][:, t, :], ALU.add) \
                                   .then_inc(dev, 1)
                elif st["kind"] == "renorm":
                    w, dst = st["w"], st["dst"]

                    def add_residual(t, h):
                        cs = slice(h * NW, (h + 1) * NW)
                        if st["lhs"]:
                            dve.wait_ge(lin_done, 2 * w + 2 * t + h + 1)
                            ps = banks[LB[h]]
                        else:
                            ps = banks[ACC[t][h]]
                        ins = dve.scalar_tensor_tensor(out=dst[:, t, cs], in0=x[:, t, cs], scalar=st["alpha"], in1=ps[:, :],
                                                       op0=ALU.mult, op1=ALU.add)
                        if st["bias"] is not None:
                            step.did(ins)
                            step.settle()
                            ins = dve.tensor_tensor(dst[:, t, cs], dst[:, t, cs], st["bias"][:, cs], ALU.add)
                        ins.then_inc(dev, 1)

                    def statistics(t):
                        dve.wait_ge(dev, at["dev"] + 2 * t + 2)
                        if st["norm"] == "layer":
                            for h in range(2):
                                step.did(dve.bn_stats(bns[:, t, h, :], dst[:, t, h * NW:(h + 1) * NW]))
                            step.settle()
                            dve.bn_aggr(mv[:, t, :], bns[:, t, :, :].rearrange("p h s -> p (h s)")).then_inc(var_done, 1)
                        else:
                            dve.tensor_tensor_reduce(out=smflat[:, 0:D], in0=dst[:, t, :], in1=dst[:, t, :], scale=1.0,
                                                     scalar=0.0, op0=ALU.mult, op1=ALU.add,
                                                     accum_out=vst[:, t:t + 1]).then_inc(var_done, 1)

                    def normalise(t):
                        dve.wait_ge(rstd_done, at["stat"] + t + 1)
                        dve.wait_ge(gb_full, 16 * st["gbv"])
                        if st["norm"] == "layer":
                            step.did(dve.tensor_scalar(x[:, t, :], dst[:, t, :], mv[:, t, 0:1], rs[:, t:t + 1], ALU.subtract,
                                                       ALU.mult))
                            step.settle()
                            step.did(dve.tensor_tensor(x[:, t, :], x[:, t, :], gb[:, 0, :], ALU.mult))
                            step.settle()
                            dve.tensor_tensor(x[:, t, :], x[:, t, :], gb[:, 1, :], ALU.add).then_inc(x_ready, 1)
                        else:
                            dve.scalar_tensor_tensor(out=r[:, t, :], in0=dst[:, t, :], scalar=rs[:, t:t + 1],
                                                     in1=gb[:, 0, :], op0=ALU.mult, op1=ALU.mult).then_inc(x_ready, 1)

                    if st["lhs"]:
                        split_lo(w + 1)
                    else:
                        dve.wait_ge(sum_done, st["at"]["ffn"])
                    add_residual(0, 0)
                    add_residual(0, 1)
                    statistics(0)
                    normalise(0)
                    if not st["lhs"]:
                        dve.wait_ge(down_done, st["at"]["d"])
                    add_residual(1, 0)
                    if st["lhs"]:
                        split_lo(w + 2, (0,))
                    add_residual(1, 1)
                    rows_lo(st, 0)
                    if st["lhs"]:
                        split_lo(w + 2, (1,))
                    statistics(1)
                    normalise(1)
                elif st["kind"] == "split":
                    hi, lo = st["dst"]
                    for g in range(st["nkc"] // 2):
                        dve.wait_ge(thi_done, at["sg"] + g + 1)
                        dve.tensor_tensor(lo[:, 2 * g:2 * g + 2, :],
                                          banks[TB[(at["tp"] + g) % 2]][:, :].rearrange("p (k s) -> p k s", s=SEQ),
                                          hi[:, 2 * g:2 * g + 2, :].bitcast(F32), ALU.subtract).then_inc(tlo_done, 1)
                elif st["kind"] == "rope":
                    dve.wait_ge(*st["after"])
                    if at["rope"]:
                        dve.wait_ge(rope_done, at["rope"])
                    nh = st["nh"]
                    x1, x2 = st["buf"][:, :, :, 0:HALF], st["buf"][:, :, :, HALF:ROT]
                    cs, sn = (f[:, st["table"]].unsqueeze(2).to_broadcast([P, T, nh, HALF]) for f in (rope_c, rope_s))
                    tm = [rtmp[:, q, 0:T * nh * HALF].rearrange("p (t h c) -> p t h c", t=T, h=nh) for q in range(4)]
                    for q, (a, b) in enumerate(((x1, cs), (x2, sn), (x2, cs), (x1, sn))):
                        step.did(dve.tensor_tensor(tm[q], a, b, ALU.mult))
                    step.settle()
                    step.did(dve.tensor_tensor(x1, tm[0], tm[1], ALU.subtract))
                    dve.tensor_tensor(x2, tm[2], tm[3], ALU.add).then_inc(rope_done, 1)
                elif st["kind"] == "dup":
                    dve.wait_ge(rope_done, at["rope"])
                    dve.tensor_copy(st["buf"][:, :, :, HD:2 * HD], st["buf"][:, :, :, 0:HD]).then_inc(rope_done, 1)
                elif st["kind"] == "headnorm":
                    nh, hd = st["nh"], st["hd"]
                    dve.wait_ge(*st["after"])
                    if at["rope"]:
                        dve.wait_ge(rope_done, at["rope"])
                    sq = sqr[:, 0:T * nh * hd].rearrange("p (t h d) -> p t h d", t=T, h=nh)
                    step.did(dve.tensor_tensor(sq, st["buf"], st["buf"], ALU.mult))
                    step.settle()
                    dve.tensor_reduce(vst[:, 0:T * nh].rearrange("p (t h) -> p t h", t=T), sq, AX.X, ALU.add) \
                       .then_inc(var_done, 1)
                    dve.wait_ge(rstd_done, at["stat"] + 1)
                    by = rs[:, 0:T * nh].rearrange("p (t h) -> p t h", t=T).unsqueeze(3).to_broadcast([P, T, nh, hd])
                    step.did(dve.tensor_tensor(st["buf"], st["buf"], by, ALU.mult))
                    step.settle()
                    g = st["gain"].unsqueeze(1).unsqueeze(1).to_broadcast([P, T, nh, hd])
                    if st["gate"] is None:
                        dve.tensor_tensor(st["buf"], st["buf"], g, ALU.mult).then_inc(rope_done, 1)
                    else:
                        step.did(dve.tensor_tensor(st["buf"], st["buf"], g, ALU.mult))
                        step.settle()
                        dve.tensor_tensor(st["buf"], st["buf"], st["gate"], ALU.mult).then_inc(rope_done, 1)
                elif st["kind"] == "layer_norm":
                    dve.wait_ge(dev, at["dev"])
                    for t in range(T):
                        for h in range(2):
                            step.did(dve.bn_stats(bns[:, t, h, :], r[:, t, h * NW:(h + 1) * NW]))
                    step.settle()
                    for t in range(T):
                        step.did(dve.bn_aggr(mv[:, t, :], bns[:, t, :, :].rearrange("p h s -> p (h s)")))
                    step.settle()
                    dve.tensor_copy(vst[:, 0:T], mv[:, :, 1]).then_inc(var_done, 1)
                    dve.wait_ge(rstd_done, at["stat"] + 1)
                    dve.wait_ge(gb_full, 16 * st["gbv"])
                    for t in range(T):
                        step.did(dve.tensor_scalar(x[:, t, :], r[:, t, :], mv[:, t, 0:1], rs[:, t:t + 1], ALU.subtract,
                                                   ALU.mult))
                        step.settle()
                        step.did(dve.tensor_tensor(x[:, t, :], x[:, t, :], gb[:, 0, :], ALU.mult))
                        step.settle()
                        dve.tensor_tensor(x[:, t, :], x[:, t, :], gb[:, 1, :], ALU.add).then_inc(x_ready, 1)
                elif st["kind"] == "rms_norm":
                    dve.wait_ge(dev, at["dev"])
                    if st["after"]:
                        dve.wait_ge(*st["after"])
                    if at["xr"]:
                        dve.wait_ge(x_ready, at["xr"])
                    for t in range(T):
                        ins = dve.tensor_tensor_reduce(out=smflat[:, 0:D], in0=st["src"][:, t, :], in1=st["src"][:, t, :], scale=1.0,
                                                       scalar=0.0, op0=ALU.mult, op1=ALU.add, accum_out=vst[:, t:t + 1])
                        if t < T - 1:
                            step.did(ins)
                            step.settle()
                    ins.then_inc(var_done, 1)
                    dve.wait_ge(rstd_done, at["stat"] + 1)
                    dve.wait_ge(gb_full, 16 * st["gbv"])
                    for t in range(T):
                        dve.scalar_tensor_tensor(out=r[:, t, :], in0=st["src"][:, t, :], scalar=rs[:, t:t + 1],
                                                 in1=gb[:, st["slot"], :], op0=ALU.mult, op1=ALU.mult).then_inc(x_ready, 1)
                elif st["kind"] == "attention":
                    U = st["units"]
                    if at["sel"]:
                        dve.wait_ge(sel_done, at["sel"])

                    def maxima(i):
                        u, k = U[i], at["unit"] + i
                        count = len(u["rows"])
                        for q, (row, off, width, bank, b0, m, products) in enumerate(u["pieces"]):
                            dve.wait_ge(s_done, u["seg0"] + bank + 1)
                            shape = (lambda f: f) if len(m.shape) == 2 else \
                                (lambda f: f.rearrange("p (g c) -> p g c", g=len(products)))
                            dve.tensor_tensor_reduce(out=shape(sm[:, k % 2, off:off + width]),
                                                     in0=shape(banks[QB[(u["seg0"] + bank) % 4]][:, b0:b0 + width]), in1=m,
                                                     scale=1.0, scalar=TAKEN, op0=ALU.add, op1=ALU.max,
                                                     accum_out=mxs[:, k % 4, q:q + 1]).then_inc(ttr_done, 1)
                        dve.wait_ge(ttr_done, u["ttr0"] + len(u["pieces"]))
                        mx, one = mxs[:, k % 4, 0:count], mx1[:, k % 4, 0:count]
                        if len(u["pieces"]) > count:
                            step.did(dve.tensor_reduce(one, mxs[:, k % 4, 0:len(u["pieces"])], AX.X, ALU.max))
                            step.settle()
                            mx = one
                        if u["sink"]:
                            j, h = u["sink"]
                            step.did(dve.tensor_tensor(one, mx, sk8[:, j, h:h + 1].to_broadcast([P, count]), ALU.max))
                            step.settle()
                            mx = one
                        dve.tensor_scalar(nb[:, k % 4, 0:count], mx, -st["scale"], None, ALU.mult).then_inc(nb_done, 1)

                    def copies(i):
                        u, k = U[i], at["unit"] + i
                        if k >= 2:
                            dve.wait_ge(pv_done, k - 1)
                        for q, (c0, c1) in enumerate(u["turns"]):
                            dve.wait_ge(tp_done, u["tp0"] + q + 1)
                            dve.tensor_copy(pts[:, k % 2, c0:c1], banks[TB[(u["tp0"] + q) % 2]][:, 0:c1 - c0]) \
                               .then_inc(pt_done, 1)

                    def reciprocal(i):
                        u, k = U[i], at["unit"] + i
                        count = len(u["rows"])
                        dve.wait_ge(p_done, k + 1)
                        if u["sink"]:
                            step.did(dve.tensor_tensor(ls[:, k % 4, 0:count], ls[:, k % 4, 0:count], es[:, k % 4, 0:count],
                                                       ALU.add))
                            step.settle()
                        dve.reciprocal(rl[:, k % 4, 0:count], ls[:, k % 4, 0:count]).then_inc(rl_done, 1)

                    for i in range(len(U) + 2):
                        if i < len(U):
                            maxima(i)
                        if 1 <= i <= len(U):
                            copies(i - 1)
                            reciprocal(i - 1)
                elif st["kind"] == "ffn":
                    w0, d0 = st["w"], st["d"]

                    def lo_up(j, s):
                        for h in range(2):
                            q = slice(h * 2048, (h + 1) * 2048)
                            dve.wait_ge(hi_done, 2 * w0 + 2 * j + h + 1)
                            dve.tensor_tensor(wlo[:, s, q], raw[:, s, q], whi[:, s, q].bitcast(F32), ALU.subtract) \
                               .then_inc(lo_done, 1)

                    def lo_down(j):
                        dve.wait_ge(dhi_done, d0 + j + 1)
                        dve.tensor_tensor(dlo[:, :, :], draw[:, :, :], dhi[:, :, :].bitcast(F32), ALU.subtract) \
                           .then_inc(dlo_done, 1)

                    def gated(j, t, b):
                        dve.wait_ge(sg_done, at["h"] + 2 * j + t + 1)
                        dve.tensor_tensor(hid[:, b, t, :], silu_g[:, t, :], banks[LB[t]][:, FN:2 * FN], ALU.mult) \
                           .then_inc(h_done, 1)

                    def hidden_lo(j, b):
                        dve.wait_ge(thi_done, at["sg"] + j + 1)
                        dve.tensor_tensor(yt_lo[:, 2 * b:2 * b + 2, :],
                                          banks[TB[(at["tp"] + b) % 2]][:, :].rearrange("p (k s) -> p k s", s=SEQ),
                                          yt_hi[:, 2 * b:2 * b + 2, :].bitcast(F32), ALU.subtract).then_inc(tlo_done, 1)

                    def slot(j, u):
                        lo_up(j + 1, (w0 + u + 1) % 2)
                        lo_down(j - 1)
                        gated(j, 0, u)
                        hidden_lo(j - 1, (u + 1) % 2)
                        gated(j, 1, u)

                    next_lo(st, w0 + 1)
                    gated(0, 0, 0)
                    gated(0, 1, 0)
                    slot(1, 1)
                    with dve.Fori(0, (FJ - 3) // 2) as i:
                        slot(i * 2 + 2, 0)
                        slot(i * 2 + 3, 1)
                    lo_down(FJ - 2)
                    gated(FJ - 1, 0, 0)
                    hidden_lo(FJ - 2, 1)
                    gated(FJ - 1, 1, 0)
                    lo_down(FJ - 1)
                    split_lo(w0 + FJ)
                    hidden_lo(FJ - 1, 0)
                    if not st["evacuate"]:
                        continue
                    dve.wait_ge(down_done, d0 + FJ)
                    for t in range(T):
                        for h in range(2):
                            q = slice(h * NW, (h + 1) * NW)
                            dve.scalar_tensor_tensor(out=st["dst"][:, t, q], in0=x[:, t, q], scalar=st["alpha"],
                                                     in1=banks[ACC[t][h]][:, :], op0=ALU.mult, op1=ALU.add).then_inc(dev, 1)
                elif st["kind"] == "conv":
                    dve.wait_ge(*st["after"])
                    u, y = headed(4), headed(7)
                    step.did(dve.tensor_tensor(blk(4), blk(4), blk(5), ALU.mult))
                    step.settle()
                    for b in range(4):
                        step.did(dve.tensor_scalar(y[:, b, :], u[:, b, :], convw[:, st["l"], 2, b:b + 1], None, ALU.mult))
                    step.settle()
                    for back in (1, 2):
                        for b in range(4):
                            step.did(dve.scalar_tensor_tensor(out=y[:, b, back:SEQ], in0=u[:, b, 0:SEQ - back],
                                                              scalar=convw[:, st["l"], 2 - back, b:b + 1],
                                                              in1=y[:, b, back:SEQ], op0=ALU.mult, op1=ALU.add))
                        step.settle()
                    step.did(dve.tensor_tensor(blk(7), blk(7), blk(6), ALU.mult))
                    step.settle()
                    step.did(dve.tensor_copy(yt_hi[:, :, :], y))
                    step.settle()
                    dve.tensor_tensor(yt_lo[:, :, :], y, yt_hi[:, :, :].bitcast(F32), ALU.subtract).then_inc(conv_done, 1)
                elif st["kind"] == "decay_sums":
                    k = 1 if st["l"] > 0 else 0
                    ha, hd_, hp = st["counts"]
                    by_channel = [lbp[:, q, :].unsqueeze(2).to_broadcast([P, HG, SEQ]) for q in (6, 7)]
                    step.did(dve.memset(sqr, 1.0))
                    step.settle()
                    step.did(dve.memset(sqr.rearrange("p (c s) -> p c s", s=HGC)[:, :, 0:1], 0.0))
                    dve.wait_ge(hg_act, ha + 1)
                    step.did(dve.scalar_tensor_tensor(out=blk(3), in0=blk(1), scalar=0.0, in1=blk(2), op0=ALU.min,
                                                      op1=ALU.subtract))
                    step.did(dve.scalar_tensor_tensor(out=blk(4), in0=blk(1), scalar=0.0, in1=blk(2), op0=ALU.max,
                                                      op1=ALU.add))
                    step.settle()
                    if k:
                        step.did(dve.tensor_tensor(headed(3), headed(3), by_channel[1], ALU.add))
                        step.did(dve.tensor_tensor(headed(4), headed(4), by_channel[1], ALU.subtract))
                        step.settle()
                        dve.tensor_tensor(headed(7), headed(3), by_channel[0], ALU.subtract).then_inc(hg_dve, 1)
                        step.did(dve.tensor_tensor(headed(6), headed(3), by_channel[0], ALU.max))
                        dve.wait_ge(hg_act, ha + 2)
                        step.settle()
                        step.did(dve.tensor_tensor(blk(3), blk(6), blk(7), ALU.add))
                        step.settle()
                    step.did(dve.tensor_tensor_scan(blk(5), sqr, blk(3), 0.0, ALU.mult, ALU.add))
                    step.settle()
                    cum = chunked(5)
                    mid, last = (cum[:, :, q:q + 1].to_broadcast([P, CH, HGC]) for q in (HGC // 2 - 1, HGC - 1))
                    step.did(dve.tensor_tensor(chunked(6), cum, mid, ALU.subtract))
                    dve.tensor_tensor(chunked(8), last, cum, ALU.subtract).then_inc(hg_dve, 1)
                elif st["kind"] == "hgrn":
                    k = 1 if st["l"] > 0 else 0
                    ha, hd_, hp = st["counts"]
                    dve.wait_ge(hg_act, ha + k + 2)
                    dve.wait_ge(aev, st["aev_all"])
                    step.did(dve.tensor_tensor(blk(6), blk(0), blk(6), ALU.mult))
                    step.did(dve.tensor_tensor(blk(7), blk(4), blk(7), ALU.mult))
                    step.did(dve.tensor_tensor(blk(8), blk(4), blk(8), ALU.mult))
                    for q in (1, 3):
                        step.did(dve.memset(blk(q), 0.0))
                    step.settle()
                    for q, dst in enumerate((1, 3)):
                        even = [blk(z).rearrange("p (b c s) -> p b c s", c=2, s=HGC)[:, :, q, :] for z in (dst, 0, 2)]
                        ins = dve.tensor_tensor(even[0], even[1], even[2], ALU.mult)
                        if q == 0:
                            step.did(ins)
                    ins.then_inc(hg_dve, 1)
                    for t in range(T):
                        dve.wait_ge(hg_pe, hp + t + 1)
                        dve.tensor_tensor(tiled(5)[:, t, :].rearrange("p (h s) -> p h s", s=P),
                                          banks[SB[t]][:, :].rearrange("p (h s) -> p h s", s=P),
                                          chmask[:, :].unsqueeze(1).to_broadcast([P, HG, P]), ALU.mult).then_inc(hg_dve, 1)
                    dve.wait_ge(hg_pe, hp + T + 1)
                    dve.tensor_copy(HSTATE[0], banks["O0"][:, :]).then_inc(hg_dve, 1)
                    for c, bank in ((1, "O1"), (2, "S0")):
                        dve.wait_ge(hg_pe, hp + T + 1 + c)
                        dve.wait_ge(hg_dve, hd_ + k + 2 + T + c)
                        for h in range(HG):
                            q = slice(h * P, (h + 1) * P)
                            ins = dve.scalar_tensor_tensor(out=HSTATE[c][:, q], in0=HSTATE[c - 1][:, q],
                                                           scalar=hdl[:, h * NCH + c:h * NCH + c + 1],
                                                           in1=banks[bank][:, q], op0=ALU.mult, op1=ALU.add)
                            if h < HG - 1:
                                step.did(ins)
                        ins.then_inc(hg_dve, 1)
                elif st["kind"] == "select":
                    A, B = blk(7, 512).rearrange("p (b s) -> p b s", b=2), None
                    for t in range(T):
                        nk = P * (t + 1)
                        acc, alt = A[:, 0, 0:nk], A[:, 1, 0:nk]
                        m, _ = causal(0, t)
                        for e in range(4):
                            k = at["rel"] + 4 * t + e
                            dve.wait_ge(rel_done, k + 1)
                            for q in range(2):
                                h = 2 * (2 * (e % 2) + q) + e // 2
                                rel = relu2[:, k % 2, q, 0:nk]
                                w = iwb[:, t, h:h + 1]
                                if e == 0 and q == 0:
                                    ins = dve.tensor_scalar(acc, rel, w, None, ALU.mult)
                                else:
                                    ins = dve.scalar_tensor_tensor(out=acc, in0=rel, scalar=w, in1=acc, op0=ALU.mult,
                                                                   op1=ALU.add)
                                if q == 0:
                                    step.did(ins)
                                    step.settle()
                            ins.then_inc(rel_used, 1)
                            dve.wait_ge(rel_used, k + 1)
                        step.did(dve.tensor_tensor(acc, acc, m, ALU.add))
                        step.settle()
                        for _ in range(TOPK // GRP):
                            step.did(dve.max(m8[:, :], acc))
                            step.settle()
                            step.did(dve.match_replace(alt, m8[:, :], acc, TAKEN))
                            step.settle()
                            acc, alt = alt, acc
                        step.did(dve.tensor_scalar(st["sel"][:, t, 0:nk], acc, TAKEN / 2, NEG, ALU.is_gt, ALU.mult))
                        step.settle()
                        dve.tensor_tensor(st["sel"][:, t, 0:nk], st["sel"][:, t, 0:nk], m, ALU.add).then_inc(sel_done, 1)
                        dve.wait_ge(sel_done, at["sel"] + t + 1)

        @block.tensor
        def _(pe):
            held = {}

            def take(bank):
                if bank in held:
                    pe.wait_ge(*held.pop(bank))

            def turn_rows(st, t):
                pe.wait_ge(x_ready, st["at"]["xr"] + t + 1)
                for g in range(2):
                    q = st["at"]["tp"] + 2 * t + g
                    name = TB[q % 2]
                    take(name)
                    for k in range(4):
                        c0 = (4 * g + k) * P
                        mm = pe.transpose(banks[name][:, k * P:(k + 1) * P], st["rows"][:, t, c0:c0 + P], ident[:, :])
                    mm.then_inc(tp_done, 1)
                    held[name] = (tlo_done, st["at"]["sg"] + 2 * t + g + 1)

            for st in stages:
                at = st["at"]
                if st["kind"] == "setup":
                    pe.wait_ge(const_done, 5 + HALF)
                elif st["kind"] == "renorm":
                    if st["lhs"]:
                        w = st["w"]
                        ready, values, (xh, xl) = st["lhs"]
                        for t in range(T):
                            for h in range(2):
                                take(LB[h])
                                wh, wl = wide(whi, w + h, KC, NW), wide(wlo, w + h, KC, NW)
                                for k in range(KC):
                                    if t == 0 and h == 0 and k % 2 == 0:
                                        pe.wait_ge(ready, values[t][k + 1])
                                    if t == 0 and k in (0, KC // 2):
                                        pe.wait_ge(lo_done, 2 * (w + h) + 1 + (k > 0))
                                    for q, (xx, ww) in enumerate(((xh, wh), (xl, wh), (xh, wl))):
                                        mm = pe.matmul(banks[LB[h]][:, :], xx[:, k, t * P:(t + 1) * P], ww[:, k, :],
                                                       start=(k == 0 and q == 0), stop=(k == KC - 1 and q == 2))
                                mm.then_inc(lin_done, 1)
                                held[LB[h]] = (dev, at["dev"] + 2 * t + h + 1)
                    else:
                        for q in range(2 * T):
                            held[ACC[q // 2][q % 2]] = (dev, at["dev"] + q + 1)
                    turn_rows(st, 0)
                elif st["kind"] == "split":
                    pe.wait_ge(*st["ready"])
                    for g in range(st["nkc"] // 2):
                        name = TB[(at["tp"] + g) % 2]
                        take(name)
                        for k in range(2):
                            for t in range(T):
                                c0, o0 = (2 * g + k) * P, k * SEQ + t * P
                                mm = pe.transpose(banks[name][:, o0:o0 + P], st["src"][:, t, c0:c0 + P], ident[:, :])
                        mm.then_inc(tp_done, 1)
                        held[name] = (tlo_done, at["sg"] + g + 1)
                elif st["kind"] == "turn":
                    pe.wait_ge(*st["ready"])
                    for t in range(T):
                        name = TB[(at["tp"] + t) % 2]
                        take(name)
                        for b in range(st["nb"]):
                            mm = pe.transpose(banks[name][:, b * P:(b + 1) * P], st["src"][:, t, b * P:(b + 1) * P], ident[:, :])
                        mm.then_inc(tp_done, 1)
                        held[name] = (turn_done, at["turn"] + t + 1)
                elif st["kind"] == "linear":
                    w, nkc = st["w"], st["nkc"]
                    ready, values, (xh, xl) = st["lhs"]
                    wh, wl = wide(whi, w, nkc, st["ncols"]), wide(wlo, w, nkc, st["ncols"])
                    frees = (aev, at["aev"]) if st["evac"] == "act" else (dev, at["dev"])

                    def needs(k):
                        if k % 2 == 0:
                            pe.wait_ge(ready, values[0][k + 1])
                        if k in (0, nkc // 2):
                            pe.wait_ge(lo_done, 2 * w + 1 + (k > 0))

                    for t in range(T):
                        ps = banks[LB[t]]
                        take(LB[t])
                        parts = [(0, st["ncols"], None)] if not st["turned"] else [(0, SEQ, 2 * t), (SEQ, 2 * SEQ, 2 * t + 1)]
                        for o0, o1, b in parts:
                            for k in range(nkc):
                                if t == 0 and o0 == 0:
                                    needs(k)
                                elif st["second"] and t == 1 and k % 4 == 0:
                                    pe.wait_ge(ready, values[1][k])
                                for q, (xx, ww) in enumerate(((xh, wh), (xl, wh), (xh, wl))):
                                    if st["turned"]:
                                        a, m = ww[:, k, b * P:(b + 1) * P], xx[:, k, :]
                                    else:
                                        a, m = xx[:, k, t * P:(t + 1) * P], ww[:, k, :]
                                    mm = pe.matmul(ps[:, o0:o1], a, m, start=(k == 0 and q == 0),
                                                   stop=(k == nkc - 1 and q == 2))
                        mm.then_inc(lin_done, 1)
                        held[LB[t]] = (frees[0], frees[1] + t + 1)
                        if st["second"] and t == 0:
                            turn_rows(st["second"], 1)
                elif st["kind"] == "attention":
                    U = st["units"]
                    for s_, v in st["ready"]:
                        pe.wait_ge(s_, v)

                    def scores(i):
                        u, was = U[i], -1
                        for q, (row, off, width, bank, b0, m, products) in enumerate(u["pieces"]):
                            name = QB[(u["seg0"] + bank) % 4]
                            if bank != was:
                                take(name)
                            for qq, kk, nk in products:
                                mm = pe.matmul(banks[name][:, b0:b0 + nk], qq, kk, start=True, stop=True)
                                b0 += nk
                            was = bank
                            if q + 1 == len(u["pieces"]) or u["pieces"][q + 1][3] != bank:
                                mm.then_inc(s_done, 1)
                                held[name] = (ttr_done, u["ttr0"] + q + 1)

                    def turned(i):
                        u, k = U[i], at["unit"] + i
                        pe.wait_ge(p_done, k + 1)
                        for q, (c0, c1) in enumerate(u["turns"]):
                            name = TB[(u["tp0"] + q) % 2]
                            take(name)
                            for c in range(c0, c1, P):
                                mm = pe.transpose(banks[name][:, c - c0:c - c0 + P], sm[:, k % 2, c:c + P], ident[:, :])
                            mm.then_inc(tp_done, 1)
                            held[name] = (pt_done, u["pt0"] + q + 1)

                    def values_(i):
                        u, k = U[i], at["unit"] + i
                        name = OB[k % 2]
                        take(name)
                        pe.wait_ge(pt_done, u["pt0"] + len(u["turns"]))
                        c = 0
                        for row, (_, vs, _) in enumerate(u["rows"]):
                            for q, v in enumerate(vs):
                                mm = pe.matmul(banks[name][:, row * u["dv"]:(row + 1) * u["dv"]],
                                               pts[:, k % 2, c * P:(c + 1) * P], v, start=(q == 0), stop=(q == len(vs) - 1))
                                c += 1
                        mm.then_inc(pv_done, 1)
                        held[name] = (o_done, k + 1)

                    for i in range(len(U) + 2):
                        if i < len(U):
                            scores(i)
                        if 1 <= i <= len(U):
                            turned(i - 1)
                        if i >= 2:
                            values_(i - 2)
                elif st["kind"] == "ffn":
                    w0, d0, sg0, tp0, h0 = st["w"], st["d"], at["sg"], at["tp"], at["h"]
                    ready, values, (xh, xl) = st["lhs"]
                    for name in list(held):
                        take(name)

                    def up(j, s, first=False):
                        wh, wl = (f[:, s, :].rearrange("p (k n) -> p k n", n=NW) for f in (whi, wlo))
                        for t in range(T):
                            if not first:
                                pe.wait_ge(h_done, h0 + 2 * j + t - 1)
                            for k in range(KC):
                                if first and k % 2 == 0 and (t == 0 or st["second"]):
                                    pe.wait_ge(ready, values[t][k + 1])
                                if t == 0 and k in (0, KC // 2):
                                    pe.wait_ge(lo_done, 2 * w0 + 2 * j + 1 + (k > 0))
                                for q, (xx, ww) in enumerate(((xh, wh), (xl, wh), (xh, wl))):
                                    mm = pe.matmul(banks[LB[t]][:, :], xx[:, k, t * P:(t + 1) * P], ww[:, k, :],
                                                   start=(k == 0 and q == 0), stop=(k == KC - 1 and q == 2))
                            mm.then_inc(lin_done, 1)
                            if t == 0 and first and st["second"]:
                                turn_rows(st["second"], 1)
                            if t == 0 and not first:
                                turned_hidden(j - 1, (s + w0 + 1) % 2)

                    def turned_hidden(j, b):
                        name = TB[(tp0 + b) % 2]
                        pe.wait_ge(h_done, h0 + 2 * j + 2)
                        pe.wait_ge(tlo_done, sg0 + j - 1)
                        for k in range(2):
                            for t in range(T):
                                o0 = k * SEQ + t * P
                                mm = pe.transpose(banks[name][:, o0:o0 + P], hid[:, b, t, k * P:(k + 1) * P], ident[:, :])
                        mm.then_inc(tp_done, 1)

                    def down(j, b, first=False, last=False):
                        pe.wait_ge(dlo_done, d0 + j + 1)
                        pe.wait_ge(tlo_done, sg0 + j + 1)
                        for t in range(T):
                            for k in range(2):
                                for h in range(2):
                                    for q, (yy, ww) in enumerate(((yt_hi, dhi), (yt_lo, dhi), (yt_hi, dlo))):
                                        mm = pe.matmul(banks[ACC[t][h]][:, :], yy[:, 2 * b + k, t * P:(t + 1) * P],
                                                       ww[:, k, h * NW:(h + 1) * NW],
                                                       start=(first and k == 0 and q == 0),
                                                       stop=(last and k == 1 and q == 2))
                            if last and t == 0:
                                mm.then_inc(sum_done, 1)
                        mm.then_inc(down_done, 1)

                    up(0, w0 % 2, first=True)
                    up(1, (w0 + 1) % 2)
                    down(0, 0, first=True)
                    with pe.Fori(0, (FJ - 3) // 2) as i:
                        up(i * 2 + 2, w0 % 2)
                        down(i * 2 + 1, 1)
                        up(i * 2 + 3, (w0 + 1) % 2)
                        down(i * 2 + 2, 0)
                    up(FJ - 1, w0 % 2)
                    down(FJ - 2, 1)
                    turned_hidden(FJ - 1, 0)
                    down(FJ - 1, 0, last=True)
                    if st["evacuate"]:
                        for q in range(4):
                            held[ACC[q // 2][q % 2]] = (dev, at["dev"] + q + 1)
                elif st["kind"] == "select":
                    pe.wait_ge(*st["ready"])
                    for e in range(4 * T):
                        t, half, pair = e // 4, (e % 4) // 2, e % 2
                        nk = P * (t + 1)
                        name = SB[(at["seg"] + e) % 2]
                        take(name)
                        q = slice(half * HD, (half + 1) * HD)
                        for b in range(2):
                            mm = pe.matmul(banks[name][:, b * SEQ:b * SEQ + nk], st["iqT"][q, 2 * pair + b, t * P:(t + 1) * P],
                                           st["kkT"][q, 1, 0:nk], start=True, stop=True)
                        mm.then_inc(s_done, 1)
                        held[name] = (rel_done, at["rel"] + e + 1)
                elif st["kind"] == "hgrn":
                    k = 1 if st["l"] > 0 else 0
                    ha, hd_, hp = st["counts"]
                    pe.wait_ge(hg_dve, hd_ + k + 2)
                    for t in range(T):
                        take(SB[t])
                        for h in range(HG):
                            q = slice(t * P, (t + 1) * P)
                            mm = pe.matmul(banks[SB[t]][:, h * P:(h + 1) * P], headed(7)[:, h, q], headed(6)[:, h, q],
                                           start=True, stop=True)
                        mm.then_inc(hg_pe, 1)
                        held[SB[t]] = (hg_dve, hd_ + k + 3 + t)
                    for t in range(T):
                        name = TB[(at["tp"] + t) % 2]
                        take(name)
                        for h in range(HG):
                            mm = pe.transpose(banks[name][:, h * P:(h + 1) * P], headed(8)[:, h, t * P:(t + 1) * P],
                                              ident[:, :])
                        mm.then_inc(tp_done, 1)
                        held[name] = (hg_act, ha + k + 3 + t)
                    pe.wait_ge(hg_act, ha + k + 2 + T)
                    pe.wait_ge(aev, st["aev_all"])
                    for c, name in enumerate(("O0", "O1", "S0")):
                        take(name)
                        rows = slice((c % 2) * HGC, (c % 2 + 1) * HGC)
                        for h in range(HG):
                            q = slice(h * P, (h + 1) * P)
                            mm = pe.matmul(banks[name][:, q], tiled(4)[rows, c // 2, q], st["hv"][rows, c // 2, q], start=True,
                                           stop=True)
                        mm.then_inc(hg_pe, 1)
                        held[name] = (hg_dve, hd_ + k + 2 + T + c + 1)
                    pe.wait_ge(hg_dve, hd_ + k + 2 + T + 3)
                    for t in range(T):
                        name = OB[t]
                        take(name)
                        for h in range(HG):
                            q = slice(h * P, (h + 1) * P)
                            pe.matmul(banks[name][:, q], tiled(5)[:, t, q], st["hv"][:, t, q], start=True, stop=False)
                            if t:
                                pe.matmul(banks[name][:, q], headed(1)[:, h, t * P:(t + 1) * P], HSTATE[2 * t - 1][:, q],
                                          start=False, stop=False)
                            mm = pe.matmul(banks[name][:, q], headed(3)[:, h, t * P:(t + 1) * P], HSTATE[2 * t][:, q],
                                           start=False, stop=True)
                        mm.then_inc(hg_pe, 1)
                        held[name] = (hg_act, ha + k + 2 + T + t + 1)


_INS = ["x", "positions", "ln_g", "ln_b", "a_w_qkv", "a_b_qkv", "a_sinks", "a_w_o", "a_b_o", "b_w_qkv", "b_w_o", "c_w_qkv",
        "c_w_o", "w_gate_up", "w_down", "mem_2", "positions_2", "norm_mix_2", "w_in_2", "conv_w_2", "dsa_q_norm_2",
        "dsa_k_norm_2", "hgrn_lower_bounds_2", "hgrn_out_norm_2", "mem_norm_2", "mem_w_kv_2", "mem_q_norm_2",
        "mem_k_norm_2", "w_lift_2", "w_out_2", "norm_ffn_2", "ffn_w_up_2", "ffn_w_down_2"]
_OUT = ((1, SEQ, D), "float32")


def kernel(**inputs):
    import concourse.bacc as _bacc
    from concourse.bass_utils import run_bass_kernel_spmd as _run

    nc = _bacc.Bacc("TRN2", target_bir_lowering=False, num_devices=1)
    arrays, args = {}, []
    for name in _INS:
        a = np.ascontiguousarray(inputs[name])
        arrays[f"in_{name}"] = a
        args.append(nc.dram_tensor(f"in_{name}", a.shape, mybir.dt.from_np(a.dtype), kind="ExternalInput").ap())
    args.append(nc.dram_tensor("out_0", _OUT[0], mybir.dt.from_np(np.dtype(_OUT[1])), kind="ExternalOutput").ap())
    build(nc, *args)
    return _run(nc, [arrays], core_ids=[0]).results[0]["out_0"]
```

```python
from contextlib import ExitStack

import concourse.bass as bass
from concourse import mybir
import numpy as np

F32 = mybir.dt.float32
F32R = mybir.dt.float32r
I32 = mybir.dt.int32
ALU = mybir.AluOpType
ACT = mybir.ActivationFunctionType
AX = mybir.AxisListType

P = 128
SEQ, D = 256, 1024
T = SEQ // P
KC = D // P
NW = 512
FF = 2816
FN = NW // 2
FJ = FF // FN
HD, ROT = 64, 16
HALF = ROT // 2
THETA = 500000.0
DEPTH, DEPTH2 = 4, 2
ALPHA = (2 * DEPTH) ** 0.25
NEG = -1e30
TAKEN = -3e38
LN_EPS, RMS_EPS = 1e-5, 1e-6
DILATIONS = (1, 4, 16)
A_REACH, B_REACH = 127, 128
TOPK = min(256, SEQ // 4)
GRP = 8
HG, HGD, HGC = 4, 128, 64
NCH = SEQ // HGC
TWO_PI = 2 * np.pi

SPLITS = (512, 512, 512, 512, 64, 64, 512, 64, 8, 512, 512, 512, 512, 512, 4096)
COL = [int(v) for v in np.cumsum((0,) + SPLITS)]
(C_AX, C_AB, C_AC, C_DQ, C_DK, C_DV, C_IQ, C_IK, C_IW, C_GQ, C_GF, C_GI, C_GG, C_MQ, C_GATE) = COL[:-1]
PI_PARTS = (6.28125, float(np.float32(TWO_PI - 6.28125)), float(TWO_PI - 6.28125 - float(np.float32(TWO_PI - 6.28125))))
PI_IN = 3.1415925
N_FIRST, N_LATE = 3, DEPTH2 * 9
SMALL = 64 + 64 + 64 + 8


class Steps:

    def __init__(self, eng, sem):
        self.eng, self.sem, self.n = eng, sem, 0

    def did(self, ins):
        ins.then_inc(self.sem, 1)
        self.n += 1

    def settle(self, but=0):
        self.eng.wait_ge(self.sem, self.n - but)


def build(nc, x_in, positions, ln_g, ln_b, a_w_qkv, a_b_qkv, a_sinks, a_w_o, a_b_o, b_w_qkv, b_w_o, c_w_qkv, c_w_o,
          w_gate_up, w_down, mem, positions_2, norm_mix, w_in, conv_w, dsa_q_norm, dsa_k_norm, hg_lower, hg_out_norm,
          mem_norm, mem_w_kv, mem_q_norm, mem_k_norm, w_lift, w_out, norm_ffn, ffn_up, ffn_down, out):
    ctx = ExitStack()
    with ctx:
        def sb(name, shape, dt=F32):
            return ctx.enter_context(nc.sbuf_tensor(name, shape, dt))

        def sem(name):
            return ctx.enter_context(nc.semaphore(name))

        raw = sb("raw", [P, 2, KC * NW])
        whi = sb("whi", [P, 2, KC * NW], F32R)
        wlo = sb("wlo", [P, 2, KC * NW], F32R)
        xt_hi = sb("xt_hi", [P, KC, SEQ], F32R)
        xt_lo = sb("xt_lo", [P, KC, SEQ], F32R)
        yt_hi = sb("yt_hi", [P, 4, SEQ], F32R)
        yt_lo_at = -(-nc.sbuf_base // 32) * 32
        yt_lo = sb("yt_lo", [P, 4, SEQ], F32R)
        x = sb("x", [P, T, D])
        r = sb("r", [P, T, D])
        tok = sb("tok", [P, 2, T, NW])
        sm = sb("sm", [P, 3, 768])
        pts = sb("pts", [P, 2, 768])
        masks = sb("masks", [P, 5, SEQ])
        zeros = sb("zeros", [P, SEQ])
        ident = sb("ident", [P, P])
        chmask = sb("chmask", [P, P])
        rope_c = sb("rope_c", [P, 2, T, HALF])
        rope_s = sb("rope_s", [P, 2, T, HALF])
        gains = sb("gains", [P, DEPTH2, 512])
        sinks = sb("sinks", [P, 2, 16])
        convw = sb("convw", [P, DEPTH2, 3, 4])
        lbp = sb("lbp", [P, 8, HG])
        small = sb("small", [P, 112])
        vst, rs, mhalf = small[:, 0:16], small[:, 16:32], small[:, 32:48]
        mv = small[:, 48:52].rearrange("p (t s) -> p t s", s=2)
        mxs = small[:, 56:72].rearrange("p (u s) -> p u s", s=4)
        mx1, nb, ls, rl, es = (small[:, q:q + 8].rearrange("p (u s) -> p u s", s=2) for q in range(72, 112, 8))
        bns = sb("bns", [P, T, 2, 6])
        iwb = sb("iwb", [P, T, 8])
        sk8 = sb("sk8", [P, 2, 16])
        hdl = sb("hdl", [P, NCH * HG])
        m8 = sb("m8", [P, T, GRP])
        AREA = 9 * 1024
        dn_off = -(-nc.sbuf_base // 32) * 32
        arena = sb("arena", [P, AREA])
        draw = nc.alloc_sbuf_tensor_at("draw", [P, 2, D], F32, offset=dn_off)
        dhi = nc.alloc_sbuf_tensor_at("dhi", [P, 2, D], F32R, offset=dn_off + 8 * D)
        dlo = nc.alloc_sbuf_tensor_at("dlo", [P, 2, D], F32R, offset=dn_off + 16 * D)
        hg_values = nc.alloc_sbuf_tensor_at("hg_values", [P, T, NW], F32, offset=yt_lo_at)
        gb = arena[:, 7 * 1024:9 * 1024].rearrange("p (a n) -> p a n", a=2)
        abias = arena[:, 3584:3584 + 1536]
        abo = arena[:, 5120:6144]

        def blk(i, n=1024):
            return arena[:, i * 1024:i * 1024 + n]

        pflat = pts[:, :, :].rearrange("p a b -> p (a b)")
        sqr, rtmp = pflat[:, 0:1024], pflat[:, 1024:1536].rearrange("p (k c) -> p k c", k=4)
        smflat = sm[:, :, :].rearrange("p a b -> p (a b)")
        mem_gain, mix_gain = smflat[:, 0:D], pflat[:, 0:D]
        hyc = smflat[:, 0:1024].rearrange("p (t c) -> p t c", t=T)
        hid = tok[:, 0].rearrange("p t c -> p (t c)").rearrange("p (b t f) -> p b t f", b=2, t=T)
        silu_g = tok[:, 1].rearrange("p t c -> p (t c)")[:, 0:T * FN].rearrange("p (t f) -> p t f", t=T)
        relu2 = blk(6).rearrange("p (b h s) -> p b h s", b=2, h=2)
        dist = blk(0, SEQ).bitcast(I32)
        dwork = blk(1, SEQ).bitcast(I32)
        rope_pos = blk(2, 2 * T).bitcast(I32).rearrange("p (b t) -> p b t", b=2)
        freq = blk(2)[:, 16:16 + HALF]
        rwork = blk(3, 6 * 2 * T * HALF).rearrange("p (k c) -> p k c", k=6)
        CH = NCH * HG
        HSTATE = [blk(0)[:, 0:512], blk(0)[:, 512:1024], blk(2)[:, 0:512]]

        def chunked(i):
            return blk(i).rearrange("p (c s) -> p c s", s=HGC)

        def headed(i):
            return blk(i).rearrange("p (h s) -> p h s", s=SEQ)

        def tiled(i):
            return blk(i).rearrange("p (t c) -> p t c", t=T)

        banks = {n: ctx.enter_context(nc.psum_tensor(f"bank_{n}", [P, 512], F32))
                 for n in ("L0", "L1", "S0", "S1", "T0", "T1", "O0", "O1")}
        LB, SB, TB, OB = (["L0", "L1"], ["S0", "S1"], ["T0", "T1"], ["O0", "O1"])
        QB = SB + LB
        ACC = [["S0", "S1"], ["O0", "O1"]]

        raw_full = [sem("raw_full0"), sem("raw_full1")]
        hi_done, lo_done = sem("hi_done"), sem("lo_done")
        lin_done = sem("lin_done")
        aev, dev = sem("act_evacuated"), sem("dve_evacuated")
        draw_full = sem("draw_full")
        dhi_done, dlo_done = sem("dhi_done"), sem("dlo_done")
        down_done = sem("down_done")
        sum_done = sem("sum_done")
        silu_done, h_done = sem("silu_done"), sem("hidden_done")
        tp_done = sem("transposed")
        thi_done, tlo_done = sem("thi_done"), sem("tlo_done")
        turn_done = sem("turn_done")
        rope_done = sem("rope_done")
        s_done = sem("s_done")
        ttr_done, nb_done = sem("ttr_done"), sem("nb_done")
        p_done = sem("p_done")
        pt_done, rl_done = sem("pt_done"), sem("rl_done")
        pv_done, o_done = sem("pv_done"), sem("o_done")
        var_done, rstd_done = sem("var_done"), sem("rstd_done")
        x_ready = sem("x_ready")
        in_full, out_full = sem("in_full"), sem("out_full")
        loaded, late_loaded = sem("loaded"), sem("late_loaded")
        gb_full, rows_full = sem("gb_full"), sem("rows_full")
        const_done = sem("const_done")
        trig = sem("trig")
        rel_done, rel_used = sem("rel_done"), sem("rel_used")
        sel_done = sem("sel_done")
        conv_done = sem("conv_done")
        hg_act, hg_dve, hg_pe = sem("hg_act"), sem("hg_dve"), sem("hg_pe")
        dve_step, act_step, pool_step = sem("dve_step"), sem("act_step"), sem("pool_step")

        stages = []
        chunks = []
        n = dict(w=0, d=0, aev=0, dev=0, tp=0, sg=0, turn=0, rope=0, seg=0, unit=0, stat=0, ffn=0, gb=0,
                 xr=0, h=0, ttr=0, p=0, pt=0, rel=0, conv=0, hga=0, hgd=0, hgp=0, sel=0, inn=0)

        def add(kind, **kw):
            st = dict(kind=kind, at=dict(n), deferred=False, **kw)
            stages.append(st)
            return st

        def load_gains(rows, after):
            add("gains", rows=rows, after=after)
            n["gb"] += len(rows)

        def split(src, ready, dst, nkc=KC):
            st = add("split", src=src, ready=ready, dst=dst, nkc=nkc)
            n["tp"] += nkc // 2
            n["sg"] += nkc // 2
            return (tlo_done, [[st["at"]["sg"] + k // 2 + 1 for k in range(nkc)]] * T, dst)

        second = [None]

        def take_second():
            st, second[0] = second[0], None
            return st

        def renorm(norm, dst, alpha, lhs=None, weights=None, bias=None):
            st = add("renorm", norm=norm, dst=dst, alpha=alpha, lhs=lhs, bias=bias, w=n["w"], gbv=n["gb"],
                     rows=x if norm == "layer" else r)
            if lhs:
                for half in range(2):
                    chunks.append(([(0, cols(weights, half * NW, (half + 1) * NW))], KC, NW))
                n["w"] += 2
            n["dev"] += 2 * T
            n["stat"] += T
            n["xr"] += T
            n["tp"] += 2 * T
            n["sg"] += 2 * T
            second[0] = st
            return (tlo_done, [[st["at"]["sg"] + 2 * t + k // 4 + 1 for k in range(KC)] for t in range(T)], (xt_hi, xt_lo))

        def linear(lhs, loads, ncols, evac, nkc=KC, turned=False, func=ACT.Copy, narrow=None, after=(),
                   into=LB, **kw):
            st = add("linear", lhs=lhs, second=take_second(), ncols=ncols, nkc=nkc, turned=turned, evac=evac, w=n["w"],
                     func=func, narrow=narrow, after=after, into=into, **kw)
            chunks.append((loads, nkc, ncols))
            n["w"] += 1
            if evac in ("act",):
                n["aev"] += 2
            else:
                n["dev"] += 2
            return st

        def cols(w, c0, c1):
            return w[:, c0:c1].rearrange("(k p) n -> p k n", p=P)

        def turn(src, ready, dst, nb_=4):
            st = add("turn", src=src, ready=ready, dst=dst, nb=nb_)
            n["tp"] += T
            n["turn"] += T
            return st

        def rope(buf, nh, table, after):
            add("rope", buf=buf, nh=nh, table=table, after=after)
            n["rope"] += 1
            return (rope_done, n["rope"])

        def headnorm(buf, nh, hd, gain, after, gate=None):
            add("headnorm", buf=buf, nh=nh, hd=hd, gain=gain, after=after, gate=gate)
            n["stat"] += 1
            n["rope"] += 1
            return (rope_done, n["rope"])

        def attention(units, scale, ready, first, behind, lead=2):
            add("attention", units=units, scale=scale, ready=ready, first=first, behind=behind, lead=lead)
            for st in behind:
                st["deferred"] = True
            bank0 = 0
            for u in units:
                u["bank0"] = bank0
                u["seg0"], u["ttr0"], u["p0"], u["tp0"], u["pt0"] = n["seg"], n["ttr"], n["p"], n["tp"], n["pt"]
                u["pieces"], off, bank, used = [], 0, 0, 0
                for row, (pieces, _, _) in enumerate(u["rows"]):
                    for mask, products in pieces:
                        width = sum(c for _, _, c in products)
                        if used + width > NW:
                            bank, used = bank + 1, 0
                        u["pieces"].append((row, off, width, bank, used, mask, products))
                        off, used = off + width, used + width
                u["cols"], u["banks"] = off, bank + 1
                per_bank = 3 * P if off > NW else NW
                u["turns"] = [(c, min(c + per_bank, off)) for c in range(0, off, per_bank)]
                bank0 += u["banks"]
                n["seg"] += u["banks"]
                n["ttr"] += len(u["pieces"])
                n["p"] += 1
                n["tp"] += len(u["turns"])
                n["pt"] += len(u["turns"])
            n["unit"] += len(units)
            return (o_done, n["unit"])

        def ffn(lhs, w_up, w_dn, alpha, evacuate=False, mem=None):
            add("ffn", lhs=lhs, second=second[0], w=n["w"], d=n["d"], wu=w_up, wd=w_dn, alpha=alpha,
                evacuate=evacuate, index=n["ffn"], mem=mem)
            second[0] = None
            n["ffn"] += 1
            for j in range(FJ):
                chunks.append((("ffn", w_up, j), KC, NW))
            n["w"] += FJ
            n["d"] += FJ
            n["dev"] += 4 if evacuate else 0
            n["h"] += 2 * FJ
            n["tp"] += FJ
            n["sg"] += FJ
            return (dev, n["dev"])

        def layer_norm():
            add("layer_norm", gbv=n["gb"])
            n["stat"] += 1
            n["xr"] += T
            return (x_ready, n["xr"])

        def mem_rows(l, after):
            add("load_mem", l=l, after=after)
            n["inn"] += 3
            st = add("mem_norm", inn=n["inn"])
            n["stat"] += 1
            n["xr"] += T
            return st

        def rms_norm():
            add("rms_norm")
            n["stat"] += 1
            n["xr"] += T
            return (x_ready, n["xr"])

        tok_i = [0]

        def next_tok():
            tok_i[0] += 1
            return tok[:, tok_i[0] % 2]

        def causal(i, t):
            return (masks[:, i, P:SEQ], P) if t == 0 else (masks[:, i, :], SEQ)

        def head_ap(buf, h, c0, c1):
            return buf[HD * (h % 2):HD * (h % 2) + HD, h // 2, c0:c1]

        add("setup")
        x_is = (in_full, 16)
        lhs = split(x, x_is, (xt_hi, xt_lo))
        for i in range(DEPTH):
            kind, j = i % 3, i // 3
            if kind == 0:
                qT = blk(0, 2048).rearrange("p (h s) -> p h s", s=SEQ)
                kT = blk(2, 1024).rearrange("p (h s) -> p h s", s=SEQ)
                vv = blk(3, 512).rearrange("p (t c) -> p t c", t=T)
                add("abias", j=j, after=[x_is])
                if i == 0:
                    add("late_loads")
                n["inn"] += 2
                pend = []
                for c in (2, 0, 1):
                    tk = next_tok()
                    if c == 1:
                        add("exp_table")
                    st = linear(lhs, [(0, cols(a_w_qkv[j], c * NW, (c + 1) * NW))], NW, "bias", tk=tk, c=c, v=vv,
                                inn=n["inn"])
                    done = (dev, n["dev"])
                    hs = tk.rearrange("p t (h d) -> p t h d", d=HD)
                    if i == 0 and c == 2:
                        add("masks")
                    ok = rope(hs, 8, 0, done)
                    for f in pend:
                        turn(*f)
                    pend = [(tk, ok, qT[:, 4 * c:4 * c + 4] if c < 2 else kT)]
                first = (turn_done, n["turn"])
                behind = [turn(*f) for f in pend]
                units = []
                for h in range(16):
                    kv, rows = h // 4, []
                    for t in range(T):
                        m, nk = causal(1, t)
                        rows.append(([(m, [(head_ap(qT, h, t * P, t * P + P),
                                            kT[HD * (h % 2):HD * (h % 2) + HD, kv, 0:nk], nk)])],
                                     [vv[:, s, kv * HD:kv * HD + HD] for s in range(nk // P)],
                                     r[:, t, h * HD:h * HD + HD]))
                    units.append(dict(rows=rows, dv=HD, sink=(j, h)))
                o_is = attention(units, HD ** -0.5, [(turn_done, n["turn"]), (dev, n["dev"])], first, behind)
                wo, bias = a_w_o[j], True
            elif kind == 1:
                qT = [blk(g).rearrange("p (h s) -> p h s", s=SEQ) for g in range(3)]
                kT = [blk(3 + g).rearrange("p (h s) -> p h s", s=SEQ) for g in range(3)]
                vv = [blk(6 + g).rearrange("p (t c) -> p t c", t=T) for g in range(3)]
                for half in range(2):
                    pend = []
                    for which, g in [(w, g) for g in range(3) for w in range(2)] + [(2, g) for g in range(3)]:
                        c0 = (g * 3 + which) * D + half * NW
                        dst = vv[g] if which == 2 else next_tok()
                        after = [(o_done, n["unit"])] if which == 2 and n["unit"] else []
                        if (which, g) == (2, 2):
                            add("exp_table")
                        st = linear(lhs, [(0, cols(b_w_qkv[j], c0, c0 + NW))], NW, "act", dst=dst, after=after)
                        done = (aev, n["aev"])
                        if which < 2:
                            ok = rope(dst.rearrange("p t (h d) -> p t h d", d=HD), 8, 0, done)
                        for f in pend:
                            turn(*f)
                        pend = [(dst, ok, (qT, kT)[which][g])] if which < 2 else []
                    units = []
                    for h in range(8):
                        hh = half * 8 + h
                        for t in range(T):
                            k0, nk = (P, P) if t == 0 else (0, SEQ)
                            prod = [(head_ap(qT[g], h, t * P, t * P + P), head_ap(kT[g], h, 0, nk), nk) for g in range(3)]
                            pieces = [(masks[:, 2:5, P:SEQ], prod)] if t == 0 else \
                                [(masks[:, 2:4, :], prod[0:2]), (masks[:, 4, :], prod[2:3])]
                            rows = [(pieces, [vv[g][:, s, h * HD:h * HD + HD] for g in range(3) for s in range(nk // P)],
                                     r[:, t, hh * HD:hh * HD + HD])]
                            units.append(dict(rows=rows, dv=HD, sink=None))
                    o_is = attention(units, HD ** -0.5, [(aev, n["aev"])], (turn_done, n["turn"]), [st], lead=1)
                wo, bias = b_w_o[j], False
            else:
                qT = blk(0, 2048).rearrange("p (h s) -> p h s", s=SEQ)
                kT = blk(2, 2048).rearrange("p (h s) -> p h s", s=SEQ)
                vv = blk(4, 2048).rearrange("p (t c) -> p t c", t=T)
                pend = []
                for c in range(6):
                    which, half = c // 2, c % 2
                    dst = vv[:, :, half * NW:(half + 1) * NW] if which == 2 else next_tok()
                    if c == 5:
                        add("exp_table")
                    st = linear(lhs, [(0, cols(c_w_qkv[j], c * NW, (c + 1) * NW))], NW, "act", dst=dst, after=[])
                    done = (aev, n["aev"])
                    if which < 2:
                        ok = rope(dst.rearrange("p t (h d) -> p t h d", d=HD), 8, 0, done)
                    for f in pend:
                        turn(*f)
                    pend = [(dst, ok, (qT, kT)[which][:, 4 * half:4 * half + 4])] if which < 2 else []
                units = []
                for h in range(16):
                    rows = []
                    for t in range(T):
                        m, nk = causal(0, t)
                        rows.append(([(m, [(head_ap(qT, h, t * P, t * P + P), head_ap(kT, h, 0, nk), nk)])],
                                     [vv[:, s, h * HD:h * HD + HD] for s in range(nk // P)],
                                     r[:, t, h * HD:h * HD + HD]))
                    units.append(dict(rows=rows, dv=HD, sink=None))
                o_is = attention(units, HD ** -0.5, [(aev, n["aev"])], (turn_done, n["turn"]), [st])
                wo, bias = c_w_o[j], False
            load_gains([ln_g[i, 0], ln_b[i, 0]], [o_is, (x_ready, n["xr"])])
            lhs = split(r, o_is, (xt_hi, xt_lo))
            if i == 1:
                add("bound_logs")
            lhs = renorm("layer", r, ALPHA, lhs, wo, abo if bias else None)
            x_is = (x_ready, n["xr"])
            load_gains([ln_g[i, 1], ln_b[i, 1]], [x_is])
            if i < DEPTH - 1:
                ffn(lhs, w_gate_up[i], w_down[i], ALPHA)
                lhs = renorm("layer", r, ALPHA)
                x_is = (x_ready, n["xr"])
            else:
                m = mem_rows(0, [x_is])
                m_is = (x_ready, n["xr"])
                ffn(lhs, w_gate_up[i], w_down[i], ALPHA, evacuate=True, mem=m)
        for l in range(DEPTH2):
            lhs = split(r, m_is, (xt_hi, xt_lo))
            mkT = blk(0).rearrange("p (h s) -> p h s", s=SEQ)
            mvv = blk(1).rearrange("p (t c) -> p t c", t=T)
            mqT = blk(2).rearrange("p (h s) -> p h s", s=SEQ)
            tk = next_tok()
            linear(lhs, [(0, cols(mem_w_kv[l], 0, NW))], NW, "act", dst=tk, after=[])
            k_in = (aev, n["aev"])
            if l == 0:
                layer_norm()
            h_is = rms_norm()
            linear(lhs, [(0, cols(mem_w_kv[l], NW, 2 * NW))], NW, "act", dst=mvv, after=[])
            lhs = split(r, h_is, (xt_hi, xt_lo))
            k_ok = headnorm(tk.rearrange("p t (h d) -> p t h d", d=128), 4, 128, gains[:, l, 384:512], k_in)
            def w_cols(c0, width=NW):
                return [(0, cols(w_in[l], c0, c0 + width))]

            def gates(branch, between=lambda: None):
                held = []
                for half in range(2):
                    gtk = next_tok()
                    linear(lhs, w_cols(C_GATE + branch * D + half * NW), NW, "act", dst=gtk, func=ACT.Sigmoid,
                           after=[(dev, n["dev"]), (rope_done, n["rope"])])
                    held.append((gtk, n["aev"]))
                    if half == 0:
                        between()
                return held

            def lift(branch, ylhs, held, first=False):
                for half, (gtk, gate_is) in enumerate(held):
                    linear(ylhs, [(0, cols(w_lift[l, branch], half * NW, (half + 1) * NW))], NW, "lift", nkc=4,
                           gate=gtk, gate_is=gate_is, half=half, first=first, into=(SB, OB)[half])

            tq = next_tok()
            linear(lhs, w_cols(C_MQ), NW, "act", dst=tq, after=[])
            turn(tk, k_ok, mkT)
            q_ok = headnorm(tq.rearrange("p t (h d) -> p t h d", d=128), 4, 128, gains[:, l, 256:384], (aev, n["aev"]))
            for b_, c0 in enumerate((C_AX, C_AC, C_AB)):
                if b_ == 2:
                    turn(tq, q_ok, mqT)
                    add("exp_table")
                st = linear(lhs, w_cols(c0), NW, "act", turned=True, dst=blk(4 + b_).rearrange("p (h s) -> p h s", s=SEQ),
                            after=[])
            conv_in = (aev, n["aev"])
            ym = blk(3).rearrange("p (t c) -> p t c", t=T)
            units = []
            for h in range(4):
                units.append(dict(dv=128, sink=None, rows=[
                    ([(zeros[:, :], [(mqT[:, h, t * P:t * P + P], mkT[:, h, :], SEQ)])],
                     [mvv[:, s, h * 128:h * 128 + 128] for s in range(T)], ym[:, t, h * 128:h * 128 + 128])
                    for t in range(T)]))
            o_is = attention(units, 128 ** -0.5, [(aev, n["aev"])], (turn_done, n["turn"]), [st])
            ylhs = split(ym, o_is, (yt_hi, yt_lo), nkc=4)
            lift(3, ylhs, gates(3), first=True)
            add("conv", l=l, after=conv_in)
            n["conv"] += 1
            ylhs = (conv_done, [[n["conv"]] * 4] * T, (yt_hi, yt_lo))
            hq = blk(0).rearrange("p (h s) -> p h s", s=SEQ)
            hz = blk(1).rearrange("p (h s) -> p h s", s=SEQ)
            hv, hgate = hg_values, tok[:, 1]
            linear(lhs, w_cols(C_GF), NW, "act", turned=True, dst=hz, after=[])
            counts = (n["hga"], n["hgd"], n["hgp"])
            add("decay_logs", l=l, counts=counts, aev_z=n["aev"])
            linear(lhs, w_cols(C_GQ), NW, "act", turned=True, dst=hq, func=ACT.Silu, after=[])
            aev_q = n["aev"]
            add("decay_sums", l=l, counts=counts)
            held_gates = gates(0, lambda: add("decays", l=l, counts=counts))
            lift(0, ylhs, held_gates)
            linear(lhs, w_cols(C_GI), NW, "act", dst=hv, after=[(dev, n["dev"])])
            add("decayed", l=l, counts=counts, aev_q=aev_q)
            linear(lhs, w_cols(C_GG), NW, "act", dst=hgate, func=ACT.Silu, after=[(dev, n["dev"])])
            add("hgrn", l=l, counts=counts, aev_all=n["aev"], hv=hv)
            n["tp"] += T
            n["hga"] += 2 + (l > 0) + 2 * T
            n["hgd"] += 2 + (l > 0) + T + 3
            n["hgp"] += T + 3 + T
            y_ok = headnorm(hyc.rearrange("p t (h d) -> p t h d", d=128), 4, 128, gains[:, l, 128:256],
                            (hg_act, n["hga"]), gate=hgate.rearrange("p t (h d) -> p t h d", d=128))
            tok_i[0] = 1
            held_gates = gates(2)
            ylhs = split(hyc, y_ok, (yt_hi, yt_lo), nkc=4)
            lift(2, ylhs, held_gates)
            iqT = blk(0).rearrange("p (h s) -> p h s", s=SEQ)
            dqT = blk(1).rearrange("p (h s) -> p h s", s=SEQ)
            kkT = blk(2, 512).rearrange("p (h s) -> p h s", s=SEQ)
            kd = blk(2)[:, 512:1024].rearrange("p (t c) -> p t c", t=T)
            dvv = blk(3, 128).rearrange("p (t c) -> p t c", t=T)
            sel = blk(4, 512).rearrange("p (t c) -> p t c", t=T)
            yb = blk(5).rearrange("p (t c) -> p t c", t=T)
            linear(lhs, [(0, cols(w_in[l], C_DK, C_DK + 128)), (128, cols(w_in[l], C_IK, C_IK + 72))], SMALL, "act",
                   narrow=(kd, dvv), after=[])
            small_ok = (aev, n["aev"])
            headnorm(kd[:, :, 0:HD].rearrange("p t (h d) -> p t h d", d=HD), 1, HD, gains[:, l, 64:128], small_ok)
            rope(kd.rearrange("p t (h e) -> p t h e", e=128)[:, :, :, 0:HD], 2, 1, small_ok)
            add("dup", buf=kd.rearrange("p t (h e) -> p t h e", e=128))
            n["rope"] += 1
            kd_ok = (rope_done, n["rope"])
            tk = next_tok()
            linear(lhs, w_cols(C_DQ), NW, "act", dst=tk, after=[(dev, n["dev"])])
            headnorm(tk.rearrange("p t (h d) -> p t h d", d=HD), 8, HD, gains[:, l, 0:64], (aev, n["aev"]))
            q_ok = rope(tk.rearrange("p t (h d) -> p t h d", d=HD), 8, 1, (aev, n["aev"]))
            turn(kd, kd_ok, kkT, 2)
            tk2 = next_tok()
            linear(lhs, w_cols(C_IQ), NW, "act", dst=tk2, after=[(dev, n["dev"])])
            i_ok = rope(tk2.rearrange("p t (h d) -> p t h d", d=HD), 8, 1, (aev, n["aev"]))
            turn(tk, q_ok, dqT)

            def selection():
                turn(tk2, i_ok, iqT)
                add("select", iqT=iqT, kkT=kkT, sel=sel, ready=(turn_done, n["turn"]))
                n["rel"] += 4 * T
                n["seg"] += 4 * T
                n["sel"] += T

            held_gates = gates(1, selection)
            gate_st = [q for q in stages if q["kind"] == "linear"][-1]
            units = []
            for h in range(8):
                rows = []
                for t in range(T):
                    nk = P * (t + 1)
                    rows.append(([(sel[:, t, 0:nk], [(head_ap(dqT, h, t * P, t * P + P),
                                                      kkT[HD * (h % 2):HD * (h % 2) + HD, 0, 0:nk], nk)])],
                                 [dvv[:, s, :] for s in range(t + 1)], yb[:, t, h * HD:h * HD + HD]))
                units.append(dict(rows=rows, dv=HD, sink=None))
            o_is = attention(units, HD ** -0.5, [(aev, small_ok[1])], (turn_done, n["turn"]), [gate_st], lead=0)
            ylhs = split(yb, o_is, (yt_hi, yt_lo), nkc=4)
            lift(1, ylhs, held_gates)
            load_gains([norm_ffn[l]], [(dev, n["dev"]), (o_done, n["unit"])])
            lhs = split(r, (dev, n["dev"]), (xt_hi, xt_lo))
            lhs = renorm("rms", x, 1.0, lhs, w_out[l])
            m = mem_rows(l + 1, [(x_ready, n["xr"]), (tp_done, n["tp"]), (o_done, n["unit"])]) if l + 1 < DEPTH2 else None
            m_is = (x_ready, n["xr"])
            ffn(lhs, ffn_up[l], ffn_down[l], 1.0, evacuate=True, mem=m)
        end = n
        WIDE = len(chunks)

        full, count = [], [0, 0]
        for w, (loads, _, _) in enumerate(chunks):
            count[w % 2] += 16 * (2 if loads[0] == "ffn" else len(loads))
            full.append(count[w % 2])

        def wide(buf, w, nkc, ncols):
            return buf[:, w % 2, 0:nkc * ncols].rearrange("p (k n) -> p k n", n=ncols)

        block = ctx.enter_context(nc.Block())

        @block.sync
        def _(sp):
            for t_, pos in enumerate((positions, positions_2)):
                sp.dma_start(rope_pos[:, t_, :], pos[0].rearrange("(t p) -> p t", p=P), allow_slow_non_contiguous=True) \
                  .then_inc(loaded, 16)
            sp.dma_start(sinks[:, :, :], a_sinks.partition_broadcast(P)).then_inc(loaded, 16)
            sp.dma_start(x[:, :, :], x_in[0].rearrange("(t p) d -> p t d", p=P)).then_inc(in_full, 16)
            for st in stages:
                if st["kind"] == "linear" or st["kind"] == "renorm" and st["lhs"]:
                    for w in range(st["w"], st["w"] + (2 if st["kind"] == "renorm" else 1)):
                        loads, nkc, ncols = chunks[w]
                        if w >= 2:
                            sp.wait_ge(lo_done, 2 * (w - 1))
                        for c0, src in loads:
                            sp.dma_start(wide(raw, w, nkc, ncols)[:, :, c0:c0 + src.shape[2]], src) \
                              .then_inc(raw_full[w % 2], 16)
                elif st["kind"] == "ffn":
                    wu = st["wu"].rearrange("(k p) (g f) -> p k g f", p=P, g=2)
                    wd = st["wd"].rearrange("(j k p) n -> p (j k) n", k=2, p=P)

                    def up(j, s):
                        sp.wait_ge(lo_done, 2 * (st["w"] - 1) + 2 * j)
                        for g in range(2):
                            sp.dma_start(raw[:, s, :].rearrange("p (k g f) -> p k g f", k=KC, g=2)[:, :, g, :],
                                         wu[:, :, g, bass.ds(j * FN, FN)]).then_inc(raw_full[s], 16)

                    def down(j):
                        sp.wait_ge(dlo_done, 2 * (st["d"] + j))
                        sp.dma_start(draw[:, :, :], wd[:, bass.ds(j * 2, 2), :]).then_inc(draw_full, 16)

                    up(0, st["w"] % 2)
                    up(1, (st["w"] + 1) % 2)
                    sp.wait_ge(o_done, st["at"]["unit"])
                    sp.wait_ge(dev, st["at"]["dev"])
                    down(0)
                    up(2, st["w"] % 2)
                    with sp.Fori(0, (FJ - 3) // 2) as i:
                        for u in range(2):
                            up(i * 2 + 3 + u, (st["w"] + 1 + u) % 2)
                            down(i * 2 + 1 + u)
                    down(FJ - 2)
                    down(FJ - 1)
            sp.wait_ge(dev, end["dev"])
            sp.dma_start(out[0].rearrange("(t p) d -> p t d", p=P), x[:, :, :]) \
              .then_inc(out_full, 16)
            sp.wait_ge(out_full, 16)

        @block.gpsimd
        def _(pool):
            step = Steps(pool, pool_step)
            step.did(pool.memset(ident[:, :], 0.0))
            step.did(pool.memset(chmask[:, :], 1.0))
            step.settle()
            pool.affine_select(out=ident[:, :], in_=ident[:, :], compare_op=ALU.not_equal, fill=1.0, base=0,
                               pattern=[[-1, P]], channel_multiplier=1).then_inc(const_done, 1)
            step.did(pool.affine_select(out=chmask[:, :], in_=chmask[:, :], compare_op=ALU.is_ge, fill=0.0, base=0,
                                        pattern=[[1, P]], channel_multiplier=-1))
            step.settle()
            pool.memset(chmask[0:HGC, HGC:P], 0.0).then_inc(const_done, 1)
            pool.memset(mhalf, -0.5).then_inc(const_done, 1)
            pool.memset(zeros[:, :], 0.0).then_inc(const_done, 1)
            pool.iota(dist[:, :], pattern=[[-1, SEQ]], base=P, channel_multiplier=1).then_inc(const_done, 1)
            for i in range(HALF):
                pool.memset(freq[:, i:i + 1], float(np.float32(THETA) ** np.float32(-2.0 * i / ROT))) \
                    .then_inc(const_done, 1)

            def rstd(st, count, scale, eps):
                pool.wait_ge(var_done, st["at"]["stat"] + 1)
                step.did(pool.tensor_scalar(vst[:, 0:count], vst[:, 0:count], scale, eps, ALU.mult, ALU.add))
                step.settle()
                pool.tensor_tensor(rs[:, 0:count], vst[:, 0:count], mhalf[:, 0:count], ALU.pow).then_inc(rstd_done, 1)

            for st in stages:
                if st["kind"] == "gains":
                    for s_, v in st["after"]:
                        if v:
                            pool.wait_ge(s_, v)
                    for k, row in enumerate(st["rows"]):
                        pool.dma_start(gb[:, k, :], row.partition_broadcast(P)).then_inc(gb_full, 16)
                elif st["kind"] == "late_loads":
                    for l in range(DEPTH2):
                        for k, (g, o, w) in enumerate(((dsa_q_norm, 0, 64), (dsa_k_norm, 64, 64), (hg_out_norm, 128, 128),
                                                       (mem_q_norm, 256, 128), (mem_k_norm, 384, 128))):
                            pool.dma_start(gains[:, l, o:o + w], g[l].partition_broadcast(P)).then_inc(late_loaded, 16)
                        for k in range(3):
                            pool.dma_start(convw[:, l, k, :], conv_w[l, k].rearrange("(b p) -> p b", p=P),
                                           allow_slow_non_contiguous=True).then_inc(late_loaded, 16)
                        pool.dma_start(lbp[:, l, :], hg_lower[l].rearrange("(h p) -> p h", p=P),
                                       allow_slow_non_contiguous=True).then_inc(late_loaded, 16)
                elif st["kind"] == "abias":
                    for s_, v in st["after"]:
                        pool.wait_ge(s_, v)
                    pool.dma_start(abias, a_b_qkv[st["j"]].partition_broadcast(P)).then_inc(rows_full, 16)
                    pool.dma_start(abo, a_b_o[st["j"]].partition_broadcast(P)).then_inc(rows_full, 16)
                elif st["kind"] == "load_mem":
                    for s_, v in st["after"]:
                        pool.wait_ge(s_, v)
                    pool.dma_start(r[:, :, :], mem[0].rearrange("(t p) d -> p t d", p=P)).then_inc(rows_full, 16)
                    pool.dma_start(mem_gain, mem_norm.partition_broadcast(P)).then_inc(rows_full, 16)
                    pool.dma_start(mix_gain, norm_mix[st["l"]].partition_broadcast(P)).then_inc(rows_full, 16)
                elif st["kind"] == "renorm":
                    for t in range(T):
                        pool.wait_ge(var_done, st["at"]["stat"] + t + 1)
                        v = vst[:, t:t + 1]
                        if st["norm"] == "layer":
                            step.did(pool.tensor_scalar(v, mv[:, t, 1:2], 1.0, LN_EPS, ALU.mult, ALU.add))
                        else:
                            step.did(pool.tensor_scalar(v, v, 1.0 / D, RMS_EPS, ALU.mult, ALU.add))
                        step.settle()
                        pool.tensor_tensor(rs[:, t:t + 1], v, mhalf[:, 0:1], ALU.pow).then_inc(rstd_done, 1)
                elif st["kind"] == "layer_norm":
                    rstd(st, T, 1.0, LN_EPS)
                elif st["kind"] in ("rms_norm", "mem_norm"):
                    rstd(st, T, 1.0 / D, RMS_EPS)
                elif st["kind"] == "headnorm":
                    rstd(st, T * st["nh"], 1.0 / st["hd"], RMS_EPS)

        @block.scalar
        def _(act):
            step = Steps(act, act_step)

            def split_hi(w, late=0):
                if w >= WIDE:
                    return
                _, nkc, ncols = chunks[w]
                act.wait_ge(raw_full[w % 2], full[w])
                if w >= 2:
                    act.wait_ge(lin_done, 2 * (w - 1) + late)
                for h in range(2):
                    ks = slice(h * nkc // 2, (h + 1) * nkc // 2)
                    act.activation(wide(whi, w, nkc, ncols)[:, ks, :], wide(raw, w, nkc, ncols)[:, ks, :], ACT.Copy) \
                       .then_inc(hi_done, 1)

            def rows_hi(st, t):
                for g in range(2):
                    q = st["at"]["tp"] + 2 * t + g
                    act.wait_ge(tp_done, q + 1)
                    act.activation(xt_hi[:, 4 * g:4 * g + 4, t * P:(t + 1) * P],
                                   banks[TB[q % 2]][:, :].rearrange("p (k s) -> p k s", s=P), ACT.Copy).then_inc(thi_done, 1)

            for st in stages:
                at = st["at"]
                if st["kind"] == "setup":
                    act.wait_ge(trig, 1)
                    act.activation(rope_c[:, :, :, :], rope_c[:, :, :, :], ACT.Sin).then_inc(trig, 1)
                    act.activation(rope_s[:, :, :, :], rope_s[:, :, :, :], ACT.Sin).then_inc(trig, 1)
                elif st["kind"] == "exp_table":
                    act.wait_ge(const_done, 5 + HALF)
                    step.settle()
                    step.did(act.activation(small[:, 52:53], zeros[:, 0:1], ACT.Exp))
                elif st["kind"] == "bound_logs":
                    act.wait_ge(trig, 4)
                    step.did(act.activation(lbp[:, 3, :], lbp[:, 2, :], ACT.Abs))
                    step.settle()
                    step.did(act.activation(lbp[:, 4, :], lbp[:, 3, :], ACT.Exp, scale=-1.0))
                    step.settle()
                    act.activation(lbp[:, 5, :], lbp[:, 4, :], ACT.Ln, bias=1.0).then_inc(trig, 1)
                elif st["kind"] == "linear":
                    if st["w"] == 0:
                        split_hi(0)
                    split_hi(st["w"] + 1)
                    if st["second"]:
                        rows_hi(st["second"], 1)
                    if st["evac"] == "act":
                        for s_, v in st["after"]:
                            if v:
                                act.wait_ge(s_, v)
                        for t in range(T):
                            act.wait_ge(lin_done, 2 * st["w"] + t + 1)
                            ps = banks[LB[t]]
                            if st["turned"]:
                                act.activation(st["dst"][:, 2 * t:2 * t + 2, :],
                                               ps[:, :].rearrange("p (h s) -> p h s", s=SEQ), st["func"]).then_inc(aev, 1)
                            elif st["narrow"]:
                                kd, dvv = st["narrow"]
                                step.did(act.activation(kd[:, t, 0:HD], ps[:, 0:HD], ACT.Copy))
                                step.did(act.activation(dvv[:, t, :], ps[:, 64:128], ACT.Copy))
                                step.did(act.activation(kd[:, t, 128:128 + HD], ps[:, 128:192], ACT.Copy))
                                act.activation(iwb[:, t, :], ps[:, 192:200], ACT.Copy, scale=8 ** -0.5).then_inc(aev, 1)
                            else:
                                act.activation(st["dst"][:, t, :], ps[:, 0:st["ncols"]], st["func"]).then_inc(aev, 1)
                elif st["kind"] == "renorm":
                    if st["lhs"]:
                        split_hi(st["w"] + 1)
                        split_hi(st["w"] + 2, late=1)
                    rows_hi(st, 0)
                elif st["kind"] == "split":
                    hi, _ = st["dst"]
                    for g in range(st["nkc"] // 2):
                        act.wait_ge(tp_done, at["tp"] + g + 1)
                        act.activation(hi[:, 2 * g:2 * g + 2, :],
                                       banks[TB[(at["tp"] + g) % 2]][:, :].rearrange("p (k s) -> p k s", s=SEQ),
                                       ACT.Copy).then_inc(thi_done, 1)
                elif st["kind"] == "turn":
                    for t in range(T):
                        act.wait_ge(tp_done, at["tp"] + t + 1)
                        act.activation(st["dst"][:, 0:st["nb"], t * P:t * P + P],
                                       banks[TB[(at["tp"] + t) % 2]][:, 0:st["nb"] * P].rearrange("p (h s) -> p h s", s=P),
                                       ACT.Copy).then_inc(turn_done, 1)
                elif st["kind"] == "attention":
                    U = st["units"]

                    def exps(i):
                        u, k = U[i], at["unit"] + i
                        act.wait_ge(nb_done, k + 1)
                        if u["sink"]:
                            j, h = u["sink"]
                            step.did(act.activation(es[:, k % 4, 0:len(u["rows"])], nb[:, k % 4, 0:len(u["rows"])], ACT.Exp,
                                                    bias=sinks[:, j, h:h + 1]))
                        for row in range(len(u["rows"])):
                            mine = [q for q in u["pieces"] if q[0] == row]
                            q = slice(mine[0][1], mine[-1][1] + mine[-1][2])
                            ins = act.activation(sm[:, k % 3, q], sm[:, k % 3, q], ACT.Exp, bias=nb[:, k % 4, row:row + 1],
                                                 scale=st["scale"], accum_out=ls[:, k % 4, row:row + 1])
                        ins.then_inc(p_done, 1)

                    def evacuate(i):
                        u, k = U[i], at["unit"] + i
                        act.wait_ge(rl_done, k + 1)
                        act.wait_ge(pv_done, k + 1)
                        for row, (_, _, o) in enumerate(u["rows"]):
                            ins = act.activation(o, banks[OB[k % 2]][:, row * u["dv"]:(row + 1) * u["dv"]], ACT.Copy,
                                                 scale=rl[:, k % 4, row:row + 1])
                        ins.then_inc(o_done, 1)

                    for i in range(len(U) + 3):
                        if i < len(U):
                            exps(i)
                        if i >= 3:
                            evacuate(i - 3)
                elif st["kind"] == "ffn":
                    w0, d0 = st["w"], st["d"]

                    def hi_up(j, s, f):
                        act.wait_ge(raw_full[s], f)
                        act.wait_ge(lin_done, 2 * (w0 - 1) + 2 * j)
                        for h in range(2):
                            q = slice(h * 2048, (h + 1) * 2048)
                            act.activation(whi[:, s, q], raw[:, s, q], ACT.Copy).then_inc(hi_done, 1)

                    def hi_down(j):
                        act.wait_ge(draw_full, 16 * (d0 + j + 1))
                        act.wait_ge(down_done, d0 + j)
                        for k in range(2):
                            act.activation(dhi[:, k, :], draw[:, k, :], ACT.Copy).then_inc(dhi_done, 1)

                    def silu(j, t):
                        act.wait_ge(lin_done, 2 * w0 + 2 * j + t + 1)
                        act.activation(silu_g[:, t, :], banks[LB[t]][:, 0:FN], ACT.Silu).then_inc(silu_done, 1)

                    def hidden_hi(j, b):
                        act.wait_ge(tp_done, at["tp"] + j + 1)
                        act.activation(yt_hi[:, 2 * b:2 * b + 2, :],
                                       banks[TB[(at["tp"] + b) % 2]][:, :].rearrange("p (k s) -> p k s", s=SEQ),
                                       ACT.Copy).then_inc(thi_done, 1)

                    def slot(j, u, f):
                        hi_up(j + 1, (w0 + u + 1) % 2, f)
                        hi_down(j - 1)
                        silu(j, 0)
                        hidden_hi(j - 1, (u + 1) % 2)
                        silu(j, 1)

                    split_hi(w0 + 1)
                    if st["second"]:
                        rows_hi(st["second"], 1)
                    silu(0, 0)
                    silu(0, 1)
                    slot(1, 1, full[w0 + 2])
                    with act.Fori(0, (FJ - 3) // 2) as i:
                        slot(i * 2 + 2, 0, i * 32 + full[w0 + 3])
                        slot(i * 2 + 3, 1, i * 32 + full[w0 + 4])
                    hi_down(FJ - 2)
                    silu(FJ - 1, 0)
                    hidden_hi(FJ - 2, 1)
                    silu(FJ - 1, 1)
                    hidden_hi(FJ - 1, 0)
                    hi_down(FJ - 1)
                    split_hi(w0 + FJ)
                elif st["kind"] == "select":
                    for e in range(4 * T):
                        t, k = e // 4, at["rel"] + e
                        nk = P * (t + 1)
                        act.wait_ge(s_done, at["seg"] + e + 1)
                        if k >= 2:
                            act.wait_ge(rel_used, k - 1)
                        act.activation(relu2[:, k % 2, :, 0:nk],
                                       banks[SB[(at["seg"] + e) % 2]][:, :].rearrange("p (h s) -> p h s", s=SEQ)[:, :, 0:nk],
                                       ACT.Relu, scale=HD ** -0.5).then_inc(rel_done, 1)
                elif st["kind"] == "decay_logs":
                    ha, hd_, hp = st["counts"]
                    act.wait_ge(aev, st["aev_z"])
                    step.did(act.activation(blk(2), blk(1), ACT.Abs))
                    step.settle()
                    step.did(act.activation(blk(2), blk(2), ACT.Exp, scale=-1.0))
                    step.settle()
                    act.activation(blk(2), blk(2), ACT.Ln, bias=1.0).then_inc(hg_act, 1)
                elif st["kind"] == "decay_sums":
                    ha, hd_, hp = st["counts"]
                    if st["l"] > 0:
                        act.wait_ge(hg_dve, hd_ + 1)
                        step.did(act.activation(blk(7), blk(7), ACT.Abs))
                        step.settle()
                        step.did(act.activation(blk(7), blk(7), ACT.Exp, scale=-1.0))
                        step.settle()
                        act.activation(blk(7), blk(7), ACT.Ln, bias=1.0).then_inc(hg_act, 1)
                elif st["kind"] == "decays":
                    k = 1 if st["l"] > 0 else 0
                    ha, hd_, hp = st["counts"]
                    act.wait_ge(hg_dve, hd_ + k + 1)
                    step.did(act.activation(blk(4), blk(4), ACT.Exp, scale=-1.0))
                    step.did(act.activation(blk(7), blk(6), ACT.Exp, scale=-1.0))
                    step.settle()
                    step.did(act.activation(blk(6), blk(6), ACT.Exp))
                    step.did(act.activation(blk(2), blk(5), ACT.Exp))
                    step.did(act.activation(hdl[:, :], chunked(5)[:, :, HGC - 1], ACT.Exp))
                    act.activation(blk(8), blk(8), ACT.Exp).then_inc(hg_act, 1)
                elif st["kind"] == "hgrn":
                    ha, hd_, hp = st["counts"]
                    for t in range(T):
                        act.wait_ge(tp_done, at["tp"] + t + 1)
                        act.activation(tiled(4)[:, t, :], banks[TB[(at["tp"] + t) % 2]][:, :], ACT.Copy) \
                           .then_inc(hg_act, 1)
                    for t in range(T):
                        act.wait_ge(hg_pe, hp + T + 3 + t + 1)
                        act.activation(hyc[:, t, :], banks[OB[t]][:, :], ACT.Copy).then_inc(hg_act, 1)

        @block.vector
        def _(dve):
            step = Steps(dve, dve_step)

            def split_lo(w, halves=(0, 1)):
                if w >= WIDE:
                    return
                _, nkc, ncols = chunks[w]
                for h in halves:
                    ks = slice(h * nkc // 2, (h + 1) * nkc // 2)
                    dve.wait_ge(hi_done, 2 * w + h + 1)
                    dve.tensor_tensor(wide(wlo, w, nkc, ncols)[:, ks, :], wide(raw, w, nkc, ncols)[:, ks, :],
                                      wide(whi, w, nkc, ncols)[:, ks, :].bitcast(F32), ALU.subtract).then_inc(lo_done, 1)

            def rows_lo(st, t):
                for g in range(2):
                    q = st["at"]["tp"] + 2 * t + g
                    dst = (slice(None), slice(4 * g, 4 * g + 4), slice(t * P, (t + 1) * P))
                    dve.wait_ge(thi_done, st["at"]["sg"] + 2 * t + g + 1)
                    dve.tensor_tensor(xt_lo[dst], banks[TB[q % 2]][:, :].rearrange("p (k s) -> p k s", s=P),
                                      xt_hi[dst].bitcast(F32), ALU.subtract).then_inc(tlo_done, 1)

            def next_lo(st, w):
                split_lo(w, (0,))
                if st["second"]:
                    rows_lo(st["second"], 1)
                split_lo(w, (1,))

            def rms_rows(st, src, gain):
                for t in range(T):
                    ins = dve.tensor_tensor_reduce(out=blk(6), in0=src[:, t, :], in1=src[:, t, :], scale=1.0,
                                                   scalar=0.0, op0=ALU.mult, op1=ALU.add, accum_out=vst[:, t:t + 1])
                    if t < T - 1:
                        step.did(ins)
                        step.settle()
                ins.then_inc(var_done, 1)
                dve.wait_ge(rstd_done, st["at"]["stat"] + 1)
                for t in range(T):
                    dve.scalar_tensor_tensor(out=r[:, t, :], in0=src[:, t, :], scalar=rs[:, t:t + 1], in1=gain,
                                             op0=ALU.mult, op1=ALU.mult).then_inc(x_ready, 1)

            def layer_rows(t, src, count):
                dve.wait_ge(var_done, count)
                step.did(dve.scalar_tensor_tensor(out=x[:, t, :], in0=src[:, t, :], scalar=mv[:, t, 0:1], in1=gb[:, 0, :],
                                                  op0=ALU.subtract, op1=ALU.mult))
                step.settle()
                dve.wait_ge(rstd_done, count)
                dve.scalar_tensor_tensor(out=x[:, t, :], in0=x[:, t, :], scalar=rs[:, t:t + 1], in1=gb[:, 1, :],
                                         op0=ALU.mult, op1=ALU.add).then_inc(x_ready, 1)

            for st in stages:
                at = st["at"]
                if st["kind"] == "setup":
                    dve.wait_ge(const_done, 5 + HALF)
                    dve.wait_ge(loaded, 16 * N_FIRST)
                    ang, turns_i, turns_f, sub, r_, c_ = (rwork[:, q, :] for q in range(6))
                    for b in range(2):
                        for t in range(T):
                            q = (b * T + t) * HALF
                            step.did(dve.tensor_copy(sub[:, q:q + HALF],
                                                     rope_pos[:, b, t:t + 1].to_broadcast([P, HALF])))
                    step.settle()
                    for q in range(2 * T):
                        step.did(dve.tensor_tensor(ang[:, q * HALF:(q + 1) * HALF], sub[:, q * HALF:(q + 1) * HALF], freq,
                                                   ALU.mult))
                    step.settle()
                    step.did(dve.tensor_scalar(turns_i.bitcast(I32), ang, 1 / TWO_PI, None, ALU.mult))
                    step.settle()
                    step.did(dve.tensor_copy(turns_f, turns_i.bitcast(I32)))
                    step.settle()
                    src = ang
                    for part in PI_PARTS:
                        step.did(dve.scalar_tensor_tensor(out=r_, in0=turns_f, scalar=-part, in1=src, op0=ALU.mult,
                                                          op1=ALU.add))
                        step.settle()
                        src = r_
                    for op, edge, by in ((ALU.is_gt, np.pi, -TWO_PI), (ALU.is_lt, -np.pi, TWO_PI)):
                        step.did(dve.tensor_scalar(sub, r_, float(edge), float(by), op, ALU.mult))
                        step.settle()
                        step.did(dve.tensor_tensor(r_, r_, sub, ALU.add))
                        step.settle()
                    step.did(dve.tensor_scalar(c_, r_, float(np.pi / 2), None, ALU.add))
                    step.settle()
                    step.did(dve.tensor_scalar(sub, c_, float(np.pi), float(-TWO_PI), ALU.is_gt, ALU.mult))
                    step.settle()
                    step.did(dve.tensor_tensor(c_, c_, sub, ALU.add))
                    step.settle()
                    for dst, a in ((rope_s, r_), (rope_c, c_)):
                        ins = dve.tensor_scalar(dst[:, :, :, :].rearrange("p b t c -> p (b t c)"), a, PI_IN, -PI_IN,
                                                ALU.min, ALU.max)
                        if dst is rope_s:
                            step.did(ins)
                    ins.then_inc(trig, 1)
                    step.settle()
                    dve.wait_ge(trig, 3)
                elif st["kind"] == "masks":
                    step.did(dve.tensor_scalar(masks[:, 0, :], dist, 0, NEG, ALU.is_lt, ALU.mult))
                    step.did(dve.tensor_scalar(masks[:, 1, :], dist, A_REACH, NEG, ALU.is_gt, ALU.mult))
                    step.did(dve.tensor_scalar(masks[:, 2, :], dist, B_REACH, NEG, ALU.is_gt, ALU.mult))
                    for g, dil in enumerate(DILATIONS[1:]):
                        step.did(dve.tensor_scalar(dwork, dist, dil - 1, None, ALU.bitwise_and))
                        step.settle()
                        step.did(dve.tensor_scalar(masks[:, 3 + g, :], dwork, 0, NEG, ALU.is_gt, ALU.mult))
                        step.settle()
                    for q in range(1, 5):
                        step.did(dve.tensor_tensor(masks[:, q, :], masks[:, q, :], masks[:, 0, :], ALU.add))
                    step.did(dve.tensor_scalar(sk8[:, :, :], sinks[:, :, :], HD ** 0.5, None, ALU.mult))
                    step.settle()
                elif st["kind"] == "bound_logs":
                    dve.wait_ge(late_loaded, 16 * N_LATE)
                    dve.tensor_tensor(lbp[:, 2, :], lbp[:, 1, :], lbp[:, 0, :], ALU.subtract).then_inc(trig, 1)
                    dve.wait_ge(trig, 5)
                    step.did(dve.scalar_tensor_tensor(out=lbp[:, 6, :], in0=lbp[:, 2, :], scalar=0.0, in1=lbp[:, 5, :],
                                                      op0=ALU.min, op1=ALU.subtract))
                    step.settle()
                    step.did(dve.tensor_tensor(lbp[:, 7, :], lbp[:, 6, :], lbp[:, 2, :], ALU.subtract))
                    step.settle()
                elif st["kind"] == "linear":
                    if st["w"] == 0:
                        split_lo(0)
                    next_lo(st, st["w"] + 1)
                    if st["evac"] == "act":
                        continue
                    if st["evac"] == "bias":
                        dve.wait_ge(rows_full, 16 * st["inn"])
                    if st["evac"] == "lift":
                        dve.wait_ge(aev, st["gate_is"])
                    for t in range(T):
                        dve.wait_ge(lin_done, 2 * st["w"] + t + 1)
                        ps = banks[st["into"][t]]
                        if st["evac"] == "bias":
                            c0 = st["c"] * NW
                            if st["c"] < 2:
                                dve.tensor_tensor(st["tk"][:, t, :], ps[:, :], abias[:, c0:c0 + NW], ALU.add).then_inc(dev, 1)
                                continue
                            kd = st["tk"][:, t, :].rearrange("p (h e d) -> p h e d", e=2, d=HD)
                            for e in range(2):
                                step.did(dve.tensor_tensor(kd[:, :, e, :],
                                                           ps[:, 0:256].rearrange("p (h d) -> p h d", d=HD),
                                                           abias[:, c0:c0 + 256].rearrange("p (h d) -> p h d", d=HD),
                                                           ALU.add))
                            dve.tensor_tensor(st["v"][:, t, :], ps[:, 256:512], abias[:, c0 + 256:c0 + 512], ALU.add) \
                               .then_inc(dev, 1)
                        else:
                            h0 = st["half"] * NW
                            if st["first"]:
                                dve.tensor_tensor(r[:, t, h0:h0 + NW], st["gate"][:, t, :], ps[:, :], ALU.mult) \
                                   .then_inc(dev, 1)
                            else:
                                step.did(dve.tensor_tensor(st["gate"][:, t, :], st["gate"][:, t, :], ps[:, :], ALU.mult))
                                step.settle()
                                dve.tensor_tensor(r[:, t, h0:h0 + NW], r[:, t, h0:h0 + NW], st["gate"][:, t, :], ALU.add) \
                                   .then_inc(dev, 1)
                elif st["kind"] == "renorm":
                    w, dst = st["w"], st["dst"]

                    def add_residual(t, h):
                        cs = slice(h * NW, (h + 1) * NW)
                        if st["lhs"]:
                            dve.wait_ge(lin_done, 2 * w + 2 * t + h + 1)
                            ps = banks[LB[h]]
                        else:
                            ps = banks[ACC[t][h]]
                        ins = dve.scalar_tensor_tensor(out=dst[:, t, cs], in0=x[:, t, cs], scalar=st["alpha"], in1=ps[:, :],
                                                       op0=ALU.mult, op1=ALU.add)
                        if st["bias"] is not None:
                            step.did(ins)
                            step.settle()
                            ins = dve.tensor_tensor(dst[:, t, cs], dst[:, t, cs], st["bias"][:, cs], ALU.add)
                        ins.then_inc(dev, 1)

                    def statistics(t):
                        dve.wait_ge(dev, at["dev"] + 2 * t + 2)
                        if st["norm"] == "layer":
                            for h in range(2):
                                step.did(dve.bn_stats(bns[:, t, h, :], dst[:, t, h * NW:(h + 1) * NW]))
                            step.settle()
                            dve.bn_aggr(mv[:, t, :], bns[:, t, :, :].rearrange("p h s -> p (h s)")).then_inc(var_done, 1)
                        else:
                            dve.tensor_tensor_reduce(out=smflat[:, 0:D], in0=dst[:, t, :], in1=dst[:, t, :], scale=1.0,
                                                     scalar=0.0, op0=ALU.mult, op1=ALU.add,
                                                     accum_out=vst[:, t:t + 1]).then_inc(var_done, 1)

                    def normalise(t):
                        dve.wait_ge(gb_full, 16 * st["gbv"])
                        if st["norm"] == "layer":
                            layer_rows(t, dst, at["stat"] + t + 1)
                        else:
                            dve.wait_ge(rstd_done, at["stat"] + t + 1)
                            dve.scalar_tensor_tensor(out=r[:, t, :], in0=dst[:, t, :], scalar=rs[:, t:t + 1],
                                                     in1=gb[:, 0, :], op0=ALU.mult, op1=ALU.mult).then_inc(x_ready, 1)

                    if st["lhs"]:
                        split_lo(w + 1)
                    else:
                        dve.wait_ge(sum_done, st["at"]["ffn"])
                    add_residual(0, 0)
                    add_residual(0, 1)
                    statistics(0)
                    normalise(0)
                    if not st["lhs"]:
                        dve.wait_ge(down_done, st["at"]["d"])
                    add_residual(1, 0)
                    if st["lhs"]:
                        split_lo(w + 2, (0,))
                    add_residual(1, 1)
                    rows_lo(st, 0)
                    split_lo(w + 2 if st["lhs"] else w, (1,))
                    statistics(1)
                    normalise(1)
                elif st["kind"] == "split":
                    hi, lo = st["dst"]
                    for g in range(st["nkc"] // 2):
                        dve.wait_ge(thi_done, at["sg"] + g + 1)
                        dve.tensor_tensor(lo[:, 2 * g:2 * g + 2, :],
                                          banks[TB[(at["tp"] + g) % 2]][:, :].rearrange("p (k s) -> p k s", s=SEQ),
                                          hi[:, 2 * g:2 * g + 2, :].bitcast(F32), ALU.subtract).then_inc(tlo_done, 1)
                elif st["kind"] == "rope":
                    dve.wait_ge(*st["after"])
                    if at["rope"]:
                        dve.wait_ge(rope_done, at["rope"])
                    nh = st["nh"]
                    x1, x2 = st["buf"][:, :, :, 0:HALF], st["buf"][:, :, :, HALF:ROT]
                    cs, sn = (f[:, st["table"]].unsqueeze(2).to_broadcast([P, T, nh, HALF]) for f in (rope_c, rope_s))
                    tm = [rtmp[:, q, 0:T * nh * HALF].rearrange("p (t h c) -> p t h c", t=T, h=nh) for q in range(4)]
                    for q, (a, b) in enumerate(((x1, cs), (x2, sn), (x2, cs), (x1, sn))):
                        step.did(dve.tensor_tensor(tm[q], a, b, ALU.mult))
                    step.settle()
                    step.did(dve.tensor_tensor(x1, tm[0], tm[1], ALU.subtract))
                    dve.tensor_tensor(x2, tm[2], tm[3], ALU.add).then_inc(rope_done, 1)
                elif st["kind"] == "dup":
                    dve.wait_ge(rope_done, at["rope"])
                    dve.tensor_copy(st["buf"][:, :, :, HD:2 * HD], st["buf"][:, :, :, 0:HD]).then_inc(rope_done, 1)
                elif st["kind"] == "headnorm":
                    nh, hd = st["nh"], st["hd"]
                    dve.wait_ge(*st["after"])
                    dve.wait_ge(x_ready, at["xr"])
                    if at["rope"]:
                        dve.wait_ge(rope_done, at["rope"])
                    sq = sqr[:, 0:T * nh * hd].rearrange("p (t h d) -> p t h d", t=T, h=nh)
                    step.did(dve.tensor_tensor(sq, st["buf"], st["buf"], ALU.mult))
                    step.settle()
                    dve.tensor_reduce(vst[:, 0:T * nh].rearrange("p (t h) -> p t h", t=T), sq, AX.X, ALU.add) \
                       .then_inc(var_done, 1)
                    dve.wait_ge(rstd_done, at["stat"] + 1)
                    by = rs[:, 0:T * nh].rearrange("p (t h) -> p t h", t=T).unsqueeze(3).to_broadcast([P, T, nh, hd])
                    step.did(dve.tensor_tensor(st["buf"], st["buf"], by, ALU.mult))
                    step.settle()
                    g = st["gain"].unsqueeze(1).unsqueeze(1).to_broadcast([P, T, nh, hd])
                    if st["gate"] is None:
                        dve.tensor_tensor(st["buf"], st["buf"], g, ALU.mult).then_inc(rope_done, 1)
                    else:
                        step.did(dve.tensor_tensor(st["buf"], st["buf"], g, ALU.mult))
                        step.settle()
                        dve.tensor_tensor(st["buf"], st["buf"], st["gate"], ALU.mult).then_inc(rope_done, 1)
                elif st["kind"] == "layer_norm":
                    dve.wait_ge(dev, at["dev"])
                    for t in range(T):
                        for h in range(2):
                            step.did(dve.bn_stats(bns[:, t, h, :], x[:, t, h * NW:(h + 1) * NW]))
                    step.settle()
                    for t in range(T):
                        step.did(dve.bn_aggr(mv[:, t, :], bns[:, t, :, :].rearrange("p h s -> p (h s)")))
                    step.settle()
                    dve.tensor_copy(vst[:, 0:T], mv[:, :, 1]).then_inc(var_done, 1)
                    dve.wait_ge(gb_full, 16 * st["gbv"])
                    for t in range(T):
                        layer_rows(t, x, at["stat"] + 1)
                elif st["kind"] == "rms_norm":
                    dve.wait_ge(dev, at["dev"])
                    if at["xr"]:
                        dve.wait_ge(x_ready, at["xr"])
                    rms_rows(st, x, mix_gain)
                elif st["kind"] == "attention":
                    U = st["units"]
                    if at["sel"]:
                        dve.wait_ge(sel_done, at["sel"])

                    def maxima(i):
                        u, k = U[i], at["unit"] + i
                        count = len(u["rows"])
                        for q, (row, off, width, bank, b0, m, products) in enumerate(u["pieces"]):
                            dve.wait_ge(s_done, u["seg0"] + bank + 1)
                            shape = (lambda f: f) if len(m.shape) == 2 else \
                                (lambda f: f.rearrange("p (g c) -> p g c", g=len(products)))
                            dve.tensor_tensor_reduce(out=shape(sm[:, k % 3, off:off + width]),
                                                     in0=shape(banks[QB[(u["bank0"] + bank) % 4]][:, b0:b0 + width]), in1=m,
                                                     scale=1.0, scalar=TAKEN, op0=ALU.add, op1=ALU.max,
                                                     accum_out=mxs[:, k % 4, q:q + 1]).then_inc(ttr_done, 1)
                        dve.wait_ge(ttr_done, u["ttr0"] + len(u["pieces"]))
                        mx, one = mxs[:, k % 4, 0:count], mx1[:, k % 4, 0:count]
                        if len(u["pieces"]) > count:
                            step.did(dve.tensor_reduce(one, mxs[:, k % 4, 0:len(u["pieces"])], AX.X, ALU.max))
                            step.settle()
                            mx = one
                        if u["sink"]:
                            j, h = u["sink"]
                            step.did(dve.tensor_tensor(one, mx, sk8[:, j, h:h + 1].to_broadcast([P, count]), ALU.max))
                            step.settle()
                            mx = one
                        dve.tensor_scalar(nb[:, k % 4, 0:count], mx, -st["scale"], None, ALU.mult).then_inc(nb_done, 1)

                    def copies(i):
                        u, k = U[i], at["unit"] + i
                        if k >= 2:
                            dve.wait_ge(pv_done, k - 1)
                        for q, (c0, c1) in enumerate(u["turns"]):
                            dve.wait_ge(tp_done, u["tp0"] + q + 1)
                            dve.tensor_copy(pts[:, k % 2, c0:c1], banks[TB[(u["tp0"] + q) % 2]][:, 0:c1 - c0]) \
                               .then_inc(pt_done, 1)

                    def reciprocal(i):
                        u, k = U[i], at["unit"] + i
                        count = len(u["rows"])
                        dve.wait_ge(p_done, k + 1)
                        if u["sink"]:
                            step.did(dve.tensor_tensor(ls[:, k % 4, 0:count], ls[:, k % 4, 0:count], es[:, k % 4, 0:count],
                                                       ALU.add))
                            step.settle()
                        dve.reciprocal(rl[:, k % 4, 0:count], ls[:, k % 4, 0:count]).then_inc(rl_done, 1)

                    for i in range(len(U) + 2):
                        if i < len(U):
                            maxima(i)
                        if i >= 2:
                            copies(i - 2)
                            reciprocal(i - 2)
                elif st["kind"] == "ffn":
                    w0, d0 = st["w"], st["d"]

                    def lo_up(j, s):
                        for h in range(2):
                            q = slice(h * 2048, (h + 1) * 2048)
                            dve.wait_ge(hi_done, 2 * w0 + 2 * j + h + 1)
                            dve.tensor_tensor(wlo[:, s, q], raw[:, s, q], whi[:, s, q].bitcast(F32), ALU.subtract) \
                               .then_inc(lo_done, 1)

                    def lo_down(j):
                        for k in range(2):
                            dve.wait_ge(dhi_done, 2 * (d0 + j) + k + 1)
                            dve.tensor_tensor(dlo[:, k, :], draw[:, k, :], dhi[:, k, :].bitcast(F32), ALU.subtract) \
                               .then_inc(dlo_done, 1)

                    def gated(j, t, b):
                        dve.wait_ge(silu_done, at["h"] + 2 * j + t + 1)
                        dve.tensor_tensor(hid[:, b, t, :], silu_g[:, t, :], banks[LB[t]][:, FN:2 * FN], ALU.mult) \
                           .then_inc(h_done, 1)

                    def hidden_lo(j, b):
                        dve.wait_ge(thi_done, at["sg"] + j + 1)
                        dve.tensor_tensor(yt_lo[:, 2 * b:2 * b + 2, :],
                                          banks[TB[(at["tp"] + b) % 2]][:, :].rearrange("p (k s) -> p k s", s=SEQ),
                                          yt_hi[:, 2 * b:2 * b + 2, :].bitcast(F32), ALU.subtract).then_inc(tlo_done, 1)

                    def slot(j, u):
                        lo_up(j + 1, (w0 + u + 1) % 2)
                        lo_down(j - 1)
                        gated(j, 0, u)
                        hidden_lo(j - 1, (u + 1) % 2)
                        gated(j, 1, u)

                    next_lo(st, w0 + 1)
                    gated(0, 0, 0)
                    gated(0, 1, 0)
                    slot(1, 1)
                    if st["mem"]:
                        dve.wait_ge(rows_full, 16 * st["mem"]["inn"])
                        rms_rows(st["mem"], r, mem_gain)
                    with dve.Fori(0, (FJ - 3) // 2) as i:
                        slot(i * 2 + 2, 0)
                        slot(i * 2 + 3, 1)
                    lo_down(FJ - 2)
                    gated(FJ - 1, 0, 0)
                    hidden_lo(FJ - 2, 1)
                    gated(FJ - 1, 1, 0)
                    hidden_lo(FJ - 1, 0)
                    lo_down(FJ - 1)
                    split_lo(w0 + FJ, (0, 1) if st["evacuate"] else (0,))
                    if not st["evacuate"]:
                        continue
                    dve.wait_ge(down_done, d0 + FJ)
                    for t in range(T):
                        for h in range(2):
                            q = slice(h * NW, (h + 1) * NW)
                            dve.scalar_tensor_tensor(out=x[:, t, q], in0=x[:, t, q], scalar=st["alpha"],
                                                     in1=banks[ACC[t][h]][:, :], op0=ALU.mult, op1=ALU.add).then_inc(dev, 1)
                elif st["kind"] == "conv":
                    dve.wait_ge(*st["after"])
                    u, y = headed(4), headed(7)
                    step.did(dve.tensor_tensor(blk(4), blk(4), blk(5), ALU.mult))
                    step.settle()
                    for b in range(4):
                        step.did(dve.tensor_scalar(y[:, b, :], u[:, b, :], convw[:, st["l"], 2, b:b + 1], None, ALU.mult))
                    step.settle()
                    for back in (1, 2):
                        for b in range(4):
                            step.did(dve.scalar_tensor_tensor(out=y[:, b, back:SEQ], in0=u[:, b, 0:SEQ - back],
                                                              scalar=convw[:, st["l"], 2 - back, b:b + 1],
                                                              in1=y[:, b, back:SEQ], op0=ALU.mult, op1=ALU.add))
                        step.settle()
                    step.did(dve.tensor_tensor(blk(7), blk(7), blk(6), ALU.mult))
                    step.settle()
                    step.did(dve.tensor_copy(yt_hi[:, :, :], y))
                    step.settle()
                    dve.tensor_tensor(yt_lo[:, :, :], y, yt_hi[:, :, :].bitcast(F32), ALU.subtract).then_inc(conv_done, 1)
                elif st["kind"] == "decay_logs":
                    k = 1 if st["l"] > 0 else 0
                    ha, hd_, hp = st["counts"]
                    by_channel = [lbp[:, q, :].unsqueeze(2).to_broadcast([P, HG, SEQ]) for q in (6, 7)]
                    step.did(dve.memset(sqr, 1.0))
                    step.settle()
                    step.did(dve.memset(sqr.rearrange("p (c s) -> p c s", s=HGC)[:, :, 0:1], 0.0))
                    dve.wait_ge(hg_act, ha + 1)
                    step.did(dve.scalar_tensor_tensor(out=blk(3), in0=blk(1), scalar=0.0, in1=blk(2), op0=ALU.min,
                                                      op1=ALU.subtract))
                    step.did(dve.scalar_tensor_tensor(out=blk(4), in0=blk(1), scalar=0.0, in1=blk(2), op0=ALU.max,
                                                      op1=ALU.add))
                    step.settle()
                    if k:
                        step.did(dve.tensor_tensor(headed(3), headed(3), by_channel[1], ALU.add))
                        step.did(dve.tensor_tensor(headed(4), headed(4), by_channel[1], ALU.subtract))
                        step.settle()
                        dve.tensor_tensor(headed(7), headed(3), by_channel[0], ALU.subtract).then_inc(hg_dve, 1)
                        step.did(dve.tensor_tensor(headed(6), headed(3), by_channel[0], ALU.max))
                elif st["kind"] == "decay_sums":
                    k = 1 if st["l"] > 0 else 0
                    ha, hd_, hp = st["counts"]
                    step.settle()
                    if k:
                        dve.wait_ge(hg_act, ha + 2)
                        step.settle()
                        step.did(dve.tensor_tensor(blk(3), blk(6), blk(7), ALU.add))
                        step.settle()
                    step.did(dve.tensor_tensor_scan(blk(5), sqr, blk(3), 0.0, ALU.mult, ALU.add))
                    step.settle()
                    cum = chunked(5)
                    mid, last = (cum[:, :, q:q + 1].to_broadcast([P, CH, HGC]) for q in (HGC // 2 - 1, HGC - 1))
                    step.did(dve.tensor_tensor(chunked(6), cum, mid, ALU.subtract))
                    dve.tensor_tensor(chunked(8), last, cum, ALU.subtract).then_inc(hg_dve, 1)
                elif st["kind"] == "decayed":
                    k = 1 if st["l"] > 0 else 0
                    ha, hd_, hp = st["counts"]
                    dve.wait_ge(hg_act, ha + k + 2)
                    dve.wait_ge(aev, st["aev_q"])
                    step.did(dve.tensor_tensor(blk(6), blk(0), blk(6), ALU.mult))
                    step.did(dve.tensor_tensor(blk(7), blk(4), blk(7), ALU.mult))
                    step.did(dve.tensor_tensor(blk(8), blk(4), blk(8), ALU.mult))
                    for q in (1, 3):
                        step.did(dve.memset(blk(q), 0.0))
                    step.settle()
                    for q, dst in enumerate((1, 3)):
                        even = [blk(z).rearrange("p (b c s) -> p b c s", c=2, s=HGC)[:, :, q, :] for z in (dst, 0, 2)]
                        ins = dve.tensor_tensor(even[0], even[1], even[2], ALU.mult)
                        if q == 0:
                            step.did(ins)
                    ins.then_inc(hg_dve, 1)
                elif st["kind"] == "hgrn":
                    k = 1 if st["l"] > 0 else 0
                    ha, hd_, hp = st["counts"]
                    for t in range(T):
                        dve.wait_ge(hg_pe, hp + t + 1)
                        dve.tensor_tensor(tiled(5)[:, t, :].rearrange("p (h s) -> p h s", s=P),
                                          banks[SB[t]][:, :].rearrange("p (h s) -> p h s", s=P),
                                          chmask[:, :].unsqueeze(1).to_broadcast([P, HG, P]), ALU.mult).then_inc(hg_dve, 1)
                    dve.wait_ge(hg_pe, hp + T + 1)
                    dve.tensor_copy(HSTATE[0], banks["O0"][:, :]).then_inc(hg_dve, 1)
                    for c, bank in ((1, "O1"), (2, "S0")):
                        dve.wait_ge(hg_pe, hp + T + 1 + c)
                        dve.wait_ge(hg_dve, hd_ + k + 2 + T + c)
                        for h in range(HG):
                            q = slice(h * P, (h + 1) * P)
                            ins = dve.scalar_tensor_tensor(out=HSTATE[c][:, q], in0=HSTATE[c - 1][:, q],
                                                           scalar=hdl[:, h * NCH + c:h * NCH + c + 1],
                                                           in1=banks[bank][:, q], op0=ALU.mult, op1=ALU.add)
                            if h < HG - 1:
                                step.did(ins)
                        ins.then_inc(hg_dve, 1)
                elif st["kind"] == "select":
                    pairs = blk(7).rearrange("p (t b s) -> p t b s", t=T, b=2)
                    score = [pairs[:, t, :, 0:P * (t + 1)] for t in range(T)]
                    for t in range(T):
                        acc = score[t][:, 0, :]
                        for e in range(4):
                            k = at["rel"] + 4 * t + e
                            dve.wait_ge(rel_done, k + 1)
                            for q in range(2):
                                h = 2 * (2 * (e % 2) + q) + e // 2
                                rel, w = relu2[:, k % 2, q, 0:P * (t + 1)], iwb[:, t, h:h + 1]
                                if e == 0 and q == 0:
                                    ins = dve.tensor_scalar(acc, rel, w, None, ALU.mult)
                                else:
                                    ins = dve.scalar_tensor_tensor(out=acc, in0=rel, scalar=w, in1=acc, op0=ALU.mult,
                                                                   op1=ALU.add)
                                if q == 0:
                                    step.did(ins)
                                    step.settle()
                            ins.then_inc(rel_used, 1)
                            dve.wait_ge(rel_used, k + 1)
                    for t in range(T):
                        step.did(dve.tensor_tensor(score[t][:, 0, :], score[t][:, 0, :], causal(0, t)[0], ALU.add))
                    for i in range(TOPK // GRP):
                        for t in range(T):
                            step.settle(1)
                            step.did(dve.max(m8[:, t, :], score[t][:, i % 2, :]))
                        for t in range(T):
                            step.settle(1)
                            step.did(dve.match_replace(score[t][:, (i + 1) % 2, :], m8[:, t, :], score[t][:, i % 2, :], TAKEN))
                    left = (TOPK // GRP) % 2
                    for t in range(T):
                        step.settle(1)
                        step.did(dve.tensor_scalar(st["sel"][:, t, 0:P * (t + 1)], score[t][:, left, :], TAKEN / 2, NEG,
                                                   ALU.is_gt, ALU.mult))
                    for t in range(T):
                        step.settle(1 - t)
                        dve.tensor_tensor(st["sel"][:, t, 0:P * (t + 1)], st["sel"][:, t, 0:P * (t + 1)], causal(0, t)[0],
                                          ALU.add).then_inc(sel_done, 1)

        @block.tensor
        def _(pe):
            held = {}

            def take(bank):
                if bank in held:
                    pe.wait_ge(*held.pop(bank))

            def turn_rows(st, t):
                pe.wait_ge(x_ready, st["at"]["xr"] + t + 1)
                for g in range(2):
                    q = st["at"]["tp"] + 2 * t + g
                    name = TB[q % 2]
                    take(name)
                    for k in range(4):
                        c0 = (4 * g + k) * P
                        mm = pe.transpose(banks[name][:, k * P:(k + 1) * P], st["rows"][:, t, c0:c0 + P], ident[:, :])
                    mm.then_inc(tp_done, 1)
                    held[name] = (tlo_done, st["at"]["sg"] + 2 * t + g + 1)

            def turn_heads(st):
                at = st["at"]
                pe.wait_ge(*st["ready"])
                for t in range(T):
                    name = TB[(at["tp"] + t) % 2]
                    take(name)
                    for b in range(st["nb"]):
                        mm = pe.transpose(banks[name][:, b * P:(b + 1) * P], st["src"][:, t, b * P:(b + 1) * P], ident[:, :])
                    mm.then_inc(tp_done, 1)
                    held[name] = (turn_done, at["turn"] + t + 1)

            def product(st):
                at = st["at"]
                w, nkc = st["w"], st["nkc"]
                ready, values, (xh, xl) = st["lhs"]
                wh, wl = wide(whi, w, nkc, st["ncols"]), wide(wlo, w, nkc, st["ncols"])
                frees = (aev, at["aev"]) if st["evac"] == "act" else (dev, at["dev"])

                def needs(k):
                    if k % 2 == 0:
                        pe.wait_ge(ready, values[0][k + 1])
                    if k in (0, nkc // 2):
                        pe.wait_ge(lo_done, 2 * w + 1 + (k > 0))

                for t in range(T):
                    ps = banks[st["into"][t]]
                    take(st["into"][t])
                    parts = [(0, st["ncols"], None)] if not st["turned"] else [(0, SEQ, 2 * t), (SEQ, 2 * SEQ, 2 * t + 1)]
                    for o0, o1, b in parts:
                        for k in range(nkc):
                            if t == 0 and o0 == 0:
                                needs(k)
                            elif st["second"] and t == 1 and k % 4 == 0:
                                pe.wait_ge(ready, values[1][k])
                            for q, (xx, ww) in enumerate(((xh, wh), (xl, wh), (xh, wl))):
                                if st["turned"]:
                                    a, m = ww[:, k, b * P:(b + 1) * P], xx[:, k, :]
                                else:
                                    a, m = xx[:, k, t * P:(t + 1) * P], ww[:, k, :]
                                mm = pe.matmul(ps[:, o0:o1], a, m, start=(k == 0 and q == 0),
                                               stop=(k == nkc - 1 and q == 2))
                    mm.then_inc(lin_done, 1)
                    held[st["into"][t]] = (frees[0], frees[1] + t + 1)
                    if st["second"] and t == 0:
                        turn_rows(st["second"], 1)

            for st in stages:
                at = st["at"]
                if st["kind"] == "setup":
                    pe.wait_ge(const_done, 5 + HALF)
                elif st["kind"] == "renorm":
                    if st["lhs"]:
                        w = st["w"]
                        ready, values, (xh, xl) = st["lhs"]
                        for t in range(T):
                            for h in range(2):
                                take(LB[h])
                                wh, wl = wide(whi, w + h, KC, NW), wide(wlo, w + h, KC, NW)
                                for k in range(KC):
                                    if t == 0 and h == 0 and k % 2 == 0:
                                        pe.wait_ge(ready, values[t][k + 1])
                                    if t == 0 and k in (0, KC // 2):
                                        pe.wait_ge(lo_done, 2 * (w + h) + 1 + (k > 0))
                                    for q, (xx, ww) in enumerate(((xh, wh), (xl, wh), (xh, wl))):
                                        mm = pe.matmul(banks[LB[h]][:, :], xx[:, k, t * P:(t + 1) * P], ww[:, k, :],
                                                       start=(k == 0 and q == 0), stop=(k == KC - 1 and q == 2))
                                mm.then_inc(lin_done, 1)
                                held[LB[h]] = (dev, at["dev"] + 2 * t + h + 1)
                    else:
                        for q in range(2 * T):
                            held[ACC[q // 2][q % 2]] = (dev, at["dev"] + q + 1)
                    turn_rows(st, 0)
                elif st["kind"] == "split":
                    pe.wait_ge(*st["ready"])
                    for g in range(st["nkc"] // 2):
                        name = TB[(at["tp"] + g) % 2]
                        take(name)
                        for k in range(2):
                            for t in range(T):
                                c0, o0 = (2 * g + k) * P, k * SEQ + t * P
                                mm = pe.transpose(banks[name][:, o0:o0 + P], st["src"][:, t, c0:c0 + P], ident[:, :])
                        mm.then_inc(tp_done, 1)
                        held[name] = (tlo_done, at["sg"] + g + 1)
                elif st["deferred"]:
                    continue
                elif st["kind"] == "turn":
                    turn_heads(st)
                elif st["kind"] == "linear":
                    product(st)
                elif st["kind"] == "attention":
                    U = st["units"]
                    pe.wait_ge(*st["first"])

                    def scores(i):
                        u, was = U[i], -1
                        for q, (row, off, width, bank, b0, m, products) in enumerate(u["pieces"]):
                            name = QB[(u["bank0"] + bank) % 4]
                            if bank != was:
                                take(name)
                            for qq, kk, nk in products:
                                mm = pe.matmul(banks[name][:, b0:b0 + nk], qq, kk, start=True, stop=True)
                                b0 += nk
                            was = bank
                            if q + 1 == len(u["pieces"]) or u["pieces"][q + 1][3] != bank:
                                mm.then_inc(s_done, 1)
                                held[name] = (ttr_done, u["ttr0"] + q + 1)

                    def turned(i):
                        u, k = U[i], at["unit"] + i
                        pe.wait_ge(p_done, k + 1)
                        for q, (c0, c1) in enumerate(u["turns"]):
                            name = TB[(u["tp0"] + q) % 2]
                            take(name)
                            for c in range(c0, c1, P):
                                mm = pe.transpose(banks[name][:, c - c0:c - c0 + P], sm[:, k % 3, c:c + P], ident[:, :])
                            mm.then_inc(tp_done, 1)
                            held[name] = (pt_done, u["pt0"] + q + 1)

                    def values_(i):
                        u, k = U[i], at["unit"] + i
                        name = OB[k % 2]
                        take(name)
                        pe.wait_ge(pt_done, u["pt0"] + len(u["turns"]))
                        c = 0
                        for row, (_, vs, _) in enumerate(u["rows"]):
                            for q, v in enumerate(vs):
                                mm = pe.matmul(banks[name][:, row * u["dv"]:(row + 1) * u["dv"]],
                                               pts[:, k % 2, c * P:(c + 1) * P], v, start=(q == 0), stop=(q == len(vs) - 1))
                                c += 1
                        mm.then_inc(pv_done, 1)
                        held[name] = (o_done, k + 1)

                    for i in range(len(U) + 3):
                        if i == st["lead"]:
                            for late in st["behind"]:
                                (turn_heads if late["kind"] == "turn" else product)(late)
                            for s_, v in st["ready"]:
                                pe.wait_ge(s_, v)
                        if i < len(U):
                            scores(i)
                        if 2 <= i < len(U) + 2:
                            turned(i - 2)
                        if i >= 3:
                            values_(i - 3)
                elif st["kind"] == "ffn":
                    w0, d0, sg0, tp0, h0 = st["w"], st["d"], at["sg"], at["tp"], at["h"]
                    ready, values, (xh, xl) = st["lhs"]
                    for name in list(held):
                        take(name)

                    def up(j, s, first=False):
                        wh, wl = (f[:, s, :].rearrange("p (k n) -> p k n", n=NW) for f in (whi, wlo))
                        for t in range(T):
                            if not first:
                                pe.wait_ge(h_done, h0 + 2 * j + t - 1)
                            for k in range(KC):
                                if first and k % 2 == 0 and (t == 0 or st["second"]):
                                    pe.wait_ge(ready, values[t][k + 1])
                                if t == 0 and k in (0, KC // 2):
                                    pe.wait_ge(lo_done, 2 * w0 + 2 * j + 1 + (k > 0))
                                for q, (xx, ww) in enumerate(((xh, wh), (xl, wh), (xh, wl))):
                                    mm = pe.matmul(banks[LB[t]][:, :], xx[:, k, t * P:(t + 1) * P], ww[:, k, :],
                                                   start=(k == 0 and q == 0), stop=(k == KC - 1 and q == 2))
                            mm.then_inc(lin_done, 1)
                            if t == 0 and first and st["second"]:
                                turn_rows(st["second"], 1)
                            if t == 0 and not first:
                                turned_hidden(j - 1, (s + w0 + 1) % 2)

                    def turned_hidden(j, b):
                        name = TB[(tp0 + b) % 2]
                        pe.wait_ge(h_done, h0 + 2 * j + 2)
                        pe.wait_ge(tlo_done, sg0 + j - 1)
                        for k in range(2):
                            for t in range(T):
                                o0 = k * SEQ + t * P
                                mm = pe.transpose(banks[name][:, o0:o0 + P], hid[:, b, t, k * P:(k + 1) * P], ident[:, :])
                        mm.then_inc(tp_done, 1)

                    def down(j, b, first=False, last=False, between=None):
                        pe.wait_ge(tlo_done, sg0 + j + 1)
                        for t in range(T):
                            for k in range(2):
                                if t == 0:
                                    pe.wait_ge(dlo_done, 2 * (d0 + j) + k + 1)
                                for h in range(2):
                                    for q, (yy, ww) in enumerate(((yt_hi, dhi), (yt_lo, dhi), (yt_hi, dlo))):
                                        mm = pe.matmul(banks[ACC[t][h]][:, :], yy[:, 2 * b + k, t * P:(t + 1) * P],
                                                       ww[:, k, h * NW:(h + 1) * NW],
                                                       start=(first and k == 0 and q == 0),
                                                       stop=(last and k == 1 and q == 2))
                            if last and t == 0:
                                mm.then_inc(sum_done, 1)
                            if between and t == 0:
                                between()
                        mm.then_inc(down_done, 1)

                    up(0, w0 % 2, first=True)
                    up(1, (w0 + 1) % 2)
                    down(0, 0, first=True)
                    with pe.Fori(0, (FJ - 3) // 2) as i:
                        up(i * 2 + 2, w0 % 2)
                        down(i * 2 + 1, 1)
                        up(i * 2 + 3, (w0 + 1) % 2)
                        down(i * 2 + 2, 0)
                    up(FJ - 1, w0 % 2)
                    down(FJ - 2, 1, between=lambda: turned_hidden(FJ - 1, 0))
                    down(FJ - 1, 0, last=True)
                    if st["evacuate"]:
                        for q in range(4):
                            held[ACC[q // 2][q % 2]] = (dev, at["dev"] + q + 1)
                elif st["kind"] == "select":
                    pe.wait_ge(*st["ready"])
                    for e in range(4 * T):
                        t, half, pair = e // 4, (e % 4) // 2, e % 2
                        nk = P * (t + 1)
                        name = SB[(at["seg"] + e) % 2]
                        take(name)
                        q = slice(half * HD, (half + 1) * HD)
                        for b in range(2):
                            mm = pe.matmul(banks[name][:, b * SEQ:b * SEQ + nk], st["iqT"][q, 2 * pair + b, t * P:(t + 1) * P],
                                           st["kkT"][q, 1, 0:nk], start=True, stop=True)
                        mm.then_inc(s_done, 1)
                        held[name] = (rel_done, at["rel"] + e + 1)
                elif st["kind"] == "hgrn":
                    k = 1 if st["l"] > 0 else 0
                    ha, hd_, hp = st["counts"]
                    pe.wait_ge(hg_dve, hd_ + k + 2)
                    for t in range(T):
                        take(SB[t])
                        for h in range(HG):
                            q = slice(t * P, (t + 1) * P)
                            mm = pe.matmul(banks[SB[t]][:, h * P:(h + 1) * P], headed(7)[:, h, q], headed(6)[:, h, q],
                                           start=True, stop=True)
                        mm.then_inc(hg_pe, 1)
                        held[SB[t]] = (hg_dve, hd_ + k + 3 + t)
                    for t in range(T):
                        name = TB[(at["tp"] + t) % 2]
                        take(name)
                        for h in range(HG):
                            mm = pe.transpose(banks[name][:, h * P:(h + 1) * P], headed(8)[:, h, t * P:(t + 1) * P],
                                              ident[:, :])
                        mm.then_inc(tp_done, 1)
                        held[name] = (hg_act, ha + k + 3 + t)
                    pe.wait_ge(hg_act, ha + k + 2 + T)
                    pe.wait_ge(aev, st["aev_all"])
                    for c, name in enumerate(("O0", "O1", "S0")):
                        take(name)
                        rows = slice((c % 2) * HGC, (c % 2 + 1) * HGC)
                        for h in range(HG):
                            q = slice(h * P, (h + 1) * P)
                            mm = pe.matmul(banks[name][:, q], tiled(4)[rows, c // 2, q], st["hv"][rows, c // 2, q], start=True,
                                           stop=True)
                        mm.then_inc(hg_pe, 1)
                        held[name] = (hg_dve, hd_ + k + 2 + T + c + 1)
                    pe.wait_ge(hg_dve, hd_ + k + 2 + T + 3)
                    for t in range(T):
                        name = OB[t]
                        take(name)
                        for h in range(HG):
                            q = slice(h * P, (h + 1) * P)
                            pe.matmul(banks[name][:, q], tiled(5)[:, t, q], st["hv"][:, t, q], start=True, stop=False)
                            if t:
                                pe.matmul(banks[name][:, q], headed(1)[:, h, t * P:(t + 1) * P], HSTATE[2 * t - 1][:, q],
                                          start=False, stop=False)
                            mm = pe.matmul(banks[name][:, q], headed(3)[:, h, t * P:(t + 1) * P], HSTATE[2 * t][:, q],
                                           start=False, stop=True)
                        mm.then_inc(hg_pe, 1)
                        held[name] = (hg_act, ha + k + 2 + T + t + 1)


_INS = ["x", "positions", "ln_g", "ln_b", "a_w_qkv", "a_b_qkv", "a_sinks", "a_w_o", "a_b_o", "b_w_qkv", "b_w_o", "c_w_qkv",
        "c_w_o", "w_gate_up", "w_down", "mem_2", "positions_2", "norm_mix_2", "w_in_2", "conv_w_2", "dsa_q_norm_2",
        "dsa_k_norm_2", "hgrn_lower_bounds_2", "hgrn_out_norm_2", "mem_norm_2", "mem_w_kv_2", "mem_q_norm_2",
        "mem_k_norm_2", "w_lift_2", "w_out_2", "norm_ffn_2", "ffn_w_up_2", "ffn_w_down_2"]
_OUT = ((1, SEQ, D), "float32")


def kernel(**inputs):
    import concourse.bacc as _bacc
    from concourse.bass_utils import run_bass_kernel_spmd as _run

    nc = _bacc.Bacc("TRN2", target_bir_lowering=False, num_devices=1)
    arrays, args = {}, []
    for name in _INS:
        a = np.ascontiguousarray(inputs[name])
        arrays[f"in_{name}"] = a
        args.append(nc.dram_tensor(f"in_{name}", a.shape, mybir.dt.from_np(a.dtype), kind="ExternalInput").ap())
    args.append(nc.dram_tensor("out_0", _OUT[0], mybir.dt.from_np(np.dtype(_OUT[1])), kind="ExternalOutput").ap())
    build(nc, *args)
    return _run(nc, [arrays], core_ids=[0]).results[0]["out_0"]
```
